# Optimizing a Trainium2 kernel written in Bass

```python
import math
import jax, jax.numpy as jnp
from jax import lax
import numpy as np

D_MODEL = 1024
BATCH = 1
SEQ = 256
DEPTH = 2
DEC_BATCH = 8
DEC_SEQ = 1
PAST_LEN = 2048
PAGE_SIZE = 128

N_HEADS = 4
HEAD_DIM = 64
GROUP_W = N_HEADS * HEAD_DIM
A_Q_LORA = 256
A_KV_LORA = 128
A_NOPE = 64
A_ROPE = 32
A_V = HEAD_DIM
ROPE_THETA = 10000.0
B_PATTERNS = ((128, 1), (512, 4), (2048, 16))
B_WIN_MAX = 2048
C_DK = HEAD_DIM
C_DV = HEAD_DIM
D_DK = 128
D_DV = HEAD_DIM
CHUNK = 64
Q_BLOCK = 128
D_FF = 2816
EPS = 1e-6
NEG_BIG = -1e30
MLA_SCALE = 1.0 / math.sqrt(A_NOPE + A_ROPE)
B_SCALE = 1.0 / math.sqrt(HEAD_DIM)
IN_WIDTHS = (A_Q_LORA, A_KV_LORA, A_ROPE,
             GROUP_W, GROUP_W, GROUP_W,
             N_HEADS * C_DK, N_HEADS * C_DK, N_HEADS * C_DV, N_HEADS, N_HEADS, N_HEADS * C_DV,
             N_HEADS * D_DK, N_HEADS * D_DK, N_HEADS * D_DV, N_HEADS * D_DV)
N_IN = sum(IN_WIDTHS)

kernel_name = 'hybrid_mla_dilated_mlstm_hgrn2_step'

def _rmsnorm(x, g):
    xf = x.astype(jnp.float32)
    y = xf * lax.rsqrt(jnp.mean(xf * xf, axis=-1, keepdims=True) + EPS)
    return (y * g.astype(jnp.float32)).astype(x.dtype)

def _swiglu(x, g, w_gate, w_up, w_down):
    h = _rmsnorm(x, g)
    return (jax.nn.silu(h @ w_gate) * (h @ w_up)) @ w_down

def _rope(x, pos):
    half = x.shape[-1] // 2
    inv = ROPE_THETA ** (-jnp.arange(half, dtype=jnp.float32) / half)
    ang = pos.astype(jnp.float32)[:, None] * inv[None, :]
    cos = jnp.cos(ang)[None, :, None, :]
    sin = jnp.sin(ang)[None, :, None, :]
    xf = x.astype(jnp.float32)
    x1, x2 = xf[..., :half], xf[..., half:]
    return jnp.concatenate([x1 * cos - x2 * sin, x1 * sin + x2 * cos], axis=-1).astype(x.dtype)

def _mla_attend(qn, qr, kn, kr, lat, w_uv, qpos, kpos):
    N, Tq = qn.shape[0], qn.shape[1]
    s = (jnp.einsum('nqhd,nkhd->nhqk', qn, kn) + jnp.einsum('nqhr,nkr->nhqk', qr, kr)).astype(jnp.float32) * MLA_SCALE
    s = jnp.where((kpos[None, :] <= qpos[:, None])[None, None], s, -jnp.inf)
    p = jax.nn.softmax(s, axis=-1).astype(lat.dtype)
    ctx = jnp.einsum('nhqk,nkc->nqhc', p, lat)
    return jnp.einsum('nqhc,chd->nqhd', ctx, w_uv).reshape(N, Tq, -1)

def _mla_prompt(qn, qr, kn, kr, lat, w_uv):
    N, T = qn.shape[0], qn.shape[1]
    nb = T // Q_BLOCK

    def blocks(x):
        return jnp.moveaxis(x.reshape((N, nb, Q_BLOCK) + x.shape[2:]), 1, 0)

    kpos = jnp.arange(T, dtype=jnp.int32)

    def one(args):
        qn_b, qr_b, s0 = args
        return _mla_attend(qn_b, qr_b, kn, kr, lat, w_uv, s0 + jnp.arange(Q_BLOCK, dtype=jnp.int32), kpos)

    o = lax.map(one, (blocks(qn), blocks(qr), jnp.arange(nb, dtype=jnp.int32) * Q_BLOCK))
    return jnp.moveaxis(o, 0, 1).reshape(N, T, -1)

def _dilation_offsets():
    return jnp.asarray(np.concatenate([np.arange(w // d + 1) * d for (w, d) in B_PATTERNS]), dtype=jnp.int32)

def _dilated_core(q, k, v, qidx):
    kidx = qidx[:, None] - _dilation_offsets()[None, :]
    valid = kidx >= 0
    kidx = jnp.maximum(kidx, 0)
    kg = k[kidx]
    vg = v[kidx]
    s = jnp.einsum('qhd,qjhd->hqj', q, kg).astype(jnp.float32) * B_SCALE
    s = jnp.where(valid[None], s, -jnp.inf)
    p = jax.nn.softmax(s, axis=-1).astype(v.dtype)
    return jnp.einsum('hqj,qjhd->qhd', p, vg)

def _dilated_prompt(q, k, v):
    N, T, H, d = q.shape
    nb = T // Q_BLOCK
    qb = q.reshape(N * nb, Q_BLOCK, H, d)
    bidx = jnp.repeat(jnp.arange(N, dtype=jnp.int32), nb)
    starts = jnp.tile(jnp.arange(nb, dtype=jnp.int32) * Q_BLOCK, N)

    def one(args):
        q_b, b, s0 = args
        return _dilated_core(q_b, k[b], v[b], s0 + jnp.arange(Q_BLOCK, dtype=jnp.int32))

    o = lax.map(one, (qb, bidx, starts))
    return o.reshape(N, T, H * d)

def _to_chunks(x, L, nc, fill=0.0):
    T = x.shape[1]
    x = jnp.pad(x, [(0, 0), (0, nc * L - T)] + [(0, 0)] * (x.ndim - 2), constant_values=fill)
    return jnp.moveaxis(x.reshape((x.shape[0], nc, L) + x.shape[2:]), 1, 0)

def _from_chunks(y, T):
    y = jnp.moveaxis(y, 0, 1)
    return y.reshape((y.shape[0], -1) + y.shape[3:])[:, :T]

def _mlstm(q, k, v, ig, lf, C0, n0, m0):
    T = q.shape[1]
    f32 = jnp.float32
    L = min(CHUNK, T)
    nc = -(-T // L)
    xs = (_to_chunks(q.astype(f32), L, nc), _to_chunks(k.astype(f32), L, nc), _to_chunks(v.astype(f32), L, nc),
          _to_chunks(ig, L, nc, NEG_BIG), _to_chunks(lf, L, nc))
    tri = jnp.tril(jnp.ones((L, L), dtype=bool))

    def step(carry, inp):
        C, n, m = carry
        qc, kc, vc, ic, fc = inp
        bt = jnp.moveaxis(jnp.cumsum(fc, axis=1), 1, 2)
        it = jnp.moveaxis(ic, 1, 2)
        Dm = jnp.where(tri, bt[..., :, None] - bt[..., None, :] + it[..., None, :], -jnp.inf)
        prev = bt + m[..., None]
        mt = jnp.maximum(prev, jnp.max(Dm, axis=-1))
        W = jnp.exp(Dm - mt[..., None])
        a = jnp.exp(prev - mt)
        qk = jnp.einsum('nthd,nshd->nhts', qc, kc) * W
        num = a[..., None] * jnp.einsum('nthd,nhde->nhte', qc, C) + jnp.einsum('nhts,nshe->nhte', qk, vc)
        den = a * jnp.einsum('nthd,nhd->nht', qc, n) + jnp.sum(qk, axis=-1)
        h = num / jnp.maximum(jnp.abs(den), jnp.exp(-mt))[..., None]
        bL = bt[..., -1]
        endw = bL[..., None] - bt + it
        m_new = jnp.maximum(bL + m, jnp.max(endw, axis=-1))
        wend = jnp.exp(endw - m_new[..., None])
        dec = jnp.exp(bL + m - m_new)
        C_new = dec[..., None, None] * C + jnp.einsum('nhs,nshd,nshe->nhde', wend, kc, vc)
        n_new = dec[..., None] * n + jnp.einsum('nhs,nshd->nhd', wend, kc)
        return (C_new, n_new, m_new), jnp.moveaxis(h, 2, 1)

    (C, n, m), hs = lax.scan(step, (C0.astype(f32), n0.astype(f32), m0.astype(f32)), xs)
    return _from_chunks(hs, T), C, n, m

def _hgrn2(q, lf, kin, v, S0):
    T = q.shape[1]
    f32 = jnp.float32
    L = min(CHUNK, T)
    nc = -(-T // L)
    xs = (_to_chunks(q, L, nc), _to_chunks(lf, L, nc), _to_chunks(kin, L, nc), _to_chunks(v.astype(f32), L, nc))
    tri = jnp.tril(jnp.ones((L, L), dtype=bool))

    def step(S, inp):
        qc, fc, kc, vc = inp
        B = jnp.cumsum(fc, axis=1)
        o = jnp.einsum('nthk,nhkv->nthv', qc * jnp.exp(B), S)
        diff = B[:, :, None] - B[:, None, :]
        dec = jnp.exp(jnp.where(tri[None, :, :, None, None], diff, -jnp.inf))
        A = jnp.einsum('nthk,ntshk,nshk->nhts', qc, dec, kc)
        o = o + jnp.einsum('nhts,nshv->nthv', A, vc)
        BL = B[:, -1]
        S_new = jnp.exp(BL)[..., None] * S + jnp.einsum('nshk,nshv->nhkv', kc * jnp.exp(BL[:, None] - B), vc)
        return S_new, o

    S, os_ = lax.scan(step, S0.astype(f32), xs)
    return _from_chunks(os_, T), S

def _token_mixer(h, pos, lp, lb, cache, page_table):
    N, T, _ = h.shape
    H = N_HEADS
    f32 = jnp.float32
    cuts = [int(c) for c in np.cumsum(IN_WIDTHS)[:-1]]
    (a_cq, a_ckv, a_kr, b_q, b_k, b_v, c_q, c_k, c_v, c_i, c_f, c_o,
     d_q, d_f, d_i, d_g) = jnp.split(h @ lp['w_in'], cuts, axis=-1)

    q = (_rmsnorm(a_cq, lp['a_gq']) @ lp['a_wuq']).reshape(N, T, H, A_NOPE + A_ROPE)
    qn = _rmsnorm(q[..., :A_NOPE], lp['a_gqn'])
    qr = _rope(_rmsnorm(q[..., A_NOPE:], lp['a_gqr']), pos)
    lat = _rmsnorm(a_ckv, lp['a_gkv'])
    kr = _rope(_rmsnorm(a_kr, lp['a_gkr'])[:, :, None, :], pos)[:, :, 0]
    w_ukv = lp['a_wukv'].reshape(A_KV_LORA, H, A_NOPE + A_V)
    w_uk, w_uv = w_ukv[..., :A_NOPE], w_ukv[..., A_NOPE:]
    if cache is None:
        kn = _rmsnorm(jnp.einsum('ntc,chd->nthd', lat, w_uk), lp['a_gkn'])
        o_a = _mla_prompt(qn, qr, kn, kr, lat, w_uv)
    else:
        lat_all = jnp.concatenate([cache['lat'][page_table].reshape(N, -1, A_KV_LORA), lat], axis=1)
        kr_all = jnp.concatenate([cache['kr'][page_table].reshape(N, -1, A_ROPE), kr], axis=1)
        kn = _rmsnorm(jnp.einsum('ntc,chd->nthd', lat_all, w_uk), lp['a_gkn'])
        o_a = _mla_attend(qn, qr, kn, kr_all, lat_all, w_uv, pos, jnp.arange(lat_all.shape[1], dtype=jnp.int32))

    qb = _rmsnorm(b_q.reshape(N, T, H, HEAD_DIM), lp['b_gq'])
    kb = _rmsnorm(b_k.reshape(N, T, H, HEAD_DIM), lp['b_gk'])
    vb = b_v.reshape(N, T, H, HEAD_DIM)
    if cache is None:
        o_b = _dilated_prompt(qb, kb, vb)
        wb = min(B_WIN_MAX, T)
        new_k, new_v = kb[:, T - wb:], vb[:, T - wb:]
    else:
        wb = cache['swa_k'].shape[1]
        k_all = jnp.concatenate([cache['swa_k'], kb], axis=1)
        v_all = jnp.concatenate([cache['swa_v'], vb], axis=1)
        o_b = jax.vmap(_dilated_core, in_axes=(0, 0, 0, None))(
            qb, k_all, v_all, wb + jnp.arange(T, dtype=jnp.int32)).reshape(N, T, -1)
        new_k, new_v = k_all[:, T:], v_all[:, T:]

    qc = c_q.reshape(N, T, H, C_DK)
    kc = c_k.reshape(N, T, H, C_DK) * (C_DK ** -0.5)
    vc = c_v.reshape(N, T, H, C_DV)
    ig = c_i.astype(f32) + lp['c_bi'].astype(f32)
    lf_c = jax.nn.log_sigmoid(c_f.astype(f32) + lp['c_bf'].astype(f32))
    if cache is None:
        C0, n0, m0 = jnp.zeros((N, H, C_DK, C_DV), f32), jnp.zeros((N, H, C_DK), f32), jnp.zeros((N, H), f32)
    else:
        C0, n0, m0 = cache['C'], cache['n'], cache['m']
    hc, C1, n1, m1 = _mlstm(qc, kc, vc, ig, lf_c, C0, n0, m0)
    o_c = (_rmsnorm(hc.astype(h.dtype), lp['c_gout'].reshape(H, C_DV))
           * jax.nn.sigmoid(c_o).reshape(N, T, H, C_DV)).reshape(N, T, -1)

    lbh = lb.reshape(H, D_DK)
    xf = d_f.reshape(N, T, H, D_DK).astype(f32)
    lf_d = jnp.logaddexp(jax.nn.log_sigmoid(xf), jnp.log(lbh) + jax.nn.log_sigmoid(-xf))
    kin = (1.0 - lbh) * jax.nn.sigmoid(-xf)
    qd = jax.nn.silu(d_q.reshape(N, T, H, D_DK).astype(f32)) * (D_DK ** -0.5)
    S0 = jnp.zeros((N, H, D_DK, D_DV), f32) if cache is None else cache['S']
    od, S1 = _hgrn2(qd, lf_d, kin, d_i.reshape(N, T, H, D_DV), S0)
    o_d = (_rmsnorm(od.astype(h.dtype), lp['d_gout'].reshape(H, D_DV))
           * jax.nn.silu(d_g).reshape(N, T, H, D_DV)).reshape(N, T, -1)

    y = jnp.concatenate([o_a, o_b, o_c, o_d], axis=-1) @ lp['w_out']
    return y, (lat, kr, new_k, new_v, C1, n1, m1, S1)

def setup_inputs(seed: int = 0) -> dict:
    key = jax.random.key(seed)
    ks = list(jax.random.split(key, 48))

    def nrm(shape, scale):
        return scale * jax.random.normal(ks.pop(), shape, jnp.float32)

    def gain(shape):
        return 1.0 + 0.05 * jax.random.normal(ks.pop(), shape, jnp.float32)

    n_pages = PAST_LEN // PAGE_SIZE
    n_pool = (DEC_BATCH * n_pages * 5) // 4
    win_buf = min(B_WIN_MAX, PAST_LEN)
    H = N_HEADS
    page_table = jax.random.permutation(ks.pop(), n_pool)[: DEC_BATCH * n_pages].reshape(DEC_BATCH, n_pages).astype(jnp.int32)
    return {
        'x_prompt': nrm((BATCH, SEQ, D_MODEL), 1.0),
        'x_sample': nrm((DEC_BATCH, DEC_SEQ, D_MODEL), 1.0),
        'cache_mla_latent': nrm((DEPTH, n_pool, PAGE_SIZE, A_KV_LORA), 1.0),
        'cache_mla_krope': nrm((DEPTH, n_pool, PAGE_SIZE, A_ROPE), 1.0),
        'cache_swa_k': nrm((DEPTH, DEC_BATCH, win_buf, H, HEAD_DIM), 1.0),
        'cache_swa_v': nrm((DEPTH, DEC_BATCH, win_buf, H, HEAD_DIM), 1.0),
        'state_mlstm_C': nrm((DEPTH, DEC_BATCH, H, C_DK, C_DV), 0.1),
        'state_mlstm_n': nrm((DEPTH, DEC_BATCH, H, C_DK), 0.1),
        'state_mlstm_m': nrm((DEPTH, DEC_BATCH, H), 0.5),
        'state_hgrn_S': nrm((DEPTH, DEC_BATCH, H, D_DK, D_DV), 0.5),
        'page_table': page_table,
        'g_ffn1': gain((DEPTH, D_MODEL)),
        'w1_gate': nrm((DEPTH, D_MODEL, D_FF), D_MODEL ** -0.5),
        'w1_up': nrm((DEPTH, D_MODEL, D_FF), D_MODEL ** -0.5),
        'w1_down': nrm((DEPTH, D_FF, D_MODEL), D_FF ** -0.5),
        'g_mix': gain((DEPTH, D_MODEL)),
        'w_in': nrm((DEPTH, D_MODEL, N_IN), D_MODEL ** -0.5),
        'a_gq': gain((DEPTH, A_Q_LORA)),
        'a_wuq': nrm((DEPTH, A_Q_LORA, H * (A_NOPE + A_ROPE)), A_Q_LORA ** -0.5),
        'a_gqn': gain((DEPTH, A_NOPE)),
        'a_gqr': gain((DEPTH, A_ROPE)),
        'a_gkv': gain((DEPTH, A_KV_LORA)),
        'a_gkr': gain((DEPTH, A_ROPE)),
        'a_wukv': nrm((DEPTH, A_KV_LORA, H * (A_NOPE + A_V)), A_KV_LORA ** -0.5),
        'a_gkn': gain((DEPTH, A_NOPE)),
        'b_gq': gain((DEPTH, HEAD_DIM)),
        'b_gk': gain((DEPTH, HEAD_DIM)),
        'c_bi': nrm((DEPTH, H), 0.1),
        'c_bf': 3.0 + nrm((DEPTH, H), 0.5),
        'c_gout': gain((DEPTH, H * C_DV)),
        'd_lb_logits': nrm((DEPTH, H * D_DK), 0.5),
        'd_gout': gain((DEPTH, H * D_DV)),
        'w_out': nrm((DEPTH, D_MODEL, D_MODEL), D_MODEL ** -0.5),
        'g_ffn2': gain((DEPTH, D_MODEL)),
        'w2_gate': nrm((DEPTH, D_MODEL, D_FF), D_MODEL ** -0.5),
        'w2_up': nrm((DEPTH, D_MODEL, D_FF), D_MODEL ** -0.5),
        'w2_down': nrm((DEPTH, D_FF, D_MODEL), D_FF ** -0.5),
    }

def reference(x_prompt, x_sample, cache_mla_latent, cache_mla_krope, cache_swa_k, cache_swa_v,
              state_mlstm_C, state_mlstm_n, state_mlstm_m, state_hgrn_S, page_table,
              g_ffn1, w1_gate, w1_up, w1_down, g_mix, w_in, a_gq, a_wuq, a_gqn, a_gqr, a_gkv, a_gkr,
              a_wukv, a_gkn, b_gq, b_gk, c_bi, c_bf, c_gout, d_lb_logits, d_gout, w_out,
              g_ffn2, w2_gate, w2_up, w2_down):
    lb_all = jnp.cumsum(jax.nn.softmax(d_lb_logits.astype(jnp.float32), axis=0), axis=0)
    lb_all = lb_all - lb_all[:1]
    xp, xs = x_prompt, x_sample
    pos_p = jnp.arange(xp.shape[1], dtype=jnp.int32)
    past = page_table.shape[1] * cache_mla_latent.shape[2]
    pos_s = past + jnp.arange(xs.shape[1], dtype=jnp.int32)
    new_p, new_s = [], []
    for l in range(DEPTH):
        lp = {'w_in': w_in[l], 'w_out': w_out[l], 'a_gq': a_gq[l], 'a_wuq': a_wuq[l], 'a_gqn': a_gqn[l],
              'a_gqr': a_gqr[l], 'a_gkv': a_gkv[l], 'a_gkr': a_gkr[l], 'a_wukv': a_wukv[l], 'a_gkn': a_gkn[l],
              'b_gq': b_gq[l], 'b_gk': b_gk[l], 'c_bi': c_bi[l], 'c_bf': c_bf[l], 'c_gout': c_gout[l],
              'd_gout': d_gout[l]}
        cache = {'lat': cache_mla_latent[l], 'kr': cache_mla_krope[l], 'swa_k': cache_swa_k[l],
                 'swa_v': cache_swa_v[l], 'C': state_mlstm_C[l], 'n': state_mlstm_n[l], 'm': state_mlstm_m[l],
                 'S': state_hgrn_S[l]}
        xp = xp + 0.5 * _swiglu(xp, g_ffn1[l], w1_gate[l], w1_up[l], w1_down[l])
        xs = xs + 0.5 * _swiglu(xs, g_ffn1[l], w1_gate[l], w1_up[l], w1_down[l])
        yp, stp = _token_mixer(_rmsnorm(xp, g_mix[l]), pos_p, lp, lb_all[l], None, None)
        ys, sts = _token_mixer(_rmsnorm(xs, g_mix[l]), pos_s, lp, lb_all[l], cache, page_table)
        xp = xp + yp
        xs = xs + ys
        xp = xp + 0.5 * _swiglu(xp, g_ffn2[l], w2_gate[l], w2_up[l], w2_down[l])
        xs = xs + 0.5 * _swiglu(xs, g_ffn2[l], w2_gate[l], w2_up[l], w2_down[l])
        new_p.append(stp)
        new_s.append(sts)

    def stacked(states, i):
        return jnp.stack([st[i] for st in states], axis=0)

    return (xp, xs,
            stacked(new_p, 0), stacked(new_p, 1), stacked(new_p, 2), stacked(new_p, 3),
            stacked(new_p, 4), stacked(new_p, 5), stacked(new_p, 6), stacked(new_p, 7),
            stacked(new_s, 0), stacked(new_s, 1), stacked(new_s, 2), stacked(new_s, 3),
            stacked(new_s, 4), stacked(new_s, 5), stacked(new_s, 6), stacked(new_s, 7))


_drawn_inputs = setup_inputs


def setup_inputs(seed=0):
    import zlib

    import numpy as np

    out = dict(_drawn_inputs(seed))
    spreads = {}
    factors = {'cache_mla_krope': 4.579,
     'a_gq': 8.0,
     'a_gqn': 8.0,
     'a_gqr': 8.0,
     'a_gkn': 8.0,
     'b_gq': 8.0,
     'c_gout': 3.014}
    for name, (base, spread) in spreads.items():
        noise = np.random.default_rng([zlib.crc32(name.encode()), seed]).standard_normal(out[name].shape)
        drawn = base * np.exp(spread * noise) if base else spread * noise
        out[name] = __import__('jax').numpy.asarray(drawn.astype(out[name].dtype))
    for name, factor in factors.items():
        out[name] = (out[name] * factor).astype(out[name].dtype)
    return out
```

```python
import concourse.bass as bass
from concourse import mybir
from contextlib import ExitStack

D_MODEL, SEQ, DEPTH, DEC, PAST, PAGE = 1024, 256, 2, 8, 2048, 128
H, HD, GW = 4, 64, 256
QL, KVL, NOPE, ROPE, DK = 256, 128, 64, 32, 128
D_FF, EPS = 2816, 1e-6
PATTERNS = ((128, 1), (512, 4), (2048, 16))
P = 128
NT = SEQ + DEC
KC = D_MODEL // P
FT = D_FF // P
BLK = 3
ROWS = (P, P, DEC)
QKW = NOPE + ROPE
PAGES = PAST // PAGE
NPAT = len(PATTERNS)

W_B, W_C, W_I, W_O = QL + KVL + ROPE, QL + KVL + ROPE + 3 * GW, QL + KVL + ROPE + 6 * GW, QL + KVL + ROPE + 6 * GW + 2 * H
W_DQ = W_O + GW
W_DF, W_DI, W_DG = W_DQ + H * DK, W_DQ + 2 * H * DK, W_DQ + 2 * H * DK + GW
N_IN = W_DG + GW
CQ, CKV, CKR, BQ, BK, BV = 0, QL, QL + KVL, W_B, W_B + GW, W_B + 2 * GW
MQ, MK, MV = W_C, W_C + GW, W_C + 2 * GW
DI, GATE = MV + GW, MV + 2 * GW
TMW = GATE + 2 * GW
SLABS = [(0, W_B, CQ), (BQ, 2 * GW, BQ), (BV, GW, BV), (MQ, 2 * GW, MQ), (MV, GW + 2 * H, MV),
         (W_O, GW, GATE), (W_DQ, H * DK, None), (W_DF, H * DK, None), (W_DI, GW, DI), (W_DG, GW, GATE + GW)]
OUT_SLABS = [(0, 3), (3, 3), (6, 2)]
NG = FT // 2
ND = KC
FFN_SLABS = NG + ND
MIX_SLABS = len(SLABS) + len(OUT_SLABS)
RING = 3
LAYER_SLABS = 2 * FFN_SLABS + MIX_SLABS
assert LAYER_SLABS % RING == 0
SLOT = 2 * KC * 2 * P

G_Q, G_KV, G_KR, G_BQ, G_BK = 0, QL, QL + KVL, QL + KVL + ROPE, QL + KVL + ROPE + HD
G_QN = G_BK + HD
G_QR, G_KN = G_QN + NOPE, G_QN + NOPE + ROPE
G_OUT = G_KN + NOPE
G_N = G_OUT + 2 * GW

LEVELS = [128, 64, 32, 16, 8, 4, 2, 1]
K_ID = 0
K_AADD = P
K_BADD = K_AADD + 3 * P
K_BMUL = K_BADD + 3 * P
K_WM = K_BMUL + 3 * P
K_LV = K_WM + 3 * P
K_SELH = K_LV + (len(LEVELS) - 1) * P
K_SELJ = K_SELH + H * P
K_COS = K_SELJ + 32
K_SIN = K_COS + BLK * ROPE // 2
K_N = K_SIN + BLK * ROPE // 2
X_MQ, X_MK, X_MV, X_DI, X_CO, X_DG, X_QD, X_F, X_K, X_I, X_LF = 0, 64, 128, 192, 256, 320, 384, 512, 640, 768, 769
X_N = 770
A_SCALE, B_SCALE, M_SCALE, D_SCALE = (NOPE + ROPE) ** -0.5, HD ** -0.5, HD ** -0.5, DK ** -0.5
X_MIN = -43.0
LAT_SLOTS = 3
K_SLOTS = 2
N_STORE = 8
N_PSTATE = 4
N_SSTATE = 3 * 4 + 1
N_SCRATCH = 11
CREDIT = 2
OUT_CREDIT = 3
RMAX = bass.bass_isa.ReduceOp.max


def tickets():
    out = []
    for n, (_, _, col) in enumerate(SLABS):
        if col is None:
            out += [(n, "head", h) for h in range(H)]
        else:
            out += [(n, "rows", b) for b in range(BLK)]
        if n == 4:
            out += [(n, "gate", 0), (n, "gate", 1)]
    return out


TICKETS = tickets()
NTK = len(TICKETS)


def build(nc, t):
    f32 = mybir.dt.float32
    ACT, ALU, AX = mybir.ActivationFunctionType, mybir.AluOpType, mybir.AxisListType
    MUL, ADD, SUB, MAX, MIN = ALU.mult, ALU.add, ALU.subtract, ALU.max, ALU.min
    ctx = ExitStack()
    with ctx:
        def sb(name, shape, dt=f32):
            return ctx.enter_context(nc.sbuf_tensor(name, shape, dt))

        made = {}

        def sem(name):
            if name not in made:
                made[name] = ctx.enter_context(nc.semaphore(name))
            return made[name]

        x_T = sb("x_T", [P, KC, NT])
        h_T = sb("h_T", [P, KC, NT])
        act_T = sb("act_T", [P, FT, NT])
        ring = sb("ring", [P, RING, SLOT])
        TM = sb("TM", [P, BLK, TMW])
        o_T = sb("o_T", [P, KC, NT])
        cst = sb("cst", [P, K_N])
        ones = sb("ones", [P, SEQ])
        eps = sb("eps", [P, 1])
        gains = sb("gains", [P, G_N])
        gcols = sb("gcols", [P, DEPTH, 3 * KC])
        lbx = sb("lbx", [P, DEPTH, H])
        lbs = sb("lbs", [P, DEPTH, 2 * H])
        lbt = sb("lbt", [P, 2, H])
        cbias = sb("cbias", [H, DEPTH, 2])
        gcol = sb("gcol", [P, 3 * KC])
        lb = sb("lb", [P, 2 * H])
        cb = sb("cb", [H, 2])
        pages = sb("pages", [1, DEC * PAGES], mybir.dt.int32)
        wuq = sb("wuq", [P, QL // P, H * QKW])
        wukv = sb("wukv", [P, H, 2 * HD])
        ssum = sb("ssum", [P, NT])
        sqx = sb("sqx", [P, NT])
        rstd = sb("rstd", [P, NT])
        sg = sb("sg", [P, 2, NT])
        st = sb("st", [P, 3 * 12])
        rs = sb("rs", [P, 3 * 12])
        rp = sb("rp", [P, 4, BLK * H * ROPE // 2])
        ctxT = sb("ctxT", [P, H, NT])
        latn = sb("latn", [P, NT])
        wuk = sb("wuk", [P, GW + DEC * H])
        qrb = sb("qrb", [P, DEC, 4, H])
        nsA = sb("nsA", [P, DEC * H])
        nsm = sb("nsm", [DEC, 2, DEC, H])
        nst1 = sb("nst1", [DEC, 2, H])
        mxs = sb("mxs", [P, 2, H])
        gT = sb("gT", [P, 5, H])
        gTs = sb("gTs", [DEC, 2, H])
        wd = sb("wd", [P, 2, H])
        emt = sb("emt", [P, 2, H])
        den = sb("den", [P, 2, H])
        lmx = sb("lmx", [P, 3, H])
        wmx = sb("wmx", [P, 6, DEC * H])
        sst = sb("sst", [P, 10])
        decs = sb("decs", [P, 5, (PAGES + 1) * H])
        SB = sb("SB", [P, DEC, NPAT, H])
        jq = sb("jq", [P, 2 * 16 + 3 * 32])
        nst = sb("nst", [P, 16])
        red = sb("red", [P, 2 * HD + 1])
        HS = sb("HS", [32, 2, HD])
        vT = sb("vT", [P, 2, DEC])
        bsum = sb("bsum", [P, DEC, 2, H])
        U = sb("U", [P, 8968])

        def cut(buf, at, *shape):
            n = 1
            for d in shape:
                n *= d
            v = buf[:, at:at + n]
            if len(shape) == 1:
                return v
            names = "abcd"[:len(shape)]
            return v.rearrange("p (" + " ".join(names) + ") -> p " + " ".join(names), **dict(zip(names[1:], shape[1:])))

        actf = act_T[:, :, :].rearrange("p f t -> p (f t)")
        hf = h_T[:, :, :].rearrange("p f t -> p (f t)")
        xin = cut(actf, 0, BLK, D_MODEL)
        QT = cut(U, 0, H, SEQ)
        KT = cut(U, 1024, H, SEQ)
        pairT = cut(U, 2048, 4, 2, SEQ)
        S = cut(U, 4096, H, 3 * P)
        PT = cut(U, 5632, H, 3 * P)
        WT = cut(U, 7168, H, 3 * P)
        CGS = cut(U, 8704, H, HD + 1)
        sq1 = cut(U, 4096, BLK, BV)
        Qk = cut(U, 4096, BLK, H, QKW)
        Kk = cut(U, 5248, BLK, H, QKW)
        sq2 = cut(U, 0, BLK, H, QKW)
        sq3 = cut(U, 1152, BLK, H, NOPE)
        cqT = cut(U, 7168, QL // P, NT)
        wukT = cut(U, 7168, H, P)
        qtT = cut(U, 7696, H, DEC)
        qtl = cut(U, 7728, H, HD)
        q4 = cut(U, 7984, H, 4, ROPE)
        qk = cut(U, 7168, H, QKW)
        vaug = cut(U, 0, 2, H, HD + 1)
        kw = cut(U, 1024, 2, H, HD)
        ATD = cut(U, 0, H, 3, P)
        HCD = cut(U, 2048, 2, 2 * H, HD)
        QP = cut(U, 3072, H, SEQ)
        KP = cut(U, 4096, H, SEQ)
        KE = cut(U, 5120, 2, H, DK)
        TMPD = cut(U, 6144, H, 2, P)
        DGS = cut(U, 6144, H, HD)
        E2 = cut(U, 7168, H, SEQ)
        SM = cut(U, 7168, 3, H, DK)
        sqo = cut(U, 3072, 2, 2 * H, HD)
        QD = cut(actf, 0, H, NT)
        FD = cut(actf, H * NT, H, NT)
        KD = cut(actf, 2 * H * NT, H, NT)
        E1 = cut(actf, 3 * H * NT, H, NT)
        D1 = cut(actf, 4 * H * NT, H, NT)
        E1g = cut(actf, 3 * H * NT, BLK, 2 * GW)
        E1v = cut(actf, 3 * H * NT, H, SEQ)
        D1v = cut(actf, 4 * H * NT, H, SEQ)
        CG = cut(hf, 0, KC, NT)
        lat = cut(U, 0, LAT_SLOTS, PAGES, KVL)
        kr = cut(U, 6144, LAT_SLOTS, PAGES * ROPE)
        krT = cut(U, 7680, 4 * P)
        SQ = cut(actf, 4096, 4, GW)
        latT = cut(hf, 0, PAGES, P)
        num, rsk, SA, PA, ssq = (decs[:, i, :] for i in range(5))
        VB = cut(U, 0, DEC, NPAT, GW)
        Qbc = cut(U, 6144, DEC, GW)
        SI = cut(U, 8192, X_N)
        KB = cut(hf, 0, K_SLOTS, NPAT, GW)
        qm = cut(hf, 0, DEC, GW)
        prod = cut(actf, 3072, NPAT, GW)
        dtmp = bsum[:, 0:2, :, :].rearrange("p a b h -> p a (b h)")
        lsum = mxs[:, 0, :]
        STC = cut(actf, 0, 16, HD)
        STD = cut(actf, 1024, 32, HD)
        OUTER = cut(actf, 3072, 32, HD)

        ps = [ctx.enter_context(nc.psum_tensor(f"bank{i}", [P, 512], f32)) for i in range(8)]

        def bank(i, rows, *shape):
            return cut(ps[i], 0, *shape)[0:rows]

        ident = cst[:, K_ID:K_ID + P]
        Lmask = cut(cst, K_LV, len(LEVELS) - 1, P)
        selh = cut(cst, K_SELH, H, P)
        cos = cut(cst, K_COS, BLK, ROPE // 2)
        sin = cut(cst, K_SIN, BLK, ROPE // 2)

        def rep(ap, at, n):
            shape = list(ap.shape)
            return ap.unsqueeze(at).broadcast_to(shape[:at] + [n] + shape[at:])

        loaded = [sem(f"slot_loaded_{i}") for i in range(RING)]
        lat_loaded = [sem(f"latent_loaded_{i}") for i in range(LAT_SLOTS)]
        lat_uses = [len(range(i, DEC, LAT_SLOTS)) for i in range(LAT_SLOTS)]
        k_loaded = [sem(f"window_k_loaded_{i}") for i in range(K_SLOTS)]
        ends = [max(i for i, k in enumerate(TICKETS) if k[0] == n) + 1 for n in range(len(SLABS))]

        def slab_arrived(eng, l, n, more=0):
            eng.wait_ge(loaded[n % RING], (l * (LAYER_SLABS // RING) + more + (n // RING + 1)) * 32)

        def settled(eng):
            eng.sem_inc(sem("settled"), 1)

        block = ctx.enter_context(nc.Block())

        @block.sync
        def _(sp):
            sp.dma_start(pages[:, :], t["page_table"]).then_inc(sem("page_table_loaded"), 16)
            for b in range(2):
                sp.dma_start(xin[:, b, :], t["x_prompt"][0, b * P:(b + 1) * P, :]).then_inc(sem("x_loaded"), 16)
            sp.dma_start(xin[0:DEC, 2, :], t["x_sample"].rearrange("b s d -> (b s) d")).then_inc(sem("x_loaded"), 16)
            for dst, name in ((cst, "constants"), (gcols, "g_col"), (lbx, "lb_col"), (cbias, "c_bias")):
                sp.dma_start(dst[:], t[name]).then_inc(sem("constants_loaded"), 16)

            def ffn(l, f, n0):
                gate, up, down = (t[f"w{f + 1}_{x}"][bass.ds(l, 1)].rearrange("a (c p) n -> p (a c) n", p=P)
                                  for x in ("gate", "up", "down"))

                def gate_up(j, n):
                    dst = ring[:, n % RING, :].rearrange("p (g c n) -> p g c n", g=2, c=KC)
                    sp.dma_start(dst[:, 0], gate[:, :, bass.ds(j * (2 * P), 2 * P)]).then_inc(loaded[n % RING], 16)
                    sp.dma_start(dst[:, 1], up[:, :, bass.ds(j * (2 * P), 2 * P)]).then_inc(loaded[n % RING], 16)

                def down_tile(m, n):
                    dst = ring[:, n % RING, 0:FT * P].rearrange("p (c n) -> p c n", c=FT)
                    for k in range(0, FT, FT // 2):
                        sp.dma_start(dst[:, k:k + FT // 2], down[:, k:k + FT // 2, bass.ds(m * P, P)])\
                            .then_inc(loaded[n % RING], 16)

                tiles, outs = l * (2 * FT) + f * FT, l * (3 * KC) + (2 * KC * f + OUT_CREDIT)
                for j in range(RING):
                    if f == 0:
                        sp.wait_ge(sem("stream_out"), outs + j - 2)
                    else:
                        sp.wait_ge(sem("stream_out"), outs - KC + (OUT_SLABS[j][0] + OUT_SLABS[j][1]))
                    gate_up(j, n0 + j)
                with sp.Fori(1, NG // RING) as i:
                    for r in range(RING):
                        sp.wait_ge(sem("gate_up_out"), tiles + i * (2 * RING) + (2 * r + 2 - 2 * RING))
                        gate_up(i * RING + r, n0 + r)
                for j in range(NG // RING * RING, NG):
                    sp.wait_ge(sem("gate_up_out"), tiles + 2 * (j - RING + 1))
                    gate_up(j, n0 + j)
                for m in range(ND):
                    if m < RING:
                        sp.wait_ge(sem("gate_up_out"), tiles + 2 * (NG + m - RING + 1))
                    else:
                        sp.wait_ge(sem("stream_out"), outs + (m - RING + 1))
                    down_tile(m, n0 + NG + m)

            with sp.Fori(0, DEPTH) as l:
                ffn(l, 0, 0)
                w_in = t["w_in"][bass.ds(l, 1)].rearrange("a (c p) n -> p (a c) n", p=P)
                w_out = t["w_out"][bass.ds(l, 1)].rearrange("a (c p) n -> p (a c) n", p=P)
                parts = [(w_in, c, w) for c, w, _ in SLABS] + [(w_out, m * P, k * P) for m, k in OUT_SLABS]
                for i, (src, c, w) in enumerate(parts):
                    n = FFN_SLABS + i
                    if i < RING:
                        sp.wait_ge(sem("stream_out"), l * (3 * KC) + (KC - RING + i + 1 + OUT_CREDIT))
                    else:
                        sp.wait_ge(sem("w_in_out"), l * NTK + ends[i - RING])
                    dst = ring[:, n % RING, 0:KC * w].rearrange("p (c n) -> p c n", c=KC)
                    for k in range(0, KC, KC // 2):
                        sp.dma_start(dst[:, k:k + KC // 2], src[:, k:k + KC // 2, c:c + w]).then_inc(loaded[n % RING], 16)
                sp.wait_ge(sem("page_table_loaded"), 16)
                sp.wait_ge(sem("mixed_turned"), (l + 1) * 4)
                sp.wait_ge(sem("scratch_stored"), (l + 1) * 16 * N_SCRATCH)
                sp.wait_ge(sem("prompt_states_stored"), (l + 1) * 16 * N_PSTATE)
                latents = t["cache_mla_latent"][bass.ds(l, 1)].rearrange("a g p c -> p (a g) c")
                kropes = t["cache_mla_krope"][bass.ds(l, 1)].rearrange("a g p c -> p (a g) c")
                for b in range(DEC):
                    slot = b % LAT_SLOTS
                    if b >= LAT_SLOTS:
                        sp.wait_ge(sem("ctx_out"), l * DEC + (b - LAT_SLOTS + 1))
                    settled(sp)
                    with sp.Fori(0, PAGES) as i:
                        page = sp.value_load(pages[0:1, bass.ds(i + b * PAGES, 1)], min_val=0,
                                             max_val=t["cache_mla_latent"].shape[1] - 1)
                        sp.dma_start(lat[:, slot, bass.ds(i, 1), :], latents[:, bass.ds(page, 1), :])\
                            .then_inc(lat_loaded[slot], 16)
                        sp.dma_start(kr[:, slot, bass.ds(i * ROPE, ROPE)].rearrange("p (a c) -> p a c", a=1),
                                     kropes[:, bass.ds(page, 1), :]).then_inc(lat_loaded[slot], 16)

                def window(x, b, dst, done):
                    src = t[f"cache_swa_{x}"][bass.ds(l, 1)].rearrange("a b t w -> (a b) t w")
                    for i, (w, d) in enumerate(PATTERNS):
                        sp.dma_start(dst[:, i, :], src[b, PAST - w:PAST - w + (w // d - 1) * d + 1:d, :]).then_inc(done, 16)

                sp.wait_ge(sem("ctx_done"), (l + 1) * DEC)
                for b in range(DEC):
                    window("v", b, VB[:, b], sem("window_v_loaded"))
                for b in range(DEC):
                    if b == 0:
                        sp.wait_ge(sem("q_spread"), (l + 1) * 4)
                    if b >= K_SLOTS:
                        sp.wait_ge(sem("window_products"), l * DEC + (b - K_SLOTS + 1))
                    window("k", b, KB[:, b % K_SLOTS], k_loaded[b % K_SLOTS])
                ffn(l, 1, FFN_SLABS + MIX_SLABS)
            sp.wait_ge(sem("y_turned"), 6)
            sp.dma_start(t["y_prompt"][0].rearrange("(b p) d -> p b d", p=P), xin[:, 0:2, :]).then_inc(sem("y_stored"), 16)
            sp.dma_start(t["y_sample"].rearrange("b s d -> (b s) d"), xin[0:DEC, 2, :]).then_inc(sem("y_stored"), 16)
            sp.wait_ge(sem("y_stored"), 32)

        @block.gpsimd
        def _(pool):
            pool.memset(ones[:, :], 1.0).then_inc(sem("ones_set"), 1)
            pool.memset(eps[:, :], EPS).then_inc(sem("ones_set"), 1)
            pool.memset(TM[:, :, :], 0.0).then_inc(sem("ones_set"), 1)
            pool.memset(qrb[:, :, :, :], 0.0).then_inc(sem("ones_set"), 1)

            def shift(l, f):
                n = (PAST - 1) * GW
                for b in range(DEC // 2):
                    pool.wait_ge(sem("ffn_tiles"), l * (2 * FT) + (f * FT + 5 * b + 1 + CREDIT))
                    for x in ("k", "v"):
                        src = t[f"cache_swa_{x}"][bass.ds(l, 1)].rearrange("a b t w -> (a b) (t w)")
                        dst = t[f"s_swa_{x}"][bass.ds(l, 1)].rearrange("a b t w -> (a b) (t w)")
                        i = f * (DEC // 2) + b
                        pool.dma_start(dst[i:i + 1, 0:n].rearrange("a (q n) -> (a q) n", q=64),
                                       src[i:i + 1, GW:GW + n].rearrange("a (q n) -> (a q) n", q=64))\
                            .then_inc(sem("window_shifted"), 16)

            with pool.Fori(0, DEPTH) as l:
                pool.dma_start(gains[:, :], t["gains"][bass.ds(l, 1)].rearrange("a n -> (a n)").partition_broadcast(P))\
                    .then_inc(sem("small_loaded"), 16)
                pool.dma_start(wuq[:, :, :], t["a_wuq"][bass.ds(l, 1)].rearrange("a (c p) n -> p (a c) n", p=P))\
                    .then_inc(sem("small_loaded"), 16)
                pool.dma_start(wukv[:, :, :], t["a_wukv"][bass.ds(l, 1)].rearrange("a p (h n) -> p (a h) n", h=H))\
                    .then_inc(sem("small_loaded"), 16)
                shift(l, 0)
                pool.wait_ge(sem("rows_final"), l + 1)
                for name, c, w in (("mla_latent", CKV, KVL), ("mla_krope", CKR, ROPE), ("swa_k", BK, GW), ("swa_v", BV, GW)):
                    pool.dma_start(t["p_" + name][bass.ds(l, 1)].rearrange("a (b p) w -> p (a b) w", p=P),
                                   TM[:, 0:2, c:c + w]).then_inc(sem("rows_stored"), 16)
                    dst = t["s_" + name][bass.ds(l, 1)]
                    if name[0:3] == "mla":
                        dst = dst.rearrange("a b w -> (a b) w")
                    else:
                        dst = dst[:, :, PAST - 1:PAST, :].rearrange("a b t w -> (a b) (t w)")
                    pool.dma_start(dst, TM[0:DEC, 2, c:c + w]).then_inc(sem("rows_stored"), 16)
                pool.wait_ge(sem("mlstm_state"), l + 1)
                pool.dma_start(t["p_mlstm_C"][bass.ds(l, 1)].rearrange("a h k v -> k (a h) v"), CGS[0:HD, :, 0:HD])\
                    .then_inc(sem("prompt_states_stored"), 16)
                pool.dma_start(t["p_mlstm_n"][bass.ds(l, 1)].rearrange("a h k -> k (a h)").unsqueeze(2),
                               CGS[0:HD, :, HD:HD + 1], allow_slow_non_contiguous=True).then_inc(sem("prompt_states_stored"), 16)
                pool.dma_start(t["p_mlstm_m"][bass.ds(l, 1)].rearrange("a (h o) -> (a h) o", o=1),
                               CG[0:H, 7, SEQ - 1:SEQ]).then_inc(sem("prompt_states_stored"), 16)
                pool.wait_ge(sem("hgrn_state"), l + 1)
                pool.dma_start(t["p_hgrn_S"][bass.ds(l, 1)].rearrange("a h k v -> k (a h) v"), DGS)\
                    .then_inc(sem("prompt_states_stored"), 16)
                scr = t["scratch"][bass.ds(l, 1)].rearrange("a b h x -> (a b) h x")
                for g in range(4):
                    pool.dma_start(scr[:, :, g * HD:(g + 1) * HD],
                                   TM[0:DEC, 2, MQ + g * GW:MQ + (g + 1) * GW].rearrange("b (h d) -> b h d", h=H))\
                        .then_inc(sem("scratch_stored"), 16)
                for x, c in ((X_CO, GATE), (X_DG, GATE + GW)):
                    pool.dma_start(scr[:, :, x:x + HD], TM[0:DEC, 2, c:c + GW].rearrange("b (h d) -> b h d", h=H))\
                        .then_inc(sem("scratch_stored"), 16)
                for g in range(3):
                    pool.dma_start(scr[:, :, X_QD + g * DK:X_QD + (g + 1) * DK], SM[0:DEC, g])\
                        .then_inc(sem("scratch_stored"), 16)
                for g in range(2):
                    pool.dma_start(scr[:, :, X_I + g:X_I + g + 1], gTs[:, g, :].unsqueeze(2), allow_slow_non_contiguous=True)\
                        .then_inc(sem("scratch_stored"), 16)
                for b in range(DEC):
                    pool.wait_ge(sem("latent_max"), l * DEC + b + 1)
                    settled(pool)
                    pool.partition_all_reduce(lmx[:, 1, :], lmx[:, 0, :], P, RMAX)\
                        .then_inc(sem("latent_max_all"), 1)
                pool.wait_ge(sem("ctx_done"), (l + 1) * DEC)
                pool.wait_ge(sem("scratch_stored"), (l + 1) * 16 * N_SCRATCH)
                for j in range(4):
                    rows = slice(32 * j, 32 * j + 32)
                    pool.dma_start(SI[rows, :], scr.rearrange("b h x -> (b h) x")).then_inc(sem("state_loaded"), 16)
                    pool.dma_start(STC[rows], t["state_mlstm_C"][bass.ds(l, 1)].rearrange(
                        "a b h k v -> (a b h) k v")[:, 16 * j:16 * j + 16, :]).then_inc(sem("state_loaded"), 16)
                    pool.dma_start(nst[rows], t["state_mlstm_n"][bass.ds(l, 1)].rearrange(
                        "a b h k -> (a b h) k")[:, 16 * j:16 * j + 16]).then_inc(sem("state_loaded"), 16)
                    pool.dma_start(sst[rows, 0:1], t["state_mlstm_m"][bass.ds(l, 1)].rearrange(
                        "a b (h o) -> (a b h) o", o=1)).then_inc(sem("state_loaded"), 16)
                    pool.dma_start(STD[rows], t["state_hgrn_S"][bass.ds(l, 1)].rearrange(
                        "a b h k v -> (a b h) k v")[:, 32 * j:32 * j + 32, :]).then_inc(sem("state_loaded"), 16)
                pool.wait_ge(sem("states_updated"), l + 1)
                for j in range(4):
                    rows = slice(32 * j, 32 * j + 32)
                    pool.dma_start(t["s_mlstm_C"][bass.ds(l, 1)].rearrange(
                        "a b h k v -> (a b h) k v")[:, 16 * j:16 * j + 16, :], STC[rows]).then_inc(sem("sample_states_stored"), 16)
                    pool.dma_start(t["s_mlstm_n"][bass.ds(l, 1)].rearrange(
                        "a b h k -> (a b h) k")[:, 16 * j:16 * j + 16], nst[rows]).then_inc(sem("sample_states_stored"), 16)
                    pool.dma_start(t["s_hgrn_S"][bass.ds(l, 1)].rearrange(
                        "a b h k v -> (a b h) k v")[:, 32 * j:32 * j + 32, :], STD[rows]).then_inc(sem("sample_states_stored"), 16)
                pool.dma_start(t["s_mlstm_m"][bass.ds(l, 1)].rearrange("a b (h o) -> (a b h) o", o=1),
                               sst[0:32, 3:4]).then_inc(sem("sample_states_stored"), 16)
                pool.wait_ge(sem("window_max"), l + 1)
                settled(pool)
                pool.partition_all_reduce(wmx[:, 2, :], wmx[:, 0, :], P, RMAX)\
                    .then_inc(sem("window_max_all"), 1)
                pool.wait_ge(sem("mixer_done"), l + 1)
                shift(l, 1)
            pool.wait_ge(sem("window_shifted"), DEPTH * DEC * 2 * 16)
            pool.wait_ge(sem("rows_stored"), DEPTH * N_STORE * 16)
            pool.wait_ge(sem("prompt_states_stored"), DEPTH * N_PSTATE * 16)
            pool.wait_ge(sem("sample_states_stored"), DEPTH * N_SSTATE * 16)
        @block.scalar
        def _(act):
            act.preload_act_table_set("natural_log_exp_and_others")
            act.wait_ge(sem("ones_set"), 4)
            act.wait_ge(sem("lb_shifted"), 1)
            act.activation(lbs[:, :, 0:H], lbs[:, :, H:2 * H], ACT.Exp).then_inc(sem("lb_exp"), 1)
            for c in range(KC):
                act.wait_ge(sem("x_turned"), c + 1)
                act.copy(x_T[:, c, :], bank(c, P, NT)).then_inc(sem("x_copied"), 1)

            def inverse_roots(dst, src, widths):
                for a, b, w in widths:
                    act.activation(dst[:, a:b], src[:, a:b], ACT.Ln, bias=eps[0:dst.shape[0], :], scale=1.0 / w)
                act.drain()
                lo, hi = widths[0][0], widths[-1][1]
                return act.activation(dst[:, lo:hi], dst[:, lo:hi], ACT.Exp, scale=-0.5)

            def norm(l, k):
                act.wait_ge(sem("mean_square"), l * 3 + (k + 1))
                inverse_roots(rstd, bank(6, P, NT), [(0, NT, D_MODEL)]).then_inc(sem("rstd_ready"), 1)

            def ffn(l, f):
                with act.Fori(0, FT // 2) as j:
                    for q in range(2):
                        act.wait_ge(sem("gate_up_out"), l * (2 * FT) + j * 2 + (f * FT + q + 1))
                        act.activation(sg[:, q, :], bank(2 * q, P, NT), ACT.Exp, scale=-1.0).then_inc(sem("gate_exp"), 1)

            def copy_out(l, first, last):
                for k in range(first, last):
                    n, kind, i = TICKETS[k]
                    act.wait_ge(sem("w_in_out"), l * NTK + (k + 1))
                    if kind == "rows":
                        w = GW if n == 4 else SLABS[n][1]
                        dst, src = TM[0:ROWS[i], i, SLABS[n][2]:SLABS[n][2] + w], bank(k % 4, ROWS[i], w)
                    elif kind == "gate":
                        dst, src = sg[0:H, i, :], bank(k % 4, H, NT)
                    else:
                        dst, src = (QD if n == 6 else FD)[:, i, :], bank(k % 4, P, NT)
                    act.copy(dst, src).then_inc(sem("w_in_copied"), 1)

            def softmax_exp(l, a):
                act.wait_ge(sem("scores_shifted"), l * 2 + (a + 1))
                act.activation(S[:, :, :], S[:, :, :], ACT.Exp).then_inc(sem("scores_exp"), 1)
                for h in range(H):
                    act.wait_ge(sem("probs_turned"), (l * 2 + a) * H + (h + 1))
                    act.copy(PT[:, h, :], bank(4 + h, P, 3 * P)).then_inc(sem("probs_copied"), 1)

            with act.Fori(0, DEPTH) as l:
                norm(l, 0)
                ffn(l, 0)
                norm(l, 1)
                copy_out(l, 0, 9)
                act.wait_ge(sem("squares1"), l + 1)
                for a, b, w in ((0, 3, QL), (3, 6, KVL), (6, 9, ROPE), (9, 33, HD)):
                    act.activation(rs[:, a:b], st[:, a:b], ACT.Ln, bias=eps[:, :], scale=1.0 / w)
                act.drain()
                act.activation(rs[:, 0:33], rs[:, 0:33], ACT.Exp, scale=-0.5).then_inc(sem("roots1"), 1)
                act.wait_ge(sem("down_turned"), l + 1)
                act.copy(cqT[:, 0, :], bank(4, P, NT))
                act.copy(cqT[:, 1, :], bank(5, P, NT))
                act.copy(latn[:, :], bank(6, P, NT)).then_inc(sem("down_copied"), 1)
                copy_out(l, 9, 12)
                act.wait_ge(sem("qk_cleared"), l + 1)
                act.wait_ge(sem("up_out"), l * 2 + 1)
                for i, bk in enumerate((4, 5, 7)):
                    act.copy(Qk[0:ROWS[i], i], bank(bk, ROWS[i], H, QKW))
                for i in range(2):
                    last = act.copy(Kk[:, i, :, 0:NOPE], cut(ps[6], i * GW, H, NOPE))
                last.then_inc(sem("up_copied"), 1)
                act.wait_ge(sem("up_out"), l * 2 + 2)
                act.copy(Kk[0:DEC, 2, :, 0:NOPE], bank(4, DEC, H, NOPE)).then_inc(sem("up_copied"), 1)
                copy_out(l, 12, ends[5])
                act.wait_ge(sem("squares2"), l + 1)
                for a, b, w in ((0, 12, NOPE), (12, 24, ROPE), (24, 36, NOPE)):
                    act.activation(rs[:, a:b], st[:, a:b], ACT.Ln, bias=eps[:, :], scale=1.0 / w)
                act.drain()
                act.activation(rs[:, :], rs[:, :], ACT.Exp, scale=-0.5).then_inc(sem("roots2"), 1)
                act.wait_ge(sem("qk_turned"), l * 2 + 1)
                for i in range(2):
                    act.copy(QT[0:QKW, 2 * i:2 * i + 2, :], bank(4 + i, QKW, 2, SEQ))
                for i in range(2):
                    last = act.copy(KT[0:QKW, 2 * i:2 * i + 2, :], bank(6 + i, QKW, 2, SEQ))
                last.then_inc(sem("qk_copied"), 1)
                act.wait_ge(sem("qk_turned"), l * 2 + 2)
                act.copy(qtT[0:HD], bank(4, HD, H, DEC))
                for j in range(4):
                    rows = slice(32 * j, 32 * j + 32)
                    act.copy(qrb[rows, :, j, :].rearrange("p b h -> p h b"), cut(ps[4], H * DEC, H, DEC)[rows])
                act.copy(wukT[0:HD], bank(5, HD, H, P))
                act.copy(nsA[:, :], bank(6, P, DEC * H))
                act.copy(wuk[:, 0:GW].rearrange("p (h d) -> p h d", h=H), wukv[:, :, 0:NOPE])\
                    .then_inc(sem("qk_copied"), 1)
                act.wait_ge(sem("u_out"), l + 1)
                act.copy(wuk[:, GW:].rearrange("p (b h) -> p h b", b=DEC), bank(7, P, H, DEC)).then_inc(sem("u_copied"), 1)
                copy_out(l, ends[5], ends[7])
                act.wait_ge(sem("pairs_turned"), l + 1)
                for i in range(4):
                    last = act.copy(pairT[:, i], bank(4 + i, P, 2, SEQ))
                last.then_inc(sem("pairs_copied"), 1)
                copy_out(l, ends[7], NTK)
                act.drain()
                act.activation(E1g[:, :, :], TM[:, :, GATE:TMW], ACT.Exp, scale=-1.0).then_inc(sem("gates_exp"), 1)
                softmax_exp(l, 0)
                act.wait_ge(sem("prompt_out"), l * 2 + 1)
                for i in range(2):
                    last = act.copy(ctxT[:, 2 * i:2 * i + 2, 0:SEQ], bank(4 + i, P, 2, SEQ))
                last.then_inc(sem("prompt_copied"), 1)
                softmax_exp(l, 1)
                act.wait_ge(sem("prompt_out"), l * 2 + 2)
                for i in range(2):
                    last = act.copy(o_T[:, 2 + i, 0:SEQ], bank(4 + i, P, SEQ))
                last.then_inc(sem("prompt_copied"), 1)
                act.wait_ge(sem("mgate"), l + 1)
                act.activation(CG[0:H, 2, :], CG[0:H, 2, :], ACT.Exp, scale=-1.0)
                act.drain()
                act.activation(CG[0:H, 2, :], CG[0:H, 2, :], ACT.Ln, bias=1.0).then_inc(sem("mgate_log"), 1)
                act.wait_ge(sem("mweights"), l + 1)
                act.activation(WT[:, :, :], WT[:, :, :], ACT.Exp, scale=-1.0)
                act.activation(wd[:, :, :], wd[:, :, :], ACT.Exp, scale=-1.0)
                act.activation(emt[:, :, :], gT[:, 2:4, :], ACT.Exp, scale=-1.0).then_inc(sem("mweights_exp"), 1)
                act.wait_ge(sem("forget_bounded"), l + 1)
                act.activation(E1[:, :, :], FD[:, :, :], ACT.Exp, scale=-1.0)
                act.activation(D1[:, :, :], QD[:, :, :], ACT.Exp, scale=-1.0).then_inc(sem("dgates_exp"), 1)
                act.wait_ge(sem("forget_ready"), l + 1)
                act.activation(D1[:, :, :], FD[:, :, :], ACT.Ln).then_inc(sem("forget_log"), 1)
                for i, half in enumerate(LEVELS):
                    act.wait_ge(sem("level_diff"), l * len(LEVELS) + (i + 1))
                    if half > 1:
                        dv, ev = (v.rearrange("p h (n r s) -> p (h n) r s", r=2, s=half) for v in (D1v, E1v))
                        act.activation(ev[:, :, 0, :], dv[:, :, 0, :], ACT.Exp, scale=-1.0)
                        act.activation(ev[:, :, 1, :], dv[:, :, 1, :], ACT.Exp).then_inc(sem("level_exp"), 1)
                    else:
                        act.activation(E1v, D1v, ACT.Exp)
                        act.activation(E2[:, :, :], D1v, ACT.Exp, scale=-1.0).then_inc(sem("level_exp"), 1)
                act.wait_ge(sem("levels_done"), l + 1)
                for h in range(H):
                    last = act.activation(E1v[:, h, :], FD[:, h, 0:SEQ], ACT.Exp, scale=-1.0, bias=FD[:, h, SEQ - 1:SEQ])
                last.then_inc(sem("end_exp"), 1)
                act.wait_ge(sem("end_turned"), l + 1)
                for i in range(2):
                    act.copy(KE[:, i], bank(6 + i, P, H, DK))
                for i in range(3):
                    last = act.copy(SM[0:DEC, i], bank(i, DEC, H, DK))
                last.then_inc(sem("end_copied"), 1)
                act.wait_ge(sem("squares3"), l + 1)
                inverse_roots(rs, st, [(0, 16, HD)]).then_inc(sem("roots3"), 1)
                for i in range(4):
                    act.wait_ge(sem("mixed_out"), l * 4 + (i + 1))
                    act.copy(o_T[:, 4 + i, 0:SEQ], bank(4 + i, P, SEQ)).then_inc(sem("mixed_turned"), 1)
                for b in range(DEC):
                    act.wait_ge(sem("kr_turned"), l * DEC + (b + 1))
                    act.copy(krT, bank(2, P, 4 * P)).then_inc(sem("kr_copied"), 1)
                    for c in range(4):
                        act.wait_ge(sem("lat_turned"), (l * DEC + b) * 4 + (c + 1))
                        act.copy(latT[:, 4 * c:4 * c + 4, :], bank(c % 2, P, 4, P)).then_inc(sem("lat_copied"), 1)
                        for g in range(4 * c, 4 * c + 4):
                            n = (l * DEC + b) * PAGES + g
                            act.wait_ge(sem("page_out"), n + 1)
                            act.activation(SQ[:, g % 4, :], bank(4 + g % 4, P, GW), ACT.Square).then_inc(sem("page_squared"), 1)
                    act.wait_ge(sem("page_taken"), (l * DEC + b + 1) * PAGES)
                    inverse_roots(rsk, ssq, [(0, PAGES * H, NOPE)]).then_inc(sem("page_roots"), 1)
                    act.wait_ge(sem("latent_shifted"), l * DEC + (b + 1))
                    act.activation(PA, SA, ACT.Exp, scale=A_SCALE).then_inc(sem("latent_exp"), 1)
                act.wait_ge(sem("oA_out"), l + 1)
                for i in range(2):
                    last = act.copy(o_T[:, i, :], bank(4 + i, P, NT))
                last.then_inc(sem("oA_copied"), 1)
                for i in range(4):
                    act.wait_ge(sem("q_spread"), l * 4 + (i + 1))
                    last = act.copy(Qbc[:, 2 * i:2 * i + 2, :], bank(i, P, 2, GW))
                last.then_inc(sem("q_spread_copied"), 1)
                act.wait_ge(sem("vnew_turned"), l + 1)
                act.copy(wmx[:, 1, :], bank(6, P, DEC * H))
                act.copy(vT[:, :, :], bank(7, P, 2, DEC)).then_inc(sem("vnew_copied"), 1)
                act.wait_ge(sem("state_m"), l + 1)
                act.activation(sst[:, 7:10], sst[:, 4:7], ACT.Exp).then_inc(sem("state_exp"), 1)
                act.wait_ge(sem("squares4"), l + 1)
                inverse_roots(rs[0:32], st[0:32], [(0, 2, HD)]).then_inc(sem("roots4"), 1)
                act.wait_ge(sem("states_turned"), l + 1)
                for g in range(2):
                    for h in range(H):
                        src = cut(ps[4 + g], 0, DEC, H)[0:HD, :, h]
                        last = act.copy(o_T[HD * (h % 2):HD * (h % 2) + HD, 4 + 2 * g + h // 2, SEQ:NT], src)
                last.then_inc(sem("states_copied"), 1)
                act.wait_ge(sem("window_shifted_max"), l + 1)
                act.activation(SB[:, :, :, :], SB[:, :, :, :], ACT.Exp, scale=B_SCALE)
                act.activation(wmx[:, 3, :], wmx[:, 3, :], ACT.Exp, scale=B_SCALE).then_inc(sem("window_exp"), 1)
                act.wait_ge(sem("rows_stored"), (l + 1) * 16 * N_STORE)
                act.wait_ge(sem("scratch_stored"), (l + 1) * 16 * N_SCRATCH)
                norm(l, 2)
                ffn(l, 1)
            for b in range(BLK):
                for g in range(2):
                    i = 2 * b + g
                    act.wait_ge(sem("y_out"), i + 1)
                    act.copy(xin[0:ROWS[b], b, g * 512:g * 512 + 512], bank(i, ROWS[b], 512)).then_inc(sem("y_turned"), 1)

        @block.vector
        def _(dve):
            dve.memset(sqx[:, :], 0.0).then_inc(sem("ffn_tiles"), CREDIT)
            dve.memset(ssum[:, :], 0.0).then_inc(sem("stream_added"), CREDIT)
            dve.memset(sst[:, :], 0.0).then_inc(sem("stream_out"), OUT_CREDIT)
            dve.wait_ge(sem("constants_loaded"), 4 * 16)
            dve.tensor_reduce(lbt[:, 0, :], lbx[:, :, :].rearrange("p l h -> p h l"), AX.X, MAX)
            dve.drain()
            dve.tensor_tensor(lbs[:, :, H:2 * H], lbx[:, :, :], rep(lbt[:, 0, :], 1, DEPTH), SUB).then_inc(sem("lb_shifted"), 1)
            dve.wait_ge(sem("lb_exp"), 1)
            dve.tensor_reduce(lbt[:, 0, :], lbs[:, :, 0:H].rearrange("p l h -> p h l"), AX.X, ADD)
            dve.drain()
            dve.reciprocal(lbt[:, 1, :], lbt[:, 0, :])
            dve.drain()
            dve.tensor_tensor(lbs[:, :, 0:H], lbs[:, :, 0:H], rep(lbt[:, 1, :], 1, DEPTH), MUL)
            dve.memset(lbt[:, 0, :], 0.0)
            dve.drain()
            for i in range(DEPTH):
                if i:
                    dve.tensor_tensor(lbt[:, 0, :], lbt[:, 0, :], lbs[:, i, 0:H], ADD)
                    dve.drain()
                dve.tensor_copy(lbs[:, i, 0:H], lbt[:, 0, :])
                dve.tensor_scalar(lbs[:, i, H:2 * H], lbt[:, 0, :], -1.0, 1.0, MUL, ADD)
            for c in range(KC):
                dve.wait_ge(sem("x_copied"), c + 1)
                dve.drain()
                dve.tensor_tensor(sqx[:, :], x_T[:, c, :], x_T[:, c, :], MUL)
                dve.drain()
                last = dve.tensor_tensor(ssum[:, :], ssum[:, :], sqx[:, :], ADD)
            last.then_inc(sem("squares_ready"), 1)

            def norm(l, k):
                dve.wait_ge(sem("rstd_ready"), l * 3 + (k + 1))
                for c in range(KC):
                    dve.scalar_tensor_tensor(h_T[:, c, :], x_T[:, c, :], gcol[:, k * KC + c:k * KC + c + 1], rstd[:, :],
                                             MUL, MUL).then_inc(sem("h_ready"), 1)

            def ffn(l, f):
                with dve.Fori(0, FT // 2) as j:
                    for q in range(2):
                        dve.wait_ge(sem("gate_exp"), l * (2 * FT) + j * 2 + (f * FT + q + 1))
                        dve.tensor_scalar(sg[:, q, :], sg[:, q, :], 1.0, None, ADD)
                        dve.drain()
                        dve.reciprocal(sg[:, q, :], sg[:, q, :])
                        dve.drain()
                        dve.tensor_tensor(sg[:, q, :], sg[:, q, :], bank(2 * q, P, NT), MUL)
                        dve.drain()
                        dve.tensor_tensor(act_T[:, bass.ds(j * 2 + q, 1), :].rearrange("p a t -> p (a t)"), sg[:, q, :],
                                          bank(2 * q + 1, P, NT), MUL).then_inc(sem("ffn_tiles"), 1)

            def stream(l, k, factor):
                for m in range(KC):
                    dve.wait_ge(sem("stream_out"), l * (3 * KC) + (k * KC + m + 1 + OUT_CREDIT))
                    dve.scalar_tensor_tensor(x_T[:, m, :], bank(4 + m % 2, P, NT), factor, x_T[:, m, :], MUL, ADD)\
                        .then_inc(sem("stream_added"), 1)
                    dve.drain()
                    dve.tensor_tensor(sqx[:, :] if m else ssum[:, :], x_T[:, m, :], x_T[:, m, :], MUL)
                    dve.drain()
                    if m:
                        last = dve.tensor_tensor(ssum[:, :], ssum[:, :], sqx[:, :], ADD)
                last.then_inc(sem("squares_ready"), 1)

            def gain(at, w, *reps):
                g = gains[:, at:at + w]
                for n in reversed(reps):
                    g = rep(g, 1, n)
                return g

            def rope(x, c, s, tmp):
                dve.tensor_tensor(tmp[0], x[0], c, MUL)
                dve.tensor_tensor(tmp[1], x[1], s, MUL)
                dve.tensor_tensor(tmp[2], x[0], s, MUL)
                dve.tensor_tensor(tmp[3], x[1], c, MUL)
                dve.drain()
                dve.tensor_tensor(x[0], tmp[0], tmp[1], SUB)
                return dve.tensor_tensor(x[1], tmp[2], tmp[3], ADD)

            def softmax(l, a, scale, mask, times):
                for h in range(H):
                    dve.wait_ge(sem("scores_out"), (l * 2 + a) * H + (h + 1))
                    dve.scalar_tensor_tensor(S[:, h, :], bank(4 + h, P, 3 * P), scale, cst[:, mask:mask + 3 * P], MUL, ADD)\
                        .then_inc(sem("scores_taken"), 1)
                dve.drain()
                tiles = (S[:, :, 0:P], S[:, :, P:3 * P])
                for i in range(2):
                    dve.tensor_reduce(mxs[:, i, :], tiles[i], AX.X, MAX)
                dve.drain()
                for i in range(2):
                    last = dve.tensor_tensor(tiles[i], tiles[i], rep(mxs[:, i, :], 2, P + i * P), SUB)
                last.then_inc(sem("scores_shifted"), 1)
                dve.wait_ge(sem("scores_exp"), l * 2 + (a + 1))
                if times is not None:
                    dve.tensor_tensor(S[:, :, :], S[:, :, :], rep(cst[:, times:times + 3 * P], 1, H), MUL)
                    dve.drain()
                for i in range(2):
                    dve.tensor_reduce(mxs[:, i, :], tiles[i], AX.X, ADD)
                dve.drain()
                dve.reciprocal(mxs[:, :, :], mxs[:, :, :])
                dve.drain()
                for i in range(2):
                    last = dve.tensor_tensor(tiles[i], tiles[i], rep(mxs[:, i, :], 2, P + i * P), MUL)
                last.then_inc(sem("probs_ready"), 1)

            def latent_rows(l):
                dve.wait_ge(sem("small_loaded"), (l + 1) * 3 * 16)
                dve.wait_ge(sem("w_in_copied"), l * NTK + 9)
                dve.tensor_tensor(sq1, TM[:, :, 0:BV], TM[:, :, 0:BV], MUL)
                dve.drain()
                dve.tensor_reduce(st[:, 0:3], sq1[:, :, CQ:CKV], AX.X, ADD)
                dve.tensor_reduce(st[:, 3:6], sq1[:, :, CKV:CKR], AX.X, ADD)
                dve.tensor_reduce(st[:, 6:9], sq1[:, :, CKR:BQ], AX.X, ADD)
                dve.tensor_reduce(st[:, 9:33].rearrange("p (b g) -> p b g", b=BLK),
                                  sq1[:, :, BQ:BV].rearrange("p b (g d) -> p b g d", d=HD), AX.X, ADD)\
                    .then_inc(sem("squares1"), 1)
                dve.wait_ge(sem("roots1"), l + 1)
                for b in range(BLK):
                    for c, w, r, g in ((CQ, QL, b, G_Q), (CKV, KVL, 3 + b, G_KV), (CKR, ROPE, 6 + b, G_KR)):
                        dve.scalar_tensor_tensor(TM[:, b, c:c + w], TM[:, b, c:c + w], rs[:, r:r + 1],
                                                 gains[:, g:g + w], MUL, MUL)
                qkb = TM[:, :, BQ:BV].rearrange("p b (g d) -> p b g d", d=HD)
                dve.tensor_tensor(qkb, qkb, rep(rs[:, 9:33].rearrange("p (b g) -> p b g", b=BLK), 3, HD), MUL)
                dve.drain()
                for i, g in enumerate((G_BQ, G_BK)):
                    dve.tensor_tensor(qkb[:, :, i * H:i * H + H, :], qkb[:, :, i * H:i * H + H, :], gain(g, HD, BLK, H), MUL)
                half = ROPE // 2
                rope((TM[:, :, CKR:CKR + half], TM[:, :, CKR + half:BQ]), cos, sin,
                     [cut(rp[:, i, :], 0, BLK, half) for i in range(4)]).then_inc(sem("rows_final"), 1)
                dve.memset(Qk[:, 2], 0.0)
                dve.memset(Kk[:, 2], 0.0).then_inc(sem("qk_cleared"), 1)

            def latent_qk(l):
                dve.wait_ge(sem("up_copied"), l * 2 + 2)
                dve.tensor_tensor(sq2, Qk, Qk, MUL)
                dve.tensor_tensor(sq3, Kk[:, :, :, 0:NOPE], Kk[:, :, :, 0:NOPE], MUL)
                dve.drain()
                for at, v in ((0, sq2[:, :, :, 0:NOPE]), (12, sq2[:, :, :, NOPE:]), (24, sq3)):
                    last = dve.tensor_reduce(st[:, at:at + 12].rearrange("p (b h) -> p b h", b=BLK), v, AX.X, ADD)
                last.then_inc(sem("squares2"), 1)
                dve.wait_ge(sem("roots2"), l + 1)
                parts = ((0, Qk[:, :, :, 0:NOPE], G_QN, NOPE), (12, Qk[:, :, :, NOPE:], G_QR, ROPE),
                         (24, Kk[:, :, :, 0:NOPE], G_KN, NOPE))
                for at, v, g, w in parts:
                    dve.tensor_tensor(v, v, rep(rs[:, at:at + 12].rearrange("p (b h) -> p b h", b=BLK), 3, w), MUL)
                dve.drain()
                for at, v, g, w in parts:
                    dve.tensor_tensor(v, v, gain(g, w, BLK, H), MUL)
                dve.tensor_copy(Kk[:, :, :, NOPE:], rep(TM[:, :, CKR:BQ], 2, H))
                dve.drain()
                mid = NOPE + ROPE // 2
                rope((Qk[:, :, :, NOPE:mid], Qk[:, :, :, mid:]), rep(cos, 2, H), rep(sin, 2, H),
                     [cut(rp[:, i, :], 0, BLK, H, ROPE // 2) for i in range(4)])
                dve.drain()
                s = slice(0, DEC)
                dve.tensor_tensor(qk[s], Qk[s, 2], Kk[s, 2], MUL)
                dve.tensor_tensor(qtl[s], Qk[s, 2, :, 0:NOPE], rep(gains[s, G_KN:G_KN + NOPE], 1, H), MUL)
                dve.tensor_copy(q4[s], rep(Qk[s, 2, :, NOPE:], 2, 4))
                dve.drain()
                dve.tensor_reduce(nst1[:, 0, :], qk[s], AX.X, ADD)
                dve.drain()
                dve.tensor_tensor(nsm[:, 0], rep(nst1[:, 0, :], 1, DEC), rep(ident[s, 0:DEC], 2, H), MUL)\
                    .then_inc(sem("qk_final"), 1)

            def output_gates(l):
                dve.wait_ge(sem("gates_exp"), l + 1)
                dve.tensor_scalar(E1g, E1g, 1.0, None, ADD)
                dve.drain()
                dve.reciprocal(E1g, E1g)
                dve.drain()
                dve.tensor_copy(TM[:, :, GATE:GATE + GW], E1g[:, :, 0:GW])
                dve.tensor_tensor(TM[:, :, GATE + GW:], TM[:, :, GATE + GW:], E1g[:, :, GW:], MUL)
                dve.drain()
                dve.tensor_tensor(TM[:, :, GATE:], TM[:, :, GATE:], gain(G_OUT, 2 * GW, BLK), MUL)

            def mlstm(l):
                dve.wait_ge(sem("w_in_out"), (l + 1) * NTK)
                r = slice(0, H)
                T = slice(0, SEQ)
                dve.tensor_scalar(CG[r, 0, :], sg[r, 0, :], cb[:, 0:1], None, ADD)
                dve.tensor_scalar(CG[r, 3, :], sg[r, 1, :], cb[:, 1:2], None, ADD)
                dve.drain()
                dve.tensor_scalar(CG[r, 6, :], CG[r, 3, :], 0.0, None, MIN)
                dve.scalar_tensor_tensor(CG[r, 2, :], CG[r, 3, :], -1.0, CG[r, 3, :], MUL, MAX).then_inc(sem("mgate"), 1)
                dve.wait_ge(sem("mgate_log"), l + 1)
                dve.tensor_tensor(CG[r, 1, :], CG[r, 6, :], CG[r, 2, :], SUB)
                dve.drain()
                dve.tensor_tensor_scan(CG[r, 3, T], ones[r, T], CG[r, 1, T], 0.0, MUL, ADD)
                dve.drain()
                dve.tensor_tensor(CG[r, 4, T], CG[r, 0, T], CG[r, 3, T], SUB)
                dve.drain()
                dve.tensor_tensor_scan(CG[r, 5, T], CG[r, 4, T], CG[r, 4, T], 0.0, MAX, MAX)
                dve.drain()
                dve.tensor_tensor(CG[r, 7, T], CG[r, 5, T], CG[r, 3, T], ADD).then_inc(sem("mgates_ready"), 1)
                dve.wait_ge(sem("mgates_out"), l + 1)
                dve.tensor_copy(gT[:, 0:4, :], bank(6, P, 4, H))
                dve.tensor_copy(gTs[:, :, :], cut(ps[6], 4 * H, 2, H)[0:DEC])
                for i in range(2):
                    dve.tensor_copy(gT[:, 4, 2 * i:2 * i + 2], bank(4 + i, P, 2, SEQ)[:, :, SEQ - 1])
                dve.drain()
                for h in range(H):
                    m = bank(4 + h // 2, P, 2, SEQ)[:, h % 2, :]
                    dve.tensor_scalar(WT[:, h, 0:SEQ], m, gT[:, 0, h:h + 1], 0.0, SUB, MAX)
                    dve.tensor_scalar(WT[:, h, SEQ:], m[:, P:SEQ], gT[:, 1, h:h + 1], 0.0, SUB, MAX)
                dve.tensor_tensor(wd[:, :, :], rep(gT[:, 4, :], 1, 2), gT[:, 0:2, :], SUB)
                dve.drain()
                dve.tensor_scalar(wd[:, :, :], wd[:, :, :], 0.0, None, MAX).then_inc(sem("mweights"), 1)
                dve.memset(vaug[:, :, :, HD:HD + 1], 1.0)
                dve.tensor_copy(vaug[:, :, :, 0:HD], TM[:, 0:2, MV:MV + GW].rearrange("p b (h d) -> p b h d", h=H))
                dve.wait_ge(sem("mweights_exp"), l + 1)
                dve.tensor_tensor(WT, WT, rep(cst[:, K_WM:K_WM + 3 * P], 1, H), MUL)
                dve.tensor_scalar(wd[:, :, :], wd[:, :, :], M_SCALE, None, MUL)
                dve.drain()
                dve.tensor_tensor(kw, TM[:, 0:2, MK:MK + GW].rearrange("p b (h d) -> p b h d", h=H),
                                  rep(wd[:, :, :], 3, HD), MUL).then_inc(sem("mkeys_ready"), 1)
                for h in range(H):
                    dve.wait_ge(sem("mscores_out"), l * H + (h + 1))
                    dve.tensor_tensor(S[:, h, :], bank(h, P, 3 * P), WT[:, h, :], MUL).then_inc(sem("mprobs_ready"), 1)
                dve.wait_ge(sem("mlstm_out"), l + 1)
                for i in range(2):
                    dve.tensor_copy(den[:, i, :], bank(4 + i, P, H, HD + 1)[:, :, HD])
                dve.tensor_copy(CGS[0:HD], bank(6, HD, H, HD + 1)).then_inc(sem("mlstm_state"), 1)
                dve.drain()
                dend = den[:, :, :].rearrange("p b h -> p (b h)")
                dve.scalar_tensor_tensor(dend, dend, -1.0, dend, MUL, MAX)
                dve.drain()
                dve.tensor_tensor(den[:, :, :], den[:, :, :], emt[:, :, :], MAX)
                dve.drain()
                dve.reciprocal(den[:, :, :], den[:, :, :])
                dve.drain()
                for i in range(2):
                    last = dve.tensor_tensor(HCD[:, i, 0:H, :], bank(4 + i, P, H, HD + 1)[:, :, 0:HD], rep(den[:, i, :], 2, HD), MUL)
                last.then_inc(sem("mlstm_taken"), 1)

            def level_mask(l, i):
                dve.wait_ge(sem("level_out"), l * len(LEVELS) + (i + 1))
                for g in range(2):
                    bk = 2 * (i % 2) + g
                    heads = slice(2 * g, 2 * g + 2)
                    if i == 0:
                        last = dve.tensor_copy(ATD[:, heads, 2, :], bank(bk, P, 2, P))
                    else:
                        last = dve.tensor_tensor(ATD[:, heads, 0:2, :] if i == 1 else TMPD[:, heads], bank(bk, P, 2, 2, P),
                                                 rep(rep(Lmask[:, i - 1, :], 1, 2), 1, 2), MUL)
                last.then_inc(sem("level_taken"), 1)
                if i > 1:
                    dve.drain()
                    last = dve.tensor_tensor(ATD[:, :, 0:2, :], ATD[:, :, 0:2, :], TMPD, ADD)
                dve.drain()
                return last

            def hgrn(l):
                dve.tensor_scalar(FD, FD, X_MIN, None, MAX).then_inc(sem("forget_bounded"), 1)
                dve.wait_ge(sem("dgates_exp"), l + 1)
                dve.tensor_scalar(KD, E1, 1.0, None, ADD)
                dve.tensor_scalar(D1, D1, 1.0, None, ADD)
                dve.drain()
                dve.reciprocal(KD, KD)
                dve.reciprocal(D1, D1)
                for h in range(H):
                    dve.tensor_scalar(FD[:, h, :], E1[:, h, :], lb[:, h:h + 1], 1.0, MUL, ADD)
                dve.drain()
                dve.tensor_tensor(FD, FD, KD, MUL)
                dve.scalar_tensor_tensor(cut(actf, 0, H * NT), cut(actf, 0, H * NT), D_SCALE,
                                         cut(actf, 4 * H * NT, H * NT), MUL, MUL).then_inc(sem("forget_ready"), 1)
                dve.drain()
                dve.tensor_tensor(KD, KD, E1, MUL)
                dve.drain()
                for h in range(H):
                    dve.tensor_scalar(KD[:, h, :], KD[:, h, :], lb[:, H + h:H + h + 1], None, MUL)
                dve.wait_ge(sem("forget_log"), l + 1)
                for h in range(H):
                    dve.tensor_tensor_scan(FD[:, h, 0:SEQ], ones[:, :], D1[:, h, 0:SEQ], 0.0, MUL, ADD)
                dve.drain()
                for i, half in enumerate(LEVELS):
                    n = SEQ // (2 * half)
                    mid = max(half - 1, 0)
                    for h in range(H):
                        fv, dv = (v.rearrange("p (n s) -> p n s", n=n) for v in (FD[:, h, 0:SEQ], D1v[:, h, :]))
                        last = dve.tensor_tensor(dv, fv, rep(fv[:, :, mid], 2, 2 * half), SUB)
                    last.then_inc(sem("level_diff"), 1)
                    if i:
                        level_mask(l, i - 1)
                    dve.wait_ge(sem("level_exp"), l * len(LEVELS) + (i + 1))
                    dve.tensor_tensor(QP, QD[:, :, 0:SEQ], E1v, MUL)
                    dve.tensor_tensor(KP, KD[:, :, 0:SEQ], E1v if half > 1 else E2, MUL).then_inc(sem("level_ready"), 1)
                level_mask(l, len(LEVELS) - 1)
                dve.tensor_copy(lbt[:, 0, :], lb[:, 0:H]).then_inc(sem("levels_done"), 1)
                dve.wait_ge(sem("end_exp"), l + 1)
                dve.tensor_tensor(KP, KD[:, :, 0:SEQ], E1v, MUL).then_inc(sem("end_ready"), 1)
                dve.wait_ge(sem("hgrn_out"), l + 1)
                for i in range(2):
                    dve.tensor_copy(HCD[:, i, H:, :], bank(4 + i, P, H, HD))
                dve.wait_ge(sem("hgrn_state_out"), l + 1)
                dve.tensor_copy(DGS, bank(3, P, H, HD)).then_inc(sem("hgrn_state"), 1)
                dve.drain()
                dve.tensor_tensor(sqo, HCD, HCD, MUL)
                dve.drain()
                dve.tensor_reduce(st[:, 0:16].rearrange("p (b h) -> p b h", b=2), sqo, AX.X, ADD).then_inc(sem("squares3"), 1)
                dve.wait_ge(sem("roots3"), l + 1)
                dve.tensor_tensor(HCD, HCD, rep(rs[:, 0:16].rearrange("p (b h) -> p b h", b=2), 3, HD), MUL)
                dve.drain()
                dve.tensor_tensor(HCD, HCD, TM[:, 0:2, GATE:].rearrange("p b (g d) -> p b g d", d=HD), MUL)\
                    .then_inc(sem("mixed_ready"), 1)

            def context(l, b):
                dve.wait_ge(sem("ctx_out"), l * DEC + (b + 1))
                t0, t1 = (cut(dtmp[:, i, :], 0, H) for i in range(2))
                new = PA[:, PAGES * H:]
                dve.tensor_tensor(t0, ps[3][:, 132:136], new, ADD)
                dve.tensor_scalar(t1, new, latn[:, SEQ + b:SEQ + b + 1], None, MUL)
                dve.drain()
                dve.reciprocal(t0, t0)
                dve.tensor_tensor(t1, t1, ps[3][:, 128:132], ADD)
                dve.drain()
                dve.tensor_tensor(ctxT[:, :, SEQ + b], t1, t0, MUL).then_inc(sem("ctx_done"), 1)

            def latent_samples(l):
                for b in range(DEC):
                    for g in range(PAGES):
                        n = (l * DEC + b) * PAGES + g
                        dve.wait_ge(sem("page_squared"), n + 1)
                        dve.tensor_reduce(ssq[:, g * H:g * H + H], SQ[:, g % 4, :].rearrange("p (h d) -> p h d", h=H), AX.X, ADD)
                        c = GW + b * H
                        dve.tensor_copy(num[:, g * H:g * H + H], ps[4 + g % 4][:, c:c + H]).then_inc(sem("page_taken"), 1)
                    if b:
                        context(l, b - 1)
                    dve.wait_ge(sem("page_roots"), l * DEC + (b + 1))
                    K = PAGES * H
                    dve.tensor_tensor(SA[:, 0:K], num[:, 0:K], rsk[:, 0:K], MUL)
                    dve.drain()
                    dve.wait_ge(sem("kr_scores"), l * DEC + (b + 1))
                    dve.tensor_tensor(SA[:, 0:K], SA[:, 0:K], ps[3][:, 0:K], ADD).then_inc(sem("kr_taken"), 1)
                    dve.drain()
                    dve.tensor_reduce(lmx[:, 0, :], SA[:, 0:K].rearrange("p (g h) -> p h g", h=H), AX.X, MAX)\
                        .then_inc(sem("latent_max"), 1)
                    dve.wait_ge(sem("latent_max_all"), l * DEC + (b + 1))
                    new = nsA[:, b * H:b * H + H]
                    dve.tensor_tensor(lmx[:, 2, :], lmx[:, 1, :], new, MAX)
                    dve.drain()
                    dve.tensor_tensor(SA[:, K:], new, lmx[:, 2, :], SUB)
                    sv = SA[:, 0:K].rearrange("p (g h) -> p g h", h=H)
                    dve.tensor_tensor(sv, sv, rep(lmx[:, 2, :], 1, PAGES), SUB).then_inc(sem("latent_shifted"), 1)
                    dve.wait_ge(sem("latent_exp"), l * DEC + (b + 1))
                    dve.tensor_reduce(lsum[:, :], PA[:, 0:K].rearrange("p (g h) -> p h g", h=H), AX.X, ADD)\
                        .then_inc(sem("latent_summed"), 1)
                context(l, DEC - 1)

            def spread(l):
                s = slice(0, DEC)
                dve.tensor_tensor(qm[s], rep(TM[s, 2, BQ:BQ + GW], 1, DEC), rep(ident[s, 0:DEC], 2, GW), MUL)
                dve.tensor_tensor(prod[s, 0, :], TM[s, 2, BQ:BQ + GW], TM[s, 2, BK:BK + GW], MUL)
                dve.drain()
                dve.tensor_reduce(nst1[:, 1, :], prod[s, 0, :].rearrange("p (h d) -> p h d", h=H), AX.X, ADD)
                dve.drain()
                dve.tensor_tensor(nsm[:, 1], rep(nst1[:, 1, :], 1, DEC), rep(ident[s, 0:DEC], 2, H), MUL)\
                    .then_inc(sem("q_masked"), 1)

            def states(l):
                dve.wait_ge(sem("state_loaded"), (l + 1) * 16 * 20)
                for j in range(4):
                    r = slice(32 * j, 32 * j + 32)
                    dve.tensor_copy(jq[r, 0:32].rearrange("p (g k) -> p g k", g=2),
                                    SI[r, 0:2 * HD].rearrange("p (g k) -> p g k", g=2)[:, :, 16 * j:16 * j + 16])
                    dve.tensor_copy(jq[r, 32:128].rearrange("p (g k) -> p g k", g=3),
                                    SI[r, X_QD:X_I].rearrange("p (g k) -> p g k", g=3)[:, :, 32 * j:32 * j + 32])
                dve.tensor_tensor(sst[:, 2:3], sst[:, 0:1], SI[:, X_LF:X_LF + 1], ADD)
                dve.drain()
                dve.tensor_tensor(sst[:, 3:4], sst[:, 2:3], SI[:, X_I:X_I + 1], MAX)
                dve.drain()
                dve.tensor_tensor(sst[:, 4:5], sst[:, 2:3], sst[:, 3:4], SUB)
                dve.tensor_tensor(sst[:, 5:6], SI[:, X_I:X_I + 1], sst[:, 3:4], SUB)
                dve.tensor_scalar(sst[:, 6:7], sst[:, 3:4], -1.0, None, MUL).then_inc(sem("state_m"), 1)
                qd, fd, kd = (jq[:, 32 + 32 * g:64 + 32 * g] for g in range(3))
                dve.tensor_tensor(OUTER, rep(kd, 2, HD), rep(SI[:, X_DI:X_DI + HD], 1, 32), MUL)
                dve.tensor_tensor(STD, STD, rep(fd, 2, HD), MUL)
                dve.drain()
                dve.tensor_tensor(STD, STD, OUTER, ADD)
                dve.drain()
                dve.tensor_tensor(OUTER, STD, rep(qd, 2, HD), MUL)
                dve.drain()
                dve.tensor_reduce(red[:, HD + 1:], OUTER.rearrange("p k v -> p v k"), AX.X, ADD)
                dve.wait_ge(sem("state_exp"), l + 1)
                q, k = jq[:, 0:16], jq[:, 16:32]
                dve.tensor_scalar(k, k, sst[:, 8:9], M_SCALE, MUL, MUL)
                dve.drain()
                O16 = OUTER[:, 0:16, :]
                dve.tensor_tensor(O16, rep(k, 2, HD), rep(SI[:, X_MV:X_MV + HD], 1, 16), MUL)
                dve.drain()
                dve.scalar_tensor_tensor(cut(actf, 0, 1024), cut(actf, 0, 1024), sst[:, 7:8], cut(actf, 3072, 1024), MUL, ADD)
                dve.scalar_tensor_tensor(nst[:, :], nst[:, :], sst[:, 7:8], k, MUL, ADD)
                dve.drain()
                dve.tensor_tensor(O16, STC, rep(q, 2, HD), MUL)
                dve.tensor_tensor(k, nst[:, :], q, MUL)
                dve.drain()
                dve.tensor_reduce(red[:, 0:HD], O16.rearrange("p k v -> p v k"), AX.X, ADD)
                dve.tensor_reduce(red[:, HD:HD + 1], k, AX.X, ADD).then_inc(sem("states_updated"), 1)
                dve.wait_ge(sem("red_out"), l + 1)
                r = slice(0, 32)
                dve.tensor_copy(sst[r, 4:5], ps[5][r, HD:HD + 1])
                dve.tensor_copy(HS[:, 1, :], ps[5][r, HD + 1:2 * HD + 1])
                dve.drain()
                dve.scalar_tensor_tensor(sst[r, 4:5], sst[r, 4:5], -1.0, sst[r, 4:5], MUL, MAX)
                dve.drain()
                dve.tensor_tensor(sst[r, 4:5], sst[r, 4:5], sst[r, 9:10], MAX)
                dve.drain()
                dve.reciprocal(sst[r, 4:5], sst[r, 4:5])
                dve.drain()
                dve.tensor_scalar(HS[:, 0, :], ps[5][r, 0:HD], sst[r, 4:5], None, MUL)
                dve.drain()
                dve.tensor_tensor(red[r, 0:2 * HD].rearrange("p (g d) -> p g d", g=2), HS[:, :, :], HS[:, :, :], MUL)
                dve.drain()
                dve.tensor_reduce(st[r, 0:2], red[r, 0:2 * HD].rearrange("p (g d) -> p g d", g=2), AX.X, ADD)\
                    .then_inc(sem("squares4"), 1)
                dve.wait_ge(sem("roots4"), l + 1)
                dve.tensor_tensor(HS[:, :, :], HS[:, :, :], rep(rs[r, 0:2], 2, HD), MUL)
                dve.drain()
                dve.tensor_tensor(HS[:, :, :], HS[:, :, :], SI[r, X_CO:X_QD].rearrange("p (g d) -> p g d", g=2), MUL)\
                    .then_inc(sem("heads_ready"), 1)

            def windows(l):
                dve.wait_ge(sem("q_spread_copied"), l + 1)
                settled(dve)
                for b in range(DEC):
                    slot = b % K_SLOTS
                    dve.drain()
                    dve.wait_ge(k_loaded[slot], (l * (DEC // K_SLOTS) + (b // K_SLOTS + 1)) * 16 * NPAT)
                    dve.tensor_tensor(prod, KB[:, slot], rep(Qbc[:, b, :], 1, NPAT), MUL).then_inc(sem("window_products"), 1)
                    dve.drain()
                    dve.tensor_reduce(SB[:, b], prod.rearrange("p i (h d) -> p i h d", h=H), AX.X, ADD)
                dve.drain()
                dve.wait_ge(sem("vnew_copied"), l + 1)

                def w(i):
                    return wmx[:, i, :].rearrange("p (b h) -> p b h", h=H)

                over_keys = SB[:, :, :, :].rearrange("p b i h -> p b h i")
                dve.tensor_reduce(w(0), over_keys, AX.X, MAX).then_inc(sem("window_max"), 1)
                dve.wait_ge(sem("window_max_all"), l + 1)
                dve.tensor_tensor(wmx[:, 2, :], wmx[:, 2, :], wmx[:, 1, :], MAX)
                dve.drain()
                dve.tensor_tensor(SB[:, :, :, :], SB[:, :, :, :], rep(w(2), 2, NPAT), SUB)
                dve.tensor_tensor(wmx[:, 3, :], wmx[:, 1, :], wmx[:, 2, :], SUB).then_inc(sem("window_shifted_max"), 1)
                dve.wait_ge(sem("window_exp"), l + 1)
                dve.tensor_scalar(wmx[:, 3, :], wmx[:, 3, :], float(NPAT), None, MUL)
                dve.tensor_reduce(w(4), over_keys, AX.X, ADD).then_inc(sem("window_summed"), 1)
                dve.wait_ge(sem("window_sum_out"), l + 1)
                dve.tensor_tensor(wmx[:, 5, :], ps[6][:, 0:DEC * H], wmx[:, 3, :], ADD)
                dve.drain()
                dve.reciprocal(wmx[:, 5, :], wmx[:, 5, :])
                dve.drain()
                dve.tensor_tensor(wmx[:, 3, :], wmx[:, 3, :], wmx[:, 5, :], MUL)
                dve.tensor_tensor(SB[:, :, :, :], SB[:, :, :, :], rep(w(5), 2, NPAT), MUL).then_inc(sem("window_probs"), 1)
                dve.drain()
                for h in range(H):
                    r = slice(HD * (h % 2), HD * (h % 2) + HD)
                    dve.tensor_tensor(bsum[r, :, 0, h], vT[r, h // 2, :], w(3)[r, :, h], MUL)
                dve.drain()
                dve.wait_ge(sem("window_out"), l + 1)
                for h in range(H):
                    r = slice(HD * (h % 2), HD * (h % 2) + HD)
                    last = dve.tensor_tensor(o_T[r, 2 + h // 2, SEQ:NT], bsum[r, :, 0, h],
                                             bank(7, P, DEC, 2, H)[r, :, h // 2, h], ADD)
                last.then_inc(sem("mixer_done"), 1)

            with dve.Fori(0, DEPTH) as l:
                dve.tensor_copy(gcol[:, :], gcols[:, bass.ds(l, 1), :].rearrange("p a n -> p (a n)"))
                dve.tensor_copy(lb[:, :], lbs[:, bass.ds(l, 1), :].rearrange("p a n -> p (a n)"))
                dve.tensor_copy(cb[:, :], cbias[:, bass.ds(l, 1), :].rearrange("p a n -> p (a n)"))
                dve.drain()
                norm(l, 0)
                ffn(l, 0)
                stream(l, 0, 0.5)
                norm(l, 1)
                latent_rows(l)
                latent_qk(l)
                output_gates(l)
                softmax(l, 0, A_SCALE, K_AADD, None)
                softmax(l, 1, B_SCALE, K_BADD, K_BMUL)
                mlstm(l)
                hgrn(l)
                latent_samples(l)
                spread(l)
                states(l)
                windows(l)
                stream(l, 1, 1.0)
                norm(l, 2)
                dve.wait_ge(sem("sample_states_stored"), (l + 1) * 16 * N_SSTATE)
                settled(dve)
                ffn(l, 1)
                stream(l, 2, 0.5)

        @block.tensor
        def _(pe):
            def turn(out, src, rows):
                return pe.transpose(out, src, ident[0:rows, 0:rows])

            pe.wait_ge(sem("constants_loaded"), 4 * 16)
            pe.wait_ge(sem("x_loaded"), 3 * 16)
            for c in range(KC):
                for b in range(BLK):
                    last = turn(bank(c, P, NT)[:, b * P:b * P + ROWS[b]], xin[0:ROWS[b], b, c * P:(c + 1) * P], ROWS[b])
                last.then_inc(sem("x_turned"), 1)
            pe.wait_ge(sem("ones_set"), 4)

            def norm(l, k):
                pe.wait_ge(sem("squares_ready"), l * 3 + (k + 1))
                pe.matmul(bank(6, P, NT), ones[:, 0:P], ssum[:, :], start=True, stop=True).then_inc(sem("mean_square"), 1)

            def ffn(l, f, n0):
                pe.wait_ge(sem("h_ready"), l * (3 * KC) + (2 * f + 1) * KC)
                settled(pe)

                def gate_up(j, n, more):
                    slab_arrived(pe, l, n, more)
                    w = ring[:, n % RING, :].rearrange("p (g c n) -> p g c n", g=2, c=KC)
                    for q in range(2):
                        pe.wait_ge(sem("ffn_tiles"), l * (2 * FT) + j * 2 + (f * FT + q + 1))
                        for g in range(2):
                            for c in range(KC):
                                last = pe.matmul(bank(2 * q + g, P, NT), w[:, g, c, q * P:(q + 1) * P], h_T[:, c, :],
                                                 start=(c == 0), stop=(c == KC - 1))
                        last.then_inc(sem("gate_up_out"), 1)

                with pe.Fori(0, NG // RING) as i:
                    for r in range(RING):
                        gate_up(i * RING + r, n0 + r, i)
                for j in range(NG // RING * RING, NG):
                    gate_up(j, n0 + j, 0)
                for m in range(ND):
                    n = n0 + NG + m
                    slab_arrived(pe, l, n)
                    pe.wait_ge(sem("stream_added"), l * (3 * KC) + (2 * f * KC + m + 1))
                    w = ring[:, n % RING, 0:FT * P].rearrange("p (c n) -> p c n", c=FT)
                    for c in range(FT):
                        if m == 0:
                            pe.wait_ge(sem("ffn_tiles"), l * (2 * FT) + (f * FT + c + 1 + CREDIT))
                        last = pe.matmul(bank(4 + m % 2, P, NT), w[:, c, :], act_T[:, c, :], start=(c == 0), stop=(c == FT - 1))
                    last.then_inc(sem("stream_out"), 1)

            def project(l, first, last_slab):
                for n in range(first, last_slab):
                    slab_arrived(pe, l, FFN_SLABS + n)
                    w = SLABS[n][1]
                    W = ring[:, (FFN_SLABS + n) % RING, 0:KC * w].rearrange("p (c n) -> p c n", c=KC)
                    for k in range(NTK):
                        if TICKETS[k][0] != n:
                            continue
                        kind, i = TICKETS[k][1:]
                        if k >= 4:
                            pe.wait_ge(sem("w_in_copied"), l * NTK + (k - 3))
                        for c in range(KC):
                            if kind == "rows":
                                cols = GW if n == 4 else w
                                last = pe.matmul(bank(k % 4, ROWS[i], cols), h_T[:, c, i * P:i * P + ROWS[i]], W[:, c, 0:cols],
                                                 start=(c == 0), stop=(c == KC - 1))
                            elif kind == "gate":
                                last = pe.matmul(bank(k % 4, H, NT), W[:, c, GW + i * H:GW + i * H + H], h_T[:, c, :],
                                                 start=(c == 0), stop=(c == KC - 1))
                            else:
                                last = pe.matmul(bank(k % 4, P, NT), W[:, c, i * P:(i + 1) * P], h_T[:, c, :],
                                                 start=(c == 0), stop=(c == KC - 1))
                        last.then_inc(sem("w_in_out"), 1)

            def latent_up(l):
                pe.wait_ge(sem("rows_final"), l + 1)
                for b in range(BLK):
                    for i, c in enumerate((CQ, CQ + P, CKV)):
                        last = turn(bank(4 + i, P, NT)[:, b * P:b * P + ROWS[b]], TM[0:ROWS[b], b, c:c + P], ROWS[b])
                last.then_inc(sem("down_turned"), 1)

            def up(l):
                pe.wait_ge(sem("down_copied"), l + 1)
                for b, bk in enumerate((4, 5, 7)):
                    for c in range(2):
                        pe.matmul(bank(bk, ROWS[b], H * QKW), cqT[:, c, b * P:b * P + ROWS[b]], wuq[:, c, :],
                                  start=(c == 0), stop=(c == 1))
                for b in range(2):
                    last = pe.matmul(cut(ps[6], b * GW, H, NOPE), latn[:, b * P:(b + 1) * P], wukv[:, :, 0:NOPE],
                                     start=True, stop=True)
                last.then_inc(sem("up_out"), 1)
                pe.wait_ge(sem("up_copied"), l * 2 + 1)
                pe.matmul(bank(4, DEC, H, NOPE), latn[:, SEQ:NT], wukv[:, :, 0:NOPE], start=True, stop=True)\
                    .then_inc(sem("up_out"), 1)

            def turn_qk(l):
                pe.wait_ge(sem("qk_final"), l + 1)
                for i, src in enumerate((Qk, Kk)):
                    for h in range(H):
                        for b in range(2):
                            last = turn(bank(4 + 2 * i + h // 2, QKW, 2, SEQ)[:, h % 2, b * P:(b + 1) * P], src[:, b, h, :], P)
                last.then_inc(sem("qk_turned"), 1)
                pe.wait_ge(sem("qk_copied"), l * 2 + 1)
                settled(pe)
                for h in range(H):
                    turn(bank(4, HD, H, DEC)[:, h, :], qtl[0:DEC, h, :], DEC)
                    turn(cut(ps[4], H * DEC, H, DEC)[:, h, :], q4[0:DEC, h].rearrange("p j r -> p (j r)"), DEC)
                    turn(bank(5, HD, H, P)[:, h, :], wukv[:, h, 0:NOPE], P)
                pe.matmul(bank(6, P, DEC, H), ones[0:DEC, 0:P], nsm[:, 0], start=True, stop=True).then_inc(sem("qk_turned"), 1)
                pe.wait_ge(sem("qk_copied"), l * 2 + 2)
                for h in range(H):
                    last = pe.matmul(bank(7, P, H, DEC)[:, h, :], wukT[0:HD, h, :], qtT[0:HD, h, :], start=True, stop=True)
                last.then_inc(sem("u_out"), 1)

            def turn_pairs(l):
                pe.wait_ge(sem("u_copied"), l + 1)
                for i, c in enumerate((BQ, BK, MQ, MK)):
                    for g in range(2):
                        for b in range(2):
                            last = turn(bank(4 + i, P, 2, SEQ)[:, g, b * P:(b + 1) * P], TM[:, b, c + g * P:c + (g + 1) * P], P)
                last.then_inc(sem("pairs_turned"), 1)

            def attend(l, a):
                if a == 0:
                    pe.wait_ge(sem("pairs_copied"), l + 1)
                else:
                    pe.wait_ge(sem("prompt_copied"), l * 2 + 1)
                for h in range(H):
                    if a == 0:
                        q, k = QT[0:QKW, h], KT[0:QKW, h]
                    else:
                        r = slice(HD * (h % 2), HD * (h % 2) + HD)
                        q, k = pairT[r, 0, h // 2], pairT[r, 1, h // 2]
                    pe.matmul(bank(4 + h, P, P), q[:, 0:P], k[:, 0:P], start=True, stop=True)
                    pe.matmul(ps[4 + h][:, P:3 * P], q[:, P:SEQ], k, start=True, stop=True).then_inc(sem("scores_out"), 1)
                pe.wait_ge(sem("scores_taken"), (l * 2 + a + 1) * H)
                pe.wait_ge(sem("probs_ready"), l * 2 + (a + 1))
                for h in range(H):
                    for c in range(3):
                        last = turn(bank(4 + h, P, 3, P)[:, c, :], S[:, h, c * P:(c + 1) * P], P)
                    last.then_inc(sem("probs_turned"), 1)
                for h in range(H):
                    pe.wait_ge(sem("probs_copied"), (l * 2 + a) * H + (h + 1 if h > 1 else 2))
                    for c in range(2):
                        w = TM[:, c, CKV:CKR] if a == 0 else TM[:, c, BV + h * HD:BV + (h + 1) * HD]
                        if a == 0:
                            out = bank(4 + h // 2, P, 2, SEQ)[:, h % 2, c * P:]
                        else:
                            out = bank(4 + h // 2, P, SEQ)[HD * (h % 2):HD * (h % 2) + HD, c * P:]
                        last = pe.matmul(out, w, PT[:, h, 0:SEQ] if c == 0 else PT[:, h, SEQ:], start=(c == 0), stop=(c == 1))
                last.then_inc(sem("prompt_out"), 1)

            def mlstm(l):
                pe.wait_ge(sem("prompt_copied"), l * 2 + 2)
                pe.wait_ge(sem("mgates_ready"), l + 1)
                settled(pe)
                g = bank(6, P, 6, H)
                for b in range(2):
                    turn(g[:, b, :], CG[0:H, 4, b * P:(b + 1) * P], H)
                    turn(g[:, 2 + b, :], CG[0:H, 7, b * P:(b + 1) * P], H)
                    turn(g[0:DEC, 4 + b, :], CG[0:H, b, SEQ:NT], H)
                for h in range(H):
                    last = pe.matmul(bank(4 + h // 2, P, 2, SEQ)[:, h % 2, :], selh[0:H, h, :], CG[0:H, 5, 0:SEQ], start=True, stop=True)
                last.then_inc(sem("mgates_out"), 1)
                for h in range(H):
                    r = slice(HD * (h % 2), HD * (h % 2) + HD)
                    q, k = pairT[r, 2, h // 2], pairT[r, 3, h // 2]
                    pe.matmul(bank(h, P, SEQ), k[:, 0:P], q, start=True, stop=True)
                    pe.matmul(ps[h][:, SEQ:3 * P], k[:, P:], q[:, P:], start=True, stop=True).then_inc(sem("mscores_out"), 1)
                pe.wait_ge(sem("mkeys_ready"), l + 1)
                pe.wait_ge(sem("mprobs_ready"), (l + 1) * H)
                for h in range(H):
                    pe.matmul(bank(4, P, H, HD + 1)[:, h, :], S[:, h, 0:P], vaug[:, 0, h, :], start=True, stop=True)
                for h in range(H):
                    for b in range(2):
                        pe.matmul(bank(5, P, H, HD + 1)[:, h, :], S[:, h, (b + 1) * P:(b + 2) * P], vaug[:, b, h, :],
                                  start=(b == 0), stop=(b == 1))
                for h in range(H):
                    for b in range(2):
                        last = pe.matmul(bank(6, HD, H, HD + 1)[:, h, :], kw[:, b, h, :], vaug[:, b, h, :],
                                         start=(b == 0), stop=(b == 1))
                last.then_inc(sem("mlstm_out"), 1)

            def hgrn(l):
                for i, half in enumerate(LEVELS):
                    pe.wait_ge(sem("level_ready"), l * len(LEVELS) + (i + 1))
                    if i >= 2:
                        pe.wait_ge(sem("level_taken"), l * len(LEVELS) + (i - 1))
                    for h in range(H):
                        bk = 2 * (i % 2) + h // 2
                        if i == 0:
                            last = pe.matmul(bank(bk, P, 2, P)[:, h % 2, :], KP[:, h, 0:P], QP[:, h, P:], start=True, stop=True)
                        else:
                            for b in range(2):
                                last = pe.matmul(bank(bk, P, 2, 2, P)[:, h % 2, b, :], KP[:, h, b * P:(b + 1) * P],
                                                 QP[:, h, b * P:(b + 1) * P], start=True, stop=True)
                    last.then_inc(sem("level_out"), 1)
                pe.wait_ge(sem("mlstm_taken"), l + 1)
                pe.wait_ge(sem("levels_done"), l + 1)

                def v(b, h):
                    return TM[:, b, DI + h * HD:DI + (h + 1) * HD]

                for h in range(H):
                    pe.matmul(bank(4, P, H, HD)[:, h, :], ATD[:, h, 0, :], v(0, h), start=True, stop=True)
                for h in range(H):
                    pe.matmul(bank(5, P, H, HD)[:, h, :], ATD[:, h, 2, :], v(0, h), start=True, stop=False)
                    last = pe.matmul(bank(5, P, H, HD)[:, h, :], ATD[:, h, 1, :], v(1, h), start=False, stop=True)
                last.then_inc(sem("hgrn_out"), 1)
                pe.wait_ge(sem("end_ready"), l + 1)
                for b in range(2):
                    for h in range(H):
                        turn(bank(6 + b, P, H, DK)[:, h, :], KP[:, h, b * P:(b + 1) * P], P)
                for i, src in enumerate((QD, FD, KD)):
                    for h in range(H):
                        last = turn(bank(i, DEC, H, DK)[:, h, :], src[:, h, SEQ:NT], P)
                last.then_inc(sem("end_turned"), 1)
                pe.wait_ge(sem("end_copied"), l + 1)
                for h in range(H):
                    for b in range(2):
                        last = pe.matmul(bank(3, P, H, HD)[:, h, :], KE[:, b, h, :], v(b, h), start=(b == 0), stop=(b == 1))
                last.then_inc(sem("hgrn_state_out"), 1)
                pe.wait_ge(sem("mixed_ready"), l + 1)
                for i in range(4):
                    for b in range(2):
                        last = turn(bank(4 + i, P, SEQ)[:, b * P:(b + 1) * P],
                                    HCD[:, b, 2 * i:2 * i + 2, :].rearrange("p h d -> p (h d)"), P)
                    last.then_inc(sem("mixed_out"), 1)

            def values(l, b):
                pe.wait_ge(sem("latent_summed"), l * DEC + (b + 1))
                if b:
                    pe.wait_ge(sem("ctx_done"), l * DEC + b)
                for g in range(PAGES):
                    pe.matmul(ps[3][:, 128:132], lat[:, b % LAT_SLOTS, g, :], PA[:, g * H:(g + 1) * H],
                              start=(g == 0), stop=(g == PAGES - 1))
                pe.matmul(ps[3][:, 132:136], ones[:, 0:P], lsum[:, :], start=True, stop=True).then_inc(sem("ctx_out"), 1)

            def latent_samples(l):
                pe.wait_ge(sem("mixed_turned"), (l + 1) * 4)
                for b in range(DEC):
                    slot = b % LAT_SLOTS
                    pe.wait_ge(lat_loaded[slot], (l * lat_uses[slot] + (b // LAT_SLOTS + 1)) * (2 * PAGES * 16))
                    for c in range(4):
                        last = turn(bank(2, P, 4, P)[:, c, :], kr[:, slot, c * P:(c + 1) * P], P)
                    last.then_inc(sem("kr_turned"), 1)
                    for c in range(4):
                        if b:
                            pe.wait_ge(sem("lat_copied"), (l * DEC + b) * 4 + (c - 1))
                        elif c >= 2:
                            pe.wait_ge(sem("lat_copied"), l * (DEC * 4) + (c - 1))
                        for g in range(4):
                            last = turn(bank(c % 2, P, 4, P)[:, g, :], lat[:, slot, 4 * c + g, :], P)
                        last.then_inc(sem("lat_turned"), 1)
                        if c == 0:
                            pe.wait_ge(sem("kr_copied"), l * DEC + (b + 1))
                            if b:
                                pe.wait_ge(sem("kr_taken"), l * DEC + b)
                            for j in range(4):
                                last = pe.matmul(cut(ps[3], 16 * j, 4, H), krT[:, j * P:(j + 1) * P], qrb[:, b], start=True, stop=True)
                            last.then_inc(sem("kr_scores"), 1)
                        pe.wait_ge(sem("lat_copied"), (l * DEC + b) * 4 + (c + 1))
                        for g in range(4 * c, 4 * c + 4):
                            n = (l * DEC + b) * PAGES + g
                            if b or g >= 4:
                                pe.wait_ge(sem("page_taken"), n - 3)
                            pe.matmul(bank(4 + g % 4, P, GW + DEC * H), latT[:, g, :], wuk[:, :], start=True, stop=True)\
                                .then_inc(sem("page_out"), 1)
                    if b:
                        values(l, b - 1)
                values(l, DEC - 1)
                pe.wait_ge(sem("ctx_done"), (l + 1) * DEC)
                for h in range(H):
                    last = pe.matmul(bank(4 + h // 2, P, NT)[HD * (h % 2):HD * (h % 2) + HD, :], wukv[:, h, NOPE:], ctxT[:, h, :],
                                     start=True, stop=True)
                last.then_inc(sem("oA_out"), 1)

            def samples(l):
                s = slice(0, DEC)
                pe.wait_ge(sem("q_masked"), l + 1)
                for i in range(4):
                    pe.matmul(bank(i, P, 2, GW), ones[s, 0:P], qm[s, 2 * i:2 * i + 2, :], start=True, stop=True)\
                        .then_inc(sem("q_spread"), 1)
                pe.matmul(bank(6, P, DEC, H), ones[s, 0:P], nsm[:, 1], start=True, stop=True)
                for g in range(2):
                    last = turn(bank(7, P, 2, DEC)[:, g, :], TM[s, 2, BV + g * P:BV + (g + 1) * P], DEC)
                last.then_inc(sem("vnew_turned"), 1)
                pe.wait_ge(sem("oA_copied"), l + 1)
                pe.wait_ge(sem("states_updated"), l + 1)
                pe.matmul(bank(5, 32, 2 * HD + 1), cst[:, K_SELJ:K_SELJ + 32], red[:, :], start=True, stop=True)\
                    .then_inc(sem("red_out"), 1)
                pe.wait_ge(sem("heads_ready"), l + 1)
                settled(pe)
                for g in range(2):
                    last = turn(bank(4 + g, HD, 32), HS[:, g, :], 32)
                last.then_inc(sem("states_turned"), 1)
                pe.wait_ge(sem("window_summed"), l + 1)
                pe.matmul(bank(6, P, DEC * H), ones[:, 0:P], wmx[:, 4, :], start=True, stop=True).then_inc(sem("window_sum_out"), 1)
                pe.wait_ge(sem("window_v_loaded"), (l + 1) * DEC * NPAT * 16)
                pe.wait_ge(sem("window_probs"), l + 1)
                for b in range(DEC):
                    for g in range(2):
                        for i in range(NPAT):
                            last = pe.matmul(bank(7, P, DEC, 2, H)[:, b, g, :], VB[:, b, i, g * P:(g + 1) * P], SB[:, b, i, :],
                                             start=(i == 0), stop=(i == NPAT - 1))
                last.then_inc(sem("window_out"), 1)

            def w_out(l):
                pe.wait_ge(sem("states_copied"), l + 1)
                pe.wait_ge(sem("mixer_done"), l + 1)
                for i, (m0, k) in enumerate(OUT_SLABS):
                    n = FFN_SLABS + len(SLABS) + i
                    slab_arrived(pe, l, n)
                    w = ring[:, n % RING, 0:KC * k * P].rearrange("p (c n) -> p c n", c=KC)
                    for m in range(m0, m0 + k):
                        pe.wait_ge(sem("stream_added"), l * (3 * KC) + (KC + m + 1))
                        for c in range(KC):
                            last = pe.matmul(bank(4 + m % 2, P, NT), w[:, c, (m - m0) * P:(m - m0 + 1) * P], o_T[:, c, :],
                                             start=(c == 0), stop=(c == KC - 1))
                        last.then_inc(sem("stream_out"), 1)

            with pe.Fori(0, DEPTH) as l:
                norm(l, 0)
                ffn(l, 0, 0)
                norm(l, 1)
                pe.wait_ge(sem("h_ready"), l * (3 * KC) + 2 * KC)
                project(l, 0, 3)
                latent_up(l)
                project(l, 3, 4)
                pe.wait_ge(sem("small_loaded"), (l + 1) * 3 * 16)
                up(l)
                project(l, 4, 6)
                turn_qk(l)
                project(l, 6, 8)
                turn_pairs(l)
                project(l, 8, len(SLABS))
                attend(l, 0)
                attend(l, 1)
                mlstm(l)
                hgrn(l)
                latent_samples(l)
                samples(l)
                w_out(l)
                norm(l, 2)
                ffn(l, 1, FFN_SLABS + MIX_SLABS)
            pe.wait_ge(sem("squares_ready"), 3 * DEPTH + 1)
            for b in range(BLK):
                for g in range(2):
                    for c in range(4):
                        last = turn(bank(2 * b + g, ROWS[b], 4, P)[:, c, :], x_T[:, 4 * g + c, b * P:b * P + ROWS[b]], P)
                    last.then_inc(sem("y_out"), 1)


def program(nc, tensors):
    build(nc, tensors)


def constants():
    import numpy as np
    out = np.zeros((P, K_N), np.float32)
    out[:, K_ID:K_ID + P] = np.eye(P)
    t = np.arange(SEQ)
    d = t[:, None] - t[None, :]
    times = sum(((d >= 0) & (d <= w) & (d % s == 0)).astype(np.float32) for w, s in PATTERNS)
    tiles = [(0, 0), (1, 0), (1, 1)]

    def put(at, m):
        for i, (a, b) in enumerate(tiles):
            out[:, at + i * P:at + (i + 1) * P] = m[a * P:(a + 1) * P, b * P:(b + 1) * P]

    put(K_AADD, np.where(d >= 0, 0.0, -1e30))
    put(K_BADD, np.where(times > 0, 0.0, -1e30))
    put(K_BMUL, times)
    for i, (a, b) in enumerate([(0, 0), (1, 0), (1, 1)]):
        out[:, K_WM + i * P:K_WM + (i + 1) * P] = (d[a * P:(a + 1) * P, b * P:(b + 1) * P] >= 0).T * M_SCALE
    s, q = np.arange(P)[:, None], np.arange(P)[None, :]
    for i, half in enumerate(LEVELS[1:]):
        same = s // (2 * half) == q // (2 * half)
        pair = (s % (2 * half) < half) & (q % (2 * half) >= half) if half > 1 else s <= q
        out[:, K_LV + i * P:K_LV + (i + 1) * P] = same & pair
    for h in range(H):
        out[h, K_SELH + h * P:K_SELH + (h + 1) * P] = 1.0
    out[np.arange(P), K_SELJ + np.arange(P) % 32] = 1.0
    half = ROPE // 2
    inv = np.float32(10000.0) ** (-np.arange(half, dtype=np.float32) / np.float32(half))
    for b in range(BLK):
        pos = (b * P + np.arange(P) if b < 2 else np.full(P, PAST)).astype(np.float32)
        ang = pos[:, None] * inv[None, :]
        out[:, K_COS + b * half:K_COS + (b + 1) * half] = np.cos(ang)
        out[:, K_SIN + b * half:K_SIN + (b + 1) * half] = np.sin(ang)
    return out


def kernel(**x):
    import numpy as np
    import concourse.bacc as bacc
    from concourse.bass_utils import run_bass_kernel_spmd

    f32 = mybir.dt.float32
    a = {k: np.ascontiguousarray(np.asarray(v)) for k, v in x.items()}
    pool = a["cache_mla_latent"].shape[1]
    ins = {k: a[k] for k in ("x_prompt", "x_sample", "cache_mla_latent", "cache_mla_krope", "state_mlstm_C", "state_mlstm_n",
                             "state_mlstm_m", "state_hgrn_S", "w1_gate", "w1_up", "w1_down", "w2_gate", "w2_up", "w2_down",
                             "w_in", "a_wuq", "a_wukv", "w_out")}
    for k in ("cache_swa_k", "cache_swa_v"):
        ins[k] = a[k].reshape(DEPTH, DEC, PAST, GW)
    ins["page_table"] = a["page_table"].reshape(1, DEC * PAGES)
    ins["gains"] = np.concatenate([a[k] for k in ("a_gq", "a_gkv", "a_gkr", "b_gq", "b_gk", "a_gqn", "a_gqr", "a_gkn",
                                                  "c_gout", "d_gout")], axis=1)
    cols = np.stack([a[k] for k in ("g_ffn1", "g_mix", "g_ffn2")], axis=1)
    ins["g_col"] = np.ascontiguousarray(cols.reshape(DEPTH, 3 * KC, P).transpose(2, 0, 1))
    ins["lb_col"] = np.ascontiguousarray(a["d_lb_logits"].reshape(DEPTH, H, DK).transpose(2, 0, 1))
    ins["c_bias"] = np.ascontiguousarray(np.stack([a["c_bi"], a["c_bf"]], axis=2).transpose(1, 0, 2))
    ins["constants"] = constants()

    nc = bacc.Bacc("TRN2", target_bir_lowering=False, num_devices=1)
    t = {k: nc.dram_tensor("in_" + k, v.shape, mybir.dt.from_np(v.dtype), kind="ExternalInput").ap() for k, v in ins.items()}
    outs = {"y_prompt": (1, SEQ, D_MODEL), "y_sample": (DEC, 1, D_MODEL),
            "p_mla_latent": (DEPTH, SEQ, KVL), "p_mla_krope": (DEPTH, SEQ, ROPE), "p_swa_k": (DEPTH, SEQ, GW), "p_swa_v": (DEPTH, SEQ, GW),
            "p_mlstm_C": (DEPTH, H, HD, HD), "p_mlstm_n": (DEPTH, H, HD), "p_mlstm_m": (DEPTH, H), "p_hgrn_S": (DEPTH, H, DK, HD),
            "s_mla_latent": (DEPTH, DEC, KVL), "s_mla_krope": (DEPTH, DEC, ROPE), "s_swa_k": (DEPTH, DEC, PAST, GW),
            "s_swa_v": (DEPTH, DEC, PAST, GW), "s_mlstm_C": (DEPTH, DEC, H, HD, HD), "s_mlstm_n": (DEPTH, DEC, H, HD),
            "s_mlstm_m": (DEPTH, DEC, H), "s_hgrn_S": (DEPTH, DEC, H, DK, HD)}
    for k, shape in outs.items():
        t[k] = nc.dram_tensor("out_" + k, shape, f32, kind="ExternalOutput").ap()
    t["scratch"] = nc.dram_tensor("scratch", (DEPTH, DEC, H, X_N), f32, kind="Internal").ap()
    nc.disable_value_cache = True
    program(nc, t)
    got = run_bass_kernel_spmd(nc, [{"in_" + k: v for k, v in ins.items()}], core_ids=[0]).results[0]
    r = {k: got["out_" + k] for k in outs}
    heads = (H, HD)
    return (r["y_prompt"], r["y_sample"],
            r["p_mla_latent"].reshape(DEPTH, 1, SEQ, KVL), r["p_mla_krope"].reshape(DEPTH, 1, SEQ, ROPE),
            r["p_swa_k"].reshape(DEPTH, 1, SEQ, *heads), r["p_swa_v"].reshape(DEPTH, 1, SEQ, *heads),
            r["p_mlstm_C"].reshape(DEPTH, 1, H, HD, HD), r["p_mlstm_n"].reshape(DEPTH, 1, H, HD),
            r["p_mlstm_m"].reshape(DEPTH, 1, H), r["p_hgrn_S"].reshape(DEPTH, 1, H, DK, HD),
            r["s_mla_latent"].reshape(DEPTH, DEC, 1, KVL), r["s_mla_krope"].reshape(DEPTH, DEC, 1, ROPE),
            r["s_swa_k"].reshape(DEPTH, DEC, PAST, *heads), r["s_swa_v"].reshape(DEPTH, DEC, PAST, *heads),
            r["s_mlstm_C"], r["s_mlstm_n"], r["s_mlstm_m"], r["s_hgrn_S"])
```

```python
import concourse.bass as bass
from concourse import mybir
from contextlib import ExitStack

D_MODEL, SEQ, DEPTH, DEC, PAST, PAGE = 1024, 256, 2, 8, 2048, 128
H, HD, GW = 4, 64, 256
QL, KVL, NOPE, ROPE, DK = 256, 128, 64, 32, 128
D_FF, EPS = 2816, 1e-6
PATTERNS = ((128, 1), (512, 4), (2048, 16))
P = 128
NT = SEQ + DEC
KC = D_MODEL // P
FT = D_FF // P
BLK = 3
ROWS = (P, P, DEC)
QKW = NOPE + ROPE
PAGES = PAST // PAGE
NPAT = len(PATTERNS)

W_B, W_C, W_I, W_O = QL + KVL + ROPE, QL + KVL + ROPE + 3 * GW, QL + KVL + ROPE + 6 * GW, QL + KVL + ROPE + 6 * GW + 2 * H
W_DQ = W_O + GW
W_DF, W_DI, W_DG = W_DQ + H * DK, W_DQ + 2 * H * DK, W_DQ + 2 * H * DK + GW
N_IN = W_DG + GW
CQ, CKV, CKR, BQ, BK, BV = 0, QL, QL + KVL, W_B, W_B + GW, W_B + 2 * GW
MQ, MK, MV = W_C, W_C + GW, W_C + 2 * GW
DI, GATE = MV + GW, MV + 2 * GW
TMW = GATE + 2 * GW
SLABS = [(0, W_B, CQ), (BQ, 2 * GW, BQ), (BV, GW, BV), (MQ, 2 * GW, MQ), (MV, GW + 2 * H, MV),
         (W_O, GW, GATE), (W_DQ, H * DK, None), (W_DF, H * DK, None), (W_DI, GW, DI), (W_DG, GW, GATE + GW)]
OUT_SLABS = [(0, 3), (3, 3), (6, 2)]
NG = FT // 2
ND = KC
FFN_SLABS = NG + ND
MIX_SLABS = len(SLABS) + len(OUT_SLABS)
RING = 3
LAYER_SLABS = 2 * FFN_SLABS + MIX_SLABS
assert LAYER_SLABS % RING == 0
SLOT = 2 * KC * 2 * P

G_Q, G_KV, G_KR, G_BQ, G_BK = 0, QL, QL + KVL, QL + KVL + ROPE, QL + KVL + ROPE + HD
G_QN = G_BK + HD
G_QR, G_KN = G_QN + NOPE, G_QN + NOPE + ROPE
G_OUT = G_KN + NOPE
G_N = G_OUT + 2 * GW

LEVELS = [128, 64, 32, 16, 8, 4, 2, 1]
K_ID = 0
K_AADD = P
K_BADD = K_AADD + 3 * P
K_BMUL = K_BADD + 3 * P
K_WM = K_BMUL + 3 * P
K_LV = K_WM + 3 * P
K_SELH = K_LV + (len(LEVELS) - 1) * P
K_SELJ = K_SELH + H * P
K_COS = K_SELJ + 32
K_SIN = K_COS + BLK * ROPE // 2
K_N = K_SIN + BLK * ROPE // 2
X_MQ, X_MK, X_MV, X_DI, X_CO, X_DG, X_QD, X_F, X_K, X_I, X_LF = 0, 64, 128, 192, 256, 320, 384, 512, 640, 768, 769
X_N = 770
A_SCALE, B_SCALE, M_SCALE, D_SCALE = (NOPE + ROPE) ** -0.5, HD ** -0.5, HD ** -0.5, DK ** -0.5
X_MIN = -43.0
RING_LAT = 2 * RING - 1
K_SLOTS = 2
KR_RING = range(3, 7)
KR_POOL = (0, 1, 3, 4, DEC - 1)
N_STORE = 8
N_PSTATE = 4
N_SSTATE = 3 * 4 + 1
N_SCRATCH = 11
CREDIT = 2
OUT_CREDIT = 3
RMAX = bass.bass_isa.ReduceOp.max


def tickets():
    out = []
    for n, (_, _, col) in enumerate(SLABS):
        if col is None:
            out += [(n, "head", h) for h in range(H)]
        else:
            out += [(n, "rows", b) for b in range(BLK)]
        if n == 4:
            out += [(n, "gate", 0), (n, "gate", 1)]
    return out


TICKETS = tickets()
NTK = len(TICKETS)


def build(nc, t):
    f32 = mybir.dt.float32
    ACT, ALU, AX = mybir.ActivationFunctionType, mybir.AluOpType, mybir.AxisListType
    MUL, ADD, SUB, MAX, MIN = ALU.mult, ALU.add, ALU.subtract, ALU.max, ALU.min
    ctx = ExitStack()
    with ctx:
        def sb(name, shape, dt=f32):
            return ctx.enter_context(nc.sbuf_tensor(name, shape, dt))

        made = {}

        def sem(name):
            if name not in made:
                made[name] = ctx.enter_context(nc.semaphore(name))
            return made[name]

        x_T = sb("x_T", [P, KC, NT])
        h_T = sb("h_T", [P, KC, NT])
        act_T = sb("act_T", [P, FT, NT])
        ring = sb("ring", [P, RING, SLOT])
        TM = sb("TM", [P, BLK, TMW])
        o_T = sb("o_T", [P, KC, NT])
        cst = sb("cst", [P, K_N])
        ones = sb("ones", [P, SEQ])
        eps = sb("eps", [P, 1])
        gains = sb("gains", [P, G_N])
        gcols = sb("gcols", [P, DEPTH, 3 * KC])
        lbx = sb("lbx", [P, DEPTH, H])
        lbs = sb("lbs", [P, DEPTH, 2 * H])
        lbt = sb("lbt", [P, 2, H])
        cbias = sb("cbias", [H, DEPTH, 2])
        gcol = sb("gcol", [P, 3 * KC])
        lb = sb("lb", [P, 2 * H])
        cb = sb("cb", [H, 2])
        pages = sb("pages", [1, DEC * PAGES], mybir.dt.int32)
        wuq = sb("wuq", [P, QL // P, H * QKW])
        wukv = sb("wukv", [P, H, 2 * HD])
        ssum = sb("ssum", [P, NT])
        sqx = sb("sqx", [P, NT])
        rstd = sb("rstd", [P, NT])
        sg = sb("sg", [P, 2, NT])
        st = sb("st", [P, 3 * 12])
        rs = sb("rs", [P, 3 * 12])
        rp = sb("rp", [P, 4, BLK * H * ROPE // 2])
        ctxT = sb("ctxT", [P, H, NT])
        latn = sb("latn", [P, NT])
        wuk = sb("wuk", [P, GW + DEC * H])
        qrb = sb("qrb", [P, DEC, 4, H])
        nsA = sb("nsA", [P, DEC * H])
        nsm = sb("nsm", [DEC, 2, DEC, H])
        nst1 = sb("nst1", [DEC, 2, H])
        mxs = sb("mxs", [P, 2, H])
        gT = sb("gT", [P, 5, H])
        gTs = sb("gTs", [DEC, 2, H])
        wd = sb("wd", [P, 2, H])
        emt = sb("emt", [P, 2, H])
        den = sb("den", [P, 2, H])
        lmx = sb("lmx", [P, 3, H])
        wmx = sb("wmx", [P, 6, DEC * H])
        sst = sb("sst", [P, 10])
        decs = sb("decs", [P, 7, (PAGES + 1) * H])
        SB = sb("SB", [P, DEC, NPAT, H])
        jq = sb("jq", [P, 2 * 16 + 3 * 32])
        nst = sb("nst", [P, 16])
        red = sb("red", [P, 2 * HD + 1])
        HS = sb("HS", [32, 2, HD])
        vT = sb("vT", [P, 2, DEC])
        bsum = sb("bsum", [P, DEC, 2, H])
        U = sb("U", [P, 8968])

        def cut(buf, at, *shape):
            n = 1
            for d in shape:
                n *= d
            v = buf[:, at:at + n]
            if len(shape) == 1:
                return v
            names = "abcd"[:len(shape)]
            return v.rearrange("p (" + " ".join(names) + ") -> p " + " ".join(names), **dict(zip(names[1:], shape[1:])))

        actf = act_T[:, :, :].rearrange("p f t -> p (f t)")
        hf = h_T[:, :, :].rearrange("p f t -> p (f t)")
        xin = cut(actf, 0, BLK, D_MODEL)
        QT = cut(U, 0, H, SEQ)
        KT = cut(U, 1024, H, SEQ)
        pairT = cut(U, 2048, 4, 2, SEQ)
        S = cut(U, 4096, H, 3 * P)
        PT = cut(U, 5632, H, 3 * P)
        WT = cut(U, 7168, H, 3 * P)
        CGS = cut(U, 8704, H, HD + 1)
        sq1 = cut(U, 4096, BLK, BV)
        Qk = cut(U, 4096, BLK, H, QKW)
        Kk = cut(U, 5248, BLK, H, QKW)
        sq2 = cut(U, 0, BLK, H, QKW)
        sq3 = cut(U, 1152, BLK, H, NOPE)
        cqT = cut(U, 7168, QL // P, NT)
        wukT = cut(U, 7168, H, P)
        qtT = cut(U, 7696, H, DEC)
        qtl = cut(U, 7728, H, HD)
        q4 = cut(U, 7984, H, 4, ROPE)
        qk = cut(U, 7168, H, QKW)
        vaug = cut(U, 0, 2, H, HD + 1)
        kw = cut(U, 1024, 2, H, HD)
        ATD = cut(U, 0, H, 3, P)
        HCD = cut(U, 2048, 2, 2 * H, HD)
        QP = [cut(U, 3072, H, SEQ), cut(hf, 0, H, SEQ)]
        KP = [cut(U, 4096, H, SEQ), cut(U, 5120, H, SEQ)]
        KE = cut(U, 5120, 2, H, DK)
        TMPD = cut(U, 6144, H, 2, P)
        DGS = cut(U, 6144, H, HD)
        E2 = cut(U, 7168, H, SEQ)
        SM = cut(U, 7168, 3, H, DK)
        sqo = cut(U, 3072, 2, 2 * H, HD)
        QD = cut(actf, 0, H, NT)
        FD = cut(actf, H * NT, H, NT)
        KD = cut(actf, 2 * H * NT, H, NT)
        E1 = cut(actf, 3 * H * NT, H, NT)
        D1 = cut(actf, 4 * H * NT, H, NT)
        E1g = o_T[:, :, :].rearrange("p c t -> p (c t)")[:, 0:BLK * 2 * GW].rearrange("p (b n) -> p b n", b=BLK)
        E1v = cut(actf, 3 * H * NT, H, SEQ)
        D1v = cut(actf, 4 * H * NT, H, SEQ)
        CG = cut(hf, 0, KC, NT)
        latU = cut(U, 0, DEC - RING_LAT, PAGES, KVL)
        krT = cut(U, 7680, 4 * P)

        def lat(b):
            if b >= RING_LAT:
                return latU[:, b - RING_LAT]
            return cut(ring[:, (FFN_SLABS + len(SLABS) + b // 2) % RING, :], (b % 2) * PAGES * KVL, PAGES, KVL)

        SQ = cut(U, 6656, 4, GW)
        latT = cut(hf, 0, PAGES, P)
        rsk, SA, PA = (decs[:, i, :] for i in range(3))
        num, ssq = decs[:, 3:5, :], decs[:, 5:7, :]
        VB = cut(U, 0, DEC, NPAT, GW)
        Qbc = cut(U, 6144, DEC, GW)
        SI = cut(U, 8192, X_N)
        KB = cut(hf, 0, K_SLOTS, NPAT, GW)
        qm = cut(hf, 0, DEC, GW)
        prod = cut(actf, 3072, NPAT, GW)
        dtmp = bsum[:, 0:2, :, :].rearrange("p a b h -> p a (b h)")
        lsum = mxs[:, 0, :]
        STC = cut(actf, 0, 16, HD)
        STD = cut(actf, 1024, 32, HD)
        OUTER = cut(actf, 3072, 32, HD)

        ps = [ctx.enter_context(nc.psum_tensor(f"bank{i}", [P, 512], f32)) for i in range(8)]

        def bank(i, rows, *shape):
            return cut(ps[i], 0, *shape)[0:rows]

        ident = cst[:, K_ID:K_ID + P]
        Lmask = cut(cst, K_LV, len(LEVELS) - 1, P)
        selh = cut(cst, K_SELH, H, P)
        cos = cut(cst, K_COS, BLK, ROPE // 2)
        sin = cut(cst, K_SIN, BLK, ROPE // 2)

        def kr(b):
            w = PAGES * ROPE
            if b in KR_RING:
                return cut(ring[:, (FFN_SLABS + len(SLABS) + RING - 1) % RING, :], PAGES * KVL + (b - KR_RING[0]) * w, w)
            return {0: cut(actf, FT * NT - w, w), 1: rp[:, :, :].rearrange("p a n -> p (a n)")[:, 0:w],
                    2: sg[:, :, :].rearrange("p a n -> p (a n)")[:, 0:w], DEC - 1: cut(U, 6144, w)}[b]

        def rotary(b):
            return kr(b).rearrange("p (g c) -> p g c", g=PAGES)

        def rep(ap, at, n):
            shape = list(ap.shape)
            return ap.unsqueeze(at).broadcast_to(shape[:at] + [n] + shape[at:])

        loaded = [sem(f"slot_loaded_{i}") for i in range(RING)]
        pages_loaded = [sem(f"pages_loaded_{b}") for b in range(DEC)]
        kr_loaded = [sem(f"rotary_keys_loaded_{b}") for b in KR_POOL]
        k_loaded = [sem(f"window_k_loaded_{i}") for i in range(K_SLOTS)]
        ends = [max(i for i, k in enumerate(TICKETS) if k[0] == n) + 1 for n in range(len(SLABS))]

        def slab_arrived(eng, l, n, more=0):
            eng.wait_ge(loaded[n % RING], (l * (LAYER_SLABS // RING) + more + (n // RING + 1)) * 32)

        def settled(eng):
            eng.sem_inc(sem("settled"), 1)

        block = ctx.enter_context(nc.Block())

        @block.sync
        def _(sp):
            sp.dma_start(pages[:, :], t["page_table"]).then_inc(sem("page_table_loaded"), 16)
            for b in range(2):
                sp.dma_start(xin[:, b, :], t["x_prompt"][0, b * P:(b + 1) * P, :]).then_inc(sem("x_loaded"), 16)
            sp.dma_start(xin[0:DEC, 2, :], t["x_sample"].rearrange("b s d -> (b s) d")).then_inc(sem("x_loaded"), 16)
            for dst, name in ((cst, "constants"), (gcols, "g_col"), (lbx, "lb_col"), (cbias, "c_bias")):
                sp.dma_start(dst[:], t[name]).then_inc(sem("constants_loaded"), 16)

            def ffn(l, f, n0):
                gate, up, down = (t[f"w{f + 1}_{x}"][bass.ds(l, 1)].rearrange("a (c p) n -> p (a c) n", p=P)
                                  for x in ("gate", "up", "down"))

                def gate_up(j, n):
                    dst = ring[:, n % RING, :].rearrange("p (g c n) -> p g c n", g=2, c=KC)
                    sp.dma_start(dst[:, 0], gate[:, :, bass.ds(j * (2 * P), 2 * P)]).then_inc(loaded[n % RING], 16)
                    sp.dma_start(dst[:, 1], up[:, :, bass.ds(j * (2 * P), 2 * P)]).then_inc(loaded[n % RING], 16)

                def down_tile(m, n):
                    dst = ring[:, n % RING, 0:FT * P].rearrange("p (c n) -> p c n", c=FT)
                    for k in range(0, FT, FT // 2):
                        sp.dma_start(dst[:, k:k + FT // 2], down[:, k:k + FT // 2, bass.ds(m * P, P)])\
                            .then_inc(loaded[n % RING], 16)

                tiles, outs = l * (2 * FT) + f * FT, l * (3 * KC) + (2 * KC * f + OUT_CREDIT)
                for j in range(RING):
                    if f == 0:
                        sp.wait_ge(sem("stream_out"), outs + j - 2)
                    else:
                        sp.wait_ge(sem("stream_out"), outs - KC + (OUT_SLABS[j][0] + OUT_SLABS[j][1]))
                    gate_up(j, n0 + j)
                with sp.Fori(1, NG // RING) as i:
                    for r in range(RING):
                        sp.wait_ge(sem("gate_up_out"), tiles + i * (2 * RING) + (2 * r + 2 - 2 * RING))
                        gate_up(i * RING + r, n0 + r)
                for j in range(NG // RING * RING, NG):
                    sp.wait_ge(sem("gate_up_out"), tiles + 2 * (j - RING + 1))
                    gate_up(j, n0 + j)
                for m in range(ND):
                    if m < RING:
                        sp.wait_ge(sem("gate_up_out"), tiles + 2 * (NG + m - RING + 1))
                    else:
                        sp.wait_ge(sem("stream_out"), outs + (m - RING + 1))
                    down_tile(m, n0 + NG + m)

            with sp.Fori(0, DEPTH) as l:
                ffn(l, 0, 0)
                w_in = t["w_in"][bass.ds(l, 1)].rearrange("a (c p) n -> p (a c) n", p=P)
                w_out = t["w_out"][bass.ds(l, 1)].rearrange("a (c p) n -> p (a c) n", p=P)

                def halves(src, c, w, n):
                    dst = ring[:, n % RING, 0:KC * w].rearrange("p (c n) -> p c n", c=KC)
                    for k in range(0, KC, KC // 2):
                        sp.dma_start(dst[:, k:k + KC // 2], src[:, k:k + KC // 2, c:c + w]).then_inc(loaded[n % RING], 16)

                def sample_pages(b, cache, dst, done):
                    settled(sp)
                    src = t[cache][bass.ds(l, 1)].rearrange("a g p c -> p (a g) c")
                    with sp.Fori(0, PAGES) as i:
                        page = sp.value_load(pages[0:1, bass.ds(i + b * PAGES, 1)], min_val=0, max_val=src.shape[1] - 1)
                        sp.dma_start(dst[:, bass.ds(i, 1), :], src[:, bass.ds(page, 1), :]).then_inc(done, 16)

                sp.wait_ge(sem("page_table_loaded"), 16)
                for i, (c, w, _) in enumerate(SLABS):
                    if i < RING:
                        sp.wait_ge(sem("stream_out"), l * (3 * KC) + (KC - RING + i + 1 + OUT_CREDIT))
                    else:
                        sp.wait_ge(sem("w_in_out"), l * NTK + ends[i - RING])
                    halves(w_in, c, w, FFN_SLABS + i)
                for b in range(RING_LAT):
                    if b % 2 == 0:
                        sp.wait_ge(sem("w_in_out"), l * NTK + ends[len(SLABS) - RING + b // 2])
                    sample_pages(b, "cache_mla_latent", lat(b), pages_loaded[b])
                sp.wait_ge(sem("mgates_ready"), l + 1)
                sample_pages(2, "cache_mla_krope", rotary(2), pages_loaded[2])
                for b in KR_RING:
                    if b not in KR_POOL:
                        sample_pages(b, "cache_mla_krope", rotary(b), pages_loaded[b])
                sp.wait_ge(sem("mixed_turned"), (l + 1) * 4)
                sp.wait_ge(sem("scratch_stored"), (l + 1) * 16 * N_SCRATCH)
                sp.wait_ge(sem("prompt_states_stored"), (l + 1) * 16 * N_PSTATE)
                for b in range(RING_LAT, DEC):
                    sample_pages(b, "cache_mla_latent", lat(b), pages_loaded[b])
                for i, (m, k) in enumerate(OUT_SLABS):
                    if i < RING - 1:
                        sp.wait_ge(sem("ctx_out"), l * DEC + (2 * i + 2))
                    else:
                        sp.wait_ge(sem("kr_turned"), l * DEC + (KR_RING[-1] + 1))
                    halves(w_out, m * P, k * P, FFN_SLABS + len(SLABS) + i)

                cache = t["cache_swa_k"][bass.ds(l, 1)].rearrange("a b t w -> (a b) t w")

                for b in range(DEC):
                    if b == 0:
                        sp.wait_ge(sem("q_spread"), (l + 1) * 4)
                    if b >= K_SLOTS:
                        sp.wait_ge(sem("window_products"), l * DEC + (b - K_SLOTS + 1))
                    for i, (w, d) in enumerate(PATTERNS):
                        sp.dma_start(KB[:, b % K_SLOTS, i, :], cache[b, PAST - w:PAST - w + (w // d - 1) * d + 1:d, :])\
                            .then_inc(k_loaded[b % K_SLOTS], 16)
                ffn(l, 1, FFN_SLABS + MIX_SLABS)
            sp.wait_ge(sem("y_turned"), 6)
            sp.dma_start(t["y_prompt"][0].rearrange("(b p) d -> p b d", p=P), xin[:, 0:2, :]).then_inc(sem("y_stored"), 16)
            sp.dma_start(t["y_sample"].rearrange("b s d -> (b s) d"), xin[0:DEC, 2, :]).then_inc(sem("y_stored"), 16)
            sp.wait_ge(sem("y_stored"), 32)

        @block.gpsimd
        def _(pool):
            pool.memset(ones[:, :], 1.0).then_inc(sem("ones_set"), 1)
            pool.memset(eps[:, :], EPS).then_inc(sem("ones_set"), 1)
            pool.memset(TM[:, :, :], 0.0).then_inc(sem("ones_set"), 1)
            pool.memset(qrb[:, :, :, :], 0.0).then_inc(sem("ones_set"), 1)

            def shift(l, f):
                n = (PAST - 1) * GW
                for b in range(DEC // 2):
                    pool.wait_ge(sem("ffn_tiles"), l * (2 * FT) + (f * FT + 5 * b + 1 + CREDIT))
                    for x in ("k", "v"):
                        src = t[f"cache_swa_{x}"][bass.ds(l, 1)].rearrange("a b t w -> (a b) (t w)")
                        dst = t[f"s_swa_{x}"][bass.ds(l, 1)].rearrange("a b t w -> (a b) (t w)")
                        i = f * (DEC // 2) + b
                        pool.dma_start(dst[i:i + 1, 0:n].rearrange("a (q n) -> (a q) n", q=64),
                                       src[i:i + 1, GW:GW + n].rearrange("a (q n) -> (a q) n", q=64))\
                            .then_inc(sem("window_shifted"), 16)

            qd, fd, kd = (jq[:, 32 + 32 * g:64 + 32 * g] for g in range(3))
            q, k = jq[:, 0:16], jq[:, 16:32]

            def state_d(l):
                pool.drain()
                pool.wait_ge(sem("state_m"), l + 1)
                pool.tensor_tensor(OUTER, rep(kd, 2, HD), rep(SI[:, X_DI:X_DI + HD], 1, 32), MUL)
                pool.tensor_tensor(STD, STD, rep(fd, 2, HD), MUL)
                pool.drain()
                pool.tensor_tensor(STD, STD, OUTER, ADD)
                pool.drain()
                pool.tensor_tensor(OUTER, STD, rep(qd, 2, HD), MUL).then_inc(sem("state_d_products"), 1)

            def state_c(l):
                pool.drain()
                pool.wait_ge(sem("state_exp"), l + 1)
                settled(pool)
                pool.tensor_scalar(k, k, sst[:, 8:9], M_SCALE, MUL, MUL)
                pool.tensor_scalar(cut(actf, 0, 1024), cut(actf, 0, 1024), sst[:, 7:8], None, MUL)
                pool.tensor_scalar(nst[:, :], nst[:, :], sst[:, 7:8], None, MUL)
                pool.drain()
                pool.wait_ge(sem("state_d_summed"), l + 1)
                O16 = OUTER[:, 0:16, :]
                pool.tensor_tensor(O16, rep(k, 2, HD), rep(SI[:, X_MV:X_MV + HD], 1, 16), MUL)
                pool.tensor_tensor(nst[:, :], nst[:, :], k, ADD)
                pool.drain()
                pool.tensor_tensor(STC, STC, O16, ADD)
                pool.tensor_tensor(k, nst[:, :], q, MUL)
                pool.drain()
                pool.tensor_tensor(O16, STC, rep(q, 2, HD), MUL).then_inc(sem("states_updated"), 1)

            with pool.Fori(0, DEPTH) as l:
                pool.dma_start(gains[:, :], t["gains"][bass.ds(l, 1)].rearrange("a n -> (a n)").partition_broadcast(P))\
                    .then_inc(sem("small_loaded"), 16)
                pool.dma_start(wuq[:, :, :], t["a_wuq"][bass.ds(l, 1)].rearrange("a (c p) n -> p (a c) n", p=P))\
                    .then_inc(sem("small_loaded"), 16)
                pool.dma_start(wukv[:, :, :], t["a_wukv"][bass.ds(l, 1)].rearrange("a p (h n) -> p (a h) n", h=H))\
                    .then_inc(sem("small_loaded"), 16)
                shift(l, 0)
                pool.wait_ge(sem("rows_final"), l + 1)
                for name, c, w in (("mla_latent", CKV, KVL), ("mla_krope", CKR, ROPE), ("swa_k", BK, GW), ("swa_v", BV, GW)):
                    pool.dma_start(t["p_" + name][bass.ds(l, 1)].rearrange("a (b p) w -> p (a b) w", p=P),
                                   TM[:, 0:2, c:c + w]).then_inc(sem("rows_stored"), 16)
                    dst = t["s_" + name][bass.ds(l, 1)]
                    if name[0:3] == "mla":
                        dst = dst.rearrange("a b w -> (a b) w")
                    else:
                        dst = dst[:, :, PAST - 1:PAST, :].rearrange("a b t w -> (a b) (t w)")
                    pool.dma_start(dst, TM[0:DEC, 2, c:c + w]).then_inc(sem("rows_stored"), 16)
                def rotary_keys(b):
                    kropes = t["cache_mla_krope"][bass.ds(l, 1)].rearrange("a g p c -> p (a g) c")
                    settled(pool)
                    with pool.Fori(0, PAGES) as i:
                        page = pool.value_load(pages[0:1, bass.ds(i + b * PAGES, 1)], min_val=0, max_val=kropes.shape[1] - 1)
                        pool.dma_start(rotary(b)[:, bass.ds(i, 1), :], kropes[:, bass.ds(page, 1), :])\
                            .then_inc(kr_loaded[KR_POOL.index(b)], 16)

                pool.wait_ge(sem("page_table_loaded"), 16)
                rotary_keys(0)
                pool.wait_ge(sem("qk_final"), l + 1)
                rotary_keys(1)
                pool.wait_ge(sem("w_in_out"), (l + 1) * NTK)
                for b in KR_RING:
                    if b in KR_POOL:
                        rotary_keys(b)

                def level_decays(i):
                    half = LEVELS[i]
                    n = SEQ // (2 * half)
                    mid = max(half - 1, 0)
                    for h in range(H):
                        fv, dv = (v.rearrange("p (n s) -> p n s", n=n) for v in (FD[:, h, 0:SEQ], D1v[:, h, :]))
                        last = pool.tensor_tensor(dv, fv, rep(fv[:, :, mid], 2, 2 * half), SUB)
                    last.then_inc(sem("level_diff"), 1)

                pool.wait_ge(sem("mgates_ready"), l + 1)
                settled(pool)
                level_decays(0)
                pool.wait_ge(sem("mlstm_state"), l + 1)
                pool.dma_start(t["p_mlstm_C"][bass.ds(l, 1)].rearrange("a h k v -> k (a h) v"), CGS[0:HD, :, 0:HD])\
                    .then_inc(sem("prompt_states_stored"), 16)
                pool.dma_start(t["p_mlstm_n"][bass.ds(l, 1)].rearrange("a h k -> k (a h)").unsqueeze(2),
                               CGS[0:HD, :, HD:HD + 1], allow_slow_non_contiguous=True).then_inc(sem("prompt_states_stored"), 16)
                pool.dma_start(t["p_mlstm_m"][bass.ds(l, 1)].rearrange("a (h o) -> (a h) o", o=1),
                               CG[0:H, 7, SEQ - 1:SEQ]).then_inc(sem("prompt_states_stored"), 16)
                for i in range(1, len(LEVELS)):
                    pool.wait_ge(sem("level_exp"), l * len(LEVELS) + i)
                    settled(pool)
                    level_decays(i)
                pool.wait_ge(sem("hgrn_state"), l + 1)
                pool.dma_start(t["p_hgrn_S"][bass.ds(l, 1)].rearrange("a h k v -> k (a h) v"), DGS)\
                    .then_inc(sem("prompt_states_stored"), 16)
                scr = t["scratch"][bass.ds(l, 1)].rearrange("a b h x -> (a b) h x")
                for g in range(4):
                    pool.dma_start(scr[:, :, g * HD:(g + 1) * HD],
                                   TM[0:DEC, 2, MQ + g * GW:MQ + (g + 1) * GW].rearrange("b (h d) -> b h d", h=H))\
                        .then_inc(sem("scratch_stored"), 16)
                for x, c in ((X_CO, GATE), (X_DG, GATE + GW)):
                    pool.dma_start(scr[:, :, x:x + HD], TM[0:DEC, 2, c:c + GW].rearrange("b (h d) -> b h d", h=H))\
                        .then_inc(sem("scratch_stored"), 16)
                for g in range(3):
                    pool.dma_start(scr[:, :, X_QD + g * DK:X_QD + (g + 1) * DK], SM[0:DEC, g])\
                        .then_inc(sem("scratch_stored"), 16)
                for g in range(2):
                    pool.dma_start(scr[:, :, X_I + g:X_I + g + 1], gTs[:, g, :].unsqueeze(2), allow_slow_non_contiguous=True)\
                        .then_inc(sem("scratch_stored"), 16)
                pool.wait_ge(sem("mixed_turned"), (l + 1) * 4)
                pool.wait_ge(sem("scratch_stored"), (l + 1) * 16 * N_SCRATCH)
                pool.wait_ge(sem("prompt_states_stored"), (l + 1) * 16 * N_PSTATE)
                for j in range(4):
                    rows = slice(32 * j, 32 * j + 32)
                    for dst, src in ((SI[rows, :], scr.rearrange("b h x -> (b h) x")),
                                     (STC[rows], t["state_mlstm_C"][bass.ds(l, 1)].rearrange(
                                         "a b h k v -> (a b h) k v")[:, 16 * j:16 * j + 16, :]),
                                     (nst[rows], t["state_mlstm_n"][bass.ds(l, 1)].rearrange(
                                         "a b h k -> (a b h) k")[:, 16 * j:16 * j + 16]),
                                     (sst[rows, 0:1], t["state_mlstm_m"][bass.ds(l, 1)].rearrange(
                                         "a b (h o) -> (a b h) o", o=1)),
                                     (STD[rows], t["state_hgrn_S"][bass.ds(l, 1)].rearrange(
                                         "a b h k v -> (a b h) k v")[:, 32 * j:32 * j + 32, :])):
                        pool.dma_start(dst, src).then_inc(sem("state_loaded"), 16)
                for b in range(DEC):
                    pool.drain()
                    pool.wait_ge(sem("latent_max"), l * DEC + b + 1)
                    settled(pool)
                    pool.partition_all_reduce(lmx[:, 1, :], lmx[:, 0, :], P, RMAX).then_inc(sem("latent_max_all"), 1)
                    if b == 0:
                        rotary_keys(DEC - 1)
                    if b == 2:
                        state_d(l)
                    if b == 4:
                        state_c(l)
                pool.wait_ge(sem("ctx_done"), (l + 1) * DEC)
                cache = t["cache_swa_v"][bass.ds(l, 1)].rearrange("a b t w -> (a b) t w")
                for b in range(DEC):
                    for i, (w, d) in enumerate(PATTERNS):
                        pool.dma_start(VB[:, b, i, :], cache[b, PAST - w:PAST - w + (w // d - 1) * d + 1:d, :])\
                            .then_inc(sem("window_v_loaded"), 16)
                pool.drain()
                pool.wait_ge(sem("window_max"), l + 1)
                settled(pool)
                pool.partition_all_reduce(wmx[:, 2, :], wmx[:, 0, :], P, RMAX)\
                    .then_inc(sem("window_max_all"), 1)
                pool.wait_ge(sem("states_updated"), l + 1)
                for j in range(4):
                    rows = slice(32 * j, 32 * j + 32)
                    pool.dma_start(t["s_mlstm_C"][bass.ds(l, 1)].rearrange(
                        "a b h k v -> (a b h) k v")[:, 16 * j:16 * j + 16, :], STC[rows]).then_inc(sem("sample_states_stored"), 16)
                    pool.dma_start(t["s_mlstm_n"][bass.ds(l, 1)].rearrange(
                        "a b h k -> (a b h) k")[:, 16 * j:16 * j + 16], nst[rows]).then_inc(sem("sample_states_stored"), 16)
                    pool.dma_start(t["s_hgrn_S"][bass.ds(l, 1)].rearrange(
                        "a b h k v -> (a b h) k v")[:, 32 * j:32 * j + 32, :], STD[rows]).then_inc(sem("sample_states_stored"), 16)
                pool.dma_start(t["s_mlstm_m"][bass.ds(l, 1)].rearrange("a b (h o) -> (a b h) o", o=1),
                               sst[0:32, 3:4]).then_inc(sem("sample_states_stored"), 16)
                pool.wait_ge(sem("mixer_done"), l + 1)
                shift(l, 1)
            pool.wait_ge(sem("window_shifted"), DEPTH * DEC * 2 * 16)
            pool.wait_ge(sem("rows_stored"), DEPTH * N_STORE * 16)
            pool.wait_ge(sem("prompt_states_stored"), DEPTH * N_PSTATE * 16)
            pool.wait_ge(sem("sample_states_stored"), DEPTH * N_SSTATE * 16)
        @block.scalar
        def _(act):
            act.preload_act_table_set("natural_log_exp_and_others")
            act.wait_ge(sem("ones_set"), 4)
            act.wait_ge(sem("lb_shifted"), 1)
            act.activation(lbs[:, :, 0:H], lbs[:, :, H:2 * H], ACT.Exp).then_inc(sem("lb_exp"), 1)
            for c in range(KC):
                act.wait_ge(sem("x_turned"), c + 1)
                act.copy(x_T[:, c, :], bank(c, P, NT)).then_inc(sem("x_copied"), 1)

            def inverse_roots(dst, src, widths):
                for a, b, w in widths:
                    act.activation(dst[:, a:b], src[:, a:b], ACT.Ln, bias=eps[0:dst.shape[0], :], scale=1.0 / w)
                act.drain()
                lo, hi = widths[0][0], widths[-1][1]
                return act.activation(dst[:, lo:hi], dst[:, lo:hi], ACT.Exp, scale=-0.5)

            def norm(l, k):
                act.wait_ge(sem("mean_square"), l * 3 + (k + 1))
                inverse_roots(rstd, bank(6, P, NT), [(0, NT, D_MODEL)]).then_inc(sem("rstd_ready"), 1)

            def sigmoid(dst, src):
                act.activation(dst, src, ACT.Exp, scale=-1.0)
                act.drain()
                act.activation(dst, dst, ACT.Ln, bias=1.0)
                act.drain()
                return act.activation(dst, dst, ACT.Exp, scale=-1.0)

            def ffn(l, f):
                with act.Fori(0, FT // 2) as j:
                    for q in range(2):
                        act.wait_ge(sem("gate_up_out"), l * (2 * FT) + j * 2 + (f * FT + q + 1))
                        act.activation(sg[:, q, :], bank(2 * q, P, NT), ACT.Exp, scale=-1.0).then_inc(sem("gate_exp"), 1)

            def copy_out(l, first, last):
                for k in range(first, last):
                    n, kind, i = TICKETS[k]
                    act.wait_ge(sem("w_in_out"), l * NTK + (k + 1))
                    if kind == "rows":
                        w = GW if n == 4 else SLABS[n][1]
                        dst, src = TM[0:ROWS[i], i, SLABS[n][2]:SLABS[n][2] + w], bank(k % 4, ROWS[i], w)
                    elif kind == "gate":
                        dst, src = sg[0:H, i, :], bank(k % 4, H, NT)
                    else:
                        dst, src = (QD if n == 6 else FD)[:, i, :], bank(k % 4, P, NT)
                    act.copy(dst, src).then_inc(sem("w_in_copied"), 1)

            def softmax_exp(l, a):
                act.wait_ge(sem("scores_shifted"), l * 2 + (a + 1))
                act.activation(S[:, :, :], S[:, :, :], ACT.Exp).then_inc(sem("scores_exp"), 1)
                for h in range(H):
                    act.wait_ge(sem("probs_turned"), (l * 2 + a) * H + (h + 1))
                    act.copy(PT[:, h, :], bank(4 + h, P, 3 * P)).then_inc(sem("probs_copied"), 1)

            with act.Fori(0, DEPTH) as l:
                norm(l, 0)
                ffn(l, 0)
                norm(l, 1)
                copy_out(l, 0, 9)
                act.wait_ge(sem("squares1"), l + 1)
                for a, b, w in ((0, 3, QL), (3, 6, KVL), (6, 9, ROPE), (9, 33, HD)):
                    act.activation(rs[:, a:b], st[:, a:b], ACT.Ln, bias=eps[:, :], scale=1.0 / w)
                act.drain()
                act.activation(rs[:, 0:33], rs[:, 0:33], ACT.Exp, scale=-0.5).then_inc(sem("roots1"), 1)
                copy_out(l, 9, 12)
                act.wait_ge(sem("down_turned"), l + 1)
                act.copy(cqT[:, 0, :], bank(4, P, NT))
                act.copy(cqT[:, 1, :], bank(5, P, NT))
                act.copy(latn[:, :], bank(6, P, NT)).then_inc(sem("down_copied"), 1)
                copy_out(l, 12, ends[4])
                act.wait_ge(sem("qk_cleared"), l + 1)
                act.wait_ge(sem("up_out"), l * 2 + 1)
                for i, bk in enumerate((4, 5, 7)):
                    act.copy(Qk[0:ROWS[i], i], bank(bk, ROWS[i], H, QKW))
                for i in range(2):
                    last = act.copy(Kk[:, i, :, 0:NOPE], cut(ps[6], i * GW, H, NOPE))
                last.then_inc(sem("up_copied"), 1)
                act.wait_ge(sem("up_out"), l * 2 + 2)
                act.copy(Kk[0:DEC, 2, :, 0:NOPE], bank(4, DEC, H, NOPE)).then_inc(sem("up_copied"), 1)
                copy_out(l, ends[4], ends[5])
                act.wait_ge(sem("squares2"), l + 1)
                for a, b, w in ((0, 12, NOPE), (12, 24, ROPE), (24, 36, NOPE)):
                    act.activation(rs[:, a:b], st[:, a:b], ACT.Ln, bias=eps[:, :], scale=1.0 / w)
                act.drain()
                act.activation(rs[:, :], rs[:, :], ACT.Exp, scale=-0.5).then_inc(sem("roots2"), 1)
                copy_out(l, ends[5], ends[6])
                act.wait_ge(sem("qk_turned"), l * 2 + 1)
                for i in range(2):
                    act.copy(QT[0:QKW, 2 * i:2 * i + 2, :], bank(4 + i, QKW, 2, SEQ))
                for i in range(2):
                    last = act.copy(KT[0:QKW, 2 * i:2 * i + 2, :], bank(6 + i, QKW, 2, SEQ))
                last.then_inc(sem("qk_copied"), 1)
                act.wait_ge(sem("qk_turned"), l * 2 + 2)
                act.copy(qtT[0:HD], bank(4, HD, H, DEC))
                for j in range(4):
                    rows = slice(32 * j, 32 * j + 32)
                    act.copy(qrb[rows, :, j, :].rearrange("p b h -> p h b"), cut(ps[4], H * DEC, H, DEC)[rows])
                act.copy(wukT[0:HD], bank(5, HD, H, P))
                act.copy(nsA[:, :], bank(6, P, DEC * H))
                act.copy(wuk[:, 0:GW].rearrange("p (h d) -> p h d", h=H), wukv[:, :, 0:NOPE])\
                    .then_inc(sem("qk_copied"), 1)
                act.wait_ge(sem("u_out"), l + 1)
                act.copy(wuk[:, GW:].rearrange("p (b h) -> p h b", b=DEC), bank(7, P, H, DEC)).then_inc(sem("u_copied"), 1)
                copy_out(l, ends[6], ends[7])
                act.wait_ge(sem("pairs_turned"), l + 1)
                for i in range(4):
                    last = act.copy(pairT[:, i], bank(4 + i, P, 2, SEQ))
                last.then_inc(sem("pairs_copied"), 1)
                act.wait_ge(sem("gates_bounded"), l * 2 + 1)
                act.activation(E1[:, :, :], FD[:, :, :], ACT.Exp, scale=-1.0)
                act.drain()
                act.activation(KD[:, :, :], E1[:, :, :], ACT.Ln, bias=1.0)
                act.drain()
                act.activation(KD[:, :, :], KD[:, :, :], ACT.Exp, scale=-1.0).then_inc(sem("dgates"), 1)
                sigmoid(D1[:, :, :], D1[:, :, :]).then_inc(sem("dgates"), 1)
                copy_out(l, ends[7], ends[8])
                act.wait_ge(sem("forget_ready"), l + 1)
                act.activation(D1[:, :, :], FD[:, :, :], ACT.Ln).then_inc(sem("forget_log"), 1)
                copy_out(l, ends[8], NTK)
                act.wait_ge(sem("gates_bounded"), l * 2 + 2)
                sigmoid(E1g, E1g).then_inc(sem("gates_sigmoid"), 1)
                softmax_exp(l, 0)
                act.wait_ge(sem("prompt_out"), l * 2 + 1)
                for i in range(2):
                    last = act.copy(ctxT[:, 2 * i:2 * i + 2, 0:SEQ], bank(4 + i, P, 2, SEQ))
                last.then_inc(sem("prompt_copied"), 1)
                softmax_exp(l, 1)
                act.wait_ge(sem("prompt_out"), l * 2 + 2)
                for i in range(2):
                    last = act.copy(o_T[:, 2 + i, 0:SEQ], bank(4 + i, P, SEQ))
                last.then_inc(sem("prompt_copied"), 1)
                act.wait_ge(sem("mgate"), l + 1)
                act.activation(CG[0:H, 2, :], CG[0:H, 2, :], ACT.Exp, scale=-1.0)
                act.drain()
                act.activation(CG[0:H, 2, :], CG[0:H, 2, :], ACT.Ln, bias=1.0).then_inc(sem("mgate_log"), 1)
                act.wait_ge(sem("mweights"), l + 1)
                act.activation(WT[:, :, :], WT[:, :, :], ACT.Exp, scale=-1.0)
                act.activation(wd[:, :, :], wd[:, :, :], ACT.Exp, scale=-1.0)
                act.activation(emt[:, :, :], gT[:, 2:4, :], ACT.Exp, scale=-1.0).then_inc(sem("mweights_exp"), 1)
                for i, half in enumerate(LEVELS):
                    if i:
                        act.wait_ge(sem("level_ready"), l * len(LEVELS) + i)
                    act.wait_ge(sem("level_diff"), l * len(LEVELS) + (i + 1))
                    if half > 1:
                        dv, ev = (v.rearrange("p h (n r s) -> p (h n) r s", r=2, s=half) for v in (D1v, E1v))
                        act.activation(ev[:, :, 0, :], dv[:, :, 0, :], ACT.Exp, scale=-1.0)
                        act.activation(ev[:, :, 1, :], dv[:, :, 1, :], ACT.Exp).then_inc(sem("level_exp"), 1)
                    else:
                        act.activation(E1v, D1v, ACT.Exp)
                        act.activation(E2[:, :, :], D1v, ACT.Exp, scale=-1.0).then_inc(sem("level_exp"), 1)
                act.wait_ge(sem("levels_done"), l + 1)
                for h in range(H):
                    last = act.activation(E1v[:, h, :], FD[:, h, 0:SEQ], ACT.Exp, scale=-1.0, bias=FD[:, h, SEQ - 1:SEQ])
                last.then_inc(sem("end_exp"), 1)
                act.wait_ge(sem("end_turned"), l + 1)
                for i in range(2):
                    act.copy(KE[:, i], bank(6 + i, P, H, DK))
                for i in range(3):
                    last = act.copy(SM[0:DEC, i], bank(i, DEC, H, DK))
                last.then_inc(sem("end_copied"), 1)
                act.wait_ge(sem("squares3"), l + 1)
                inverse_roots(rs, st, [(0, 16, HD)]).then_inc(sem("roots3"), 1)
                for i in range(4):
                    act.wait_ge(sem("mixed_out"), l * 4 + (i + 1))
                    act.copy(o_T[:, 4 + i, 0:SEQ], bank(4 + i, P, SEQ)).then_inc(sem("mixed_turned"), 1)
                act.wait_ge(sem("scratch_stored"), (l + 1) * 16 * N_SCRATCH)
                act.wait_ge(sem("prompt_states_stored"), (l + 1) * 16 * N_PSTATE)

                def copy_pages(b, c):
                    act.wait_ge(sem("lat_turned"), (l * DEC + b) * 4 + (c + 1))
                    act.copy(latT[:, 4 * c:4 * c + 4, :], bank(c % 2, P, 4, P)).then_inc(sem("lat_copied"), 1)

                def roots(b):
                    act.wait_ge(sem("page_taken"), (l * DEC + b + 1) * PAGES)
                    inverse_roots(rsk, ssq[:, b % 2, :], [(0, PAGES * H, NOPE)]).then_inc(sem("page_roots"), 1)

                def exps(b):
                    act.wait_ge(sem("latent_shifted"), l * DEC + (b + 1))
                    act.activation(PA, SA, ACT.Exp, scale=A_SCALE).then_inc(sem("latent_exp"), 1)
                    if b == 3:
                        act.wait_ge(sem("state_m"), l + 1)
                        act.activation(sst[:, 7:10], sst[:, 4:7], ACT.Exp).then_inc(sem("state_exp"), 1)

                copy_pages(0, 0)
                for b in range(DEC):
                    for c in range(4):
                        if c < 3:
                            copy_pages(b, c + 1)
                        elif b + 1 < DEC:
                            copy_pages(b + 1, 0)
                        if c == 2:
                            act.wait_ge(sem("kr_turned"), l * DEC + (b + 1))
                            act.copy(krT, bank(2, P, 4 * P)).then_inc(sem("kr_copied"), 1)
                        for g in range(4 * c, 4 * c + 4):
                            n = (l * DEC + b) * PAGES + g
                            act.wait_ge(sem("page_out"), n + 1)
                            act.activation(SQ[:, g % 4, :], bank(4 + g % 4, P, GW), ACT.Square).then_inc(sem("page_squared"), 1)
                        if b and c == 0:
                            roots(b - 1)
                        if b and c == 2:
                            exps(b - 1)
                roots(DEC - 1)
                exps(DEC - 1)
                act.wait_ge(sem("oA_out"), l + 1)
                for i in range(2):
                    last = act.copy(o_T[:, i, :], bank(4 + i, P, NT))
                last.then_inc(sem("oA_copied"), 1)
                for i in range(4):
                    act.wait_ge(sem("q_spread"), l * 4 + (i + 1))
                    last = act.copy(Qbc[:, 2 * i:2 * i + 2, :], bank(i, P, 2, GW))
                last.then_inc(sem("q_spread_copied"), 1)
                act.wait_ge(sem("vnew_turned"), l + 1)
                act.copy(wmx[:, 1, :], bank(6, P, DEC * H))
                act.copy(vT[:, :, :], bank(7, P, 2, DEC)).then_inc(sem("vnew_copied"), 1)
                act.wait_ge(sem("squares4"), l + 1)
                inverse_roots(rs[0:32], st[0:32], [(0, 2, HD)]).then_inc(sem("roots4"), 1)
                act.wait_ge(sem("states_turned"), l + 1)
                for g in range(2):
                    for h in range(H):
                        src = cut(ps[4 + g], 0, DEC, H)[0:HD, :, h]
                        last = act.copy(o_T[HD * (h % 2):HD * (h % 2) + HD, 4 + 2 * g + h // 2, SEQ:NT], src)
                last.then_inc(sem("states_copied"), 1)
                act.wait_ge(sem("window_shifted_max"), l + 1)
                act.activation(SB[:, :, :, :], SB[:, :, :, :], ACT.Exp, scale=B_SCALE)
                act.activation(wmx[:, 3, :], wmx[:, 3, :], ACT.Exp, scale=B_SCALE).then_inc(sem("window_exp"), 1)
                act.wait_ge(sem("rows_stored"), (l + 1) * 16 * N_STORE)
                norm(l, 2)
                ffn(l, 1)
            for b in range(BLK):
                for g in range(2):
                    i = 2 * b + g
                    act.wait_ge(sem("y_out"), i + 1)
                    act.copy(xin[0:ROWS[b], b, g * 512:g * 512 + 512], bank(i, ROWS[b], 512)).then_inc(sem("y_turned"), 1)

        @block.vector
        def _(dve):
            dve.memset(sqx[:, :], 0.0).then_inc(sem("ffn_tiles"), CREDIT)
            dve.memset(ssum[:, :], 0.0).then_inc(sem("stream_added"), CREDIT)
            dve.memset(sst[:, :], 0.0).then_inc(sem("stream_out"), OUT_CREDIT)
            dve.wait_ge(sem("constants_loaded"), 4 * 16)
            dve.tensor_reduce(lbt[:, 0, :], lbx[:, :, :].rearrange("p l h -> p h l"), AX.X, MAX)
            dve.drain()
            dve.tensor_tensor(lbs[:, :, H:2 * H], lbx[:, :, :], rep(lbt[:, 0, :], 1, DEPTH), SUB).then_inc(sem("lb_shifted"), 1)
            dve.wait_ge(sem("lb_exp"), 1)
            dve.tensor_reduce(lbt[:, 0, :], lbs[:, :, 0:H].rearrange("p l h -> p h l"), AX.X, ADD)
            dve.drain()
            dve.reciprocal(lbt[:, 1, :], lbt[:, 0, :])
            dve.drain()
            dve.tensor_tensor(lbs[:, :, 0:H], lbs[:, :, 0:H], rep(lbt[:, 1, :], 1, DEPTH), MUL)
            dve.memset(lbt[:, 0, :], 0.0)
            dve.drain()
            for i in range(DEPTH):
                if i:
                    dve.tensor_tensor(lbt[:, 0, :], lbt[:, 0, :], lbs[:, i, 0:H], ADD)
                    dve.drain()
                dve.tensor_copy(lbs[:, i, 0:H], lbt[:, 0, :])
                dve.tensor_scalar(lbs[:, i, H:2 * H], lbt[:, 0, :], -1.0, 1.0, MUL, ADD)
            for c in range(KC):
                dve.wait_ge(sem("x_copied"), c + 1)
                dve.drain()
                dve.tensor_tensor(sqx[:, :], x_T[:, c, :], x_T[:, c, :], MUL)
                dve.drain()
                last = dve.tensor_tensor(ssum[:, :], ssum[:, :], sqx[:, :], ADD)
            last.then_inc(sem("squares_ready"), 1)

            def norm(l, k):
                dve.wait_ge(sem("rstd_ready"), l * 3 + (k + 1))
                for c in range(KC):
                    dve.scalar_tensor_tensor(h_T[:, c, :], x_T[:, c, :], gcol[:, k * KC + c:k * KC + c + 1], rstd[:, :],
                                             MUL, MUL).then_inc(sem("h_ready"), 1)

            def ffn(l, f):
                with dve.Fori(0, FT // 2) as j:
                    for q in range(2):
                        dve.wait_ge(sem("gate_exp"), l * (2 * FT) + j * 2 + (f * FT + q + 1))
                        dve.tensor_scalar(sg[:, q, :], sg[:, q, :], 1.0, None, ADD)
                        dve.drain()
                        dve.reciprocal(sg[:, q, :], sg[:, q, :])
                        dve.drain()
                        dve.tensor_tensor(sg[:, q, :], sg[:, q, :], bank(2 * q, P, NT), MUL)
                        dve.drain()
                        dve.tensor_tensor(act_T[:, bass.ds(j * 2 + q, 1), :].rearrange("p a t -> p (a t)"), sg[:, q, :],
                                          bank(2 * q + 1, P, NT), MUL).then_inc(sem("ffn_tiles"), 1)

            def stream(l, k, factor):
                for m in range(KC):
                    dve.wait_ge(sem("stream_out"), l * (3 * KC) + (k * KC + m + 1 + OUT_CREDIT))
                    dve.scalar_tensor_tensor(x_T[:, m, :], bank(4 + m % 2, P, NT), factor, x_T[:, m, :], MUL, ADD)\
                        .then_inc(sem("stream_added"), 1)
                    dve.drain()
                    dve.tensor_tensor(sqx[:, :] if m else ssum[:, :], x_T[:, m, :], x_T[:, m, :], MUL)
                    dve.drain()
                    if m:
                        last = dve.tensor_tensor(ssum[:, :], ssum[:, :], sqx[:, :], ADD)
                last.then_inc(sem("squares_ready"), 1)

            def gain(at, w, *reps):
                g = gains[:, at:at + w]
                for n in reversed(reps):
                    g = rep(g, 1, n)
                return g

            def rope(x, c, s, tmp):
                dve.tensor_tensor(tmp[0], x[0], c, MUL)
                dve.tensor_tensor(tmp[1], x[1], s, MUL)
                dve.tensor_tensor(tmp[2], x[0], s, MUL)
                dve.tensor_tensor(tmp[3], x[1], c, MUL)
                dve.drain()
                dve.tensor_tensor(x[0], tmp[0], tmp[1], SUB)
                return dve.tensor_tensor(x[1], tmp[2], tmp[3], ADD)

            def softmax(l, a, scale, mask, times):
                for h in range(H):
                    dve.wait_ge(sem("scores_out"), (l * 2 + a) * H + (h + 1))
                    dve.scalar_tensor_tensor(S[:, h, :], bank(4 + h, P, 3 * P), scale, cst[:, mask:mask + 3 * P], MUL, ADD)\
                        .then_inc(sem("scores_taken"), 1)
                dve.drain()
                tiles = (S[:, :, 0:P], S[:, :, P:3 * P])
                for i in range(2):
                    dve.tensor_reduce(mxs[:, i, :], tiles[i], AX.X, MAX)
                dve.drain()
                for i in range(2):
                    last = dve.tensor_tensor(tiles[i], tiles[i], rep(mxs[:, i, :], 2, P + i * P), SUB)
                last.then_inc(sem("scores_shifted"), 1)
                dve.wait_ge(sem("scores_exp"), l * 2 + (a + 1))
                if times is not None:
                    dve.tensor_tensor(S[:, :, :], S[:, :, :], rep(cst[:, times:times + 3 * P], 1, H), MUL)
                    dve.drain()
                for i in range(2):
                    dve.tensor_reduce(mxs[:, i, :], tiles[i], AX.X, ADD)
                dve.drain()
                dve.reciprocal(mxs[:, :, :], mxs[:, :, :])
                dve.drain()
                for i in range(2):
                    last = dve.tensor_tensor(tiles[i], tiles[i], rep(mxs[:, i, :], 2, P + i * P), MUL)
                last.then_inc(sem("probs_ready"), 1)

            def latent_rows(l):
                dve.wait_ge(sem("small_loaded"), (l + 1) * 3 * 16)
                dve.wait_ge(sem("w_in_copied"), l * NTK + 9)
                dve.tensor_tensor(sq1, TM[:, :, 0:BV], TM[:, :, 0:BV], MUL)
                dve.drain()
                dve.tensor_reduce(st[:, 0:3], sq1[:, :, CQ:CKV], AX.X, ADD)
                dve.tensor_reduce(st[:, 3:6], sq1[:, :, CKV:CKR], AX.X, ADD)
                dve.tensor_reduce(st[:, 6:9], sq1[:, :, CKR:BQ], AX.X, ADD)
                dve.tensor_reduce(st[:, 9:33].rearrange("p (b g) -> p b g", b=BLK),
                                  sq1[:, :, BQ:BV].rearrange("p b (g d) -> p b g d", d=HD), AX.X, ADD)\
                    .then_inc(sem("squares1"), 1)
                dve.wait_ge(sem("roots1"), l + 1)
                for b in range(BLK):
                    for c, w, r, g in ((CQ, QL, b, G_Q), (CKV, KVL, 3 + b, G_KV), (CKR, ROPE, 6 + b, G_KR)):
                        dve.scalar_tensor_tensor(TM[:, b, c:c + w], TM[:, b, c:c + w], rs[:, r:r + 1],
                                                 gains[:, g:g + w], MUL, MUL)
                qkb = TM[:, :, BQ:BV].rearrange("p b (g d) -> p b g d", d=HD)
                dve.tensor_tensor(qkb, qkb, rep(rs[:, 9:33].rearrange("p (b g) -> p b g", b=BLK), 3, HD), MUL)
                dve.drain()
                for i, g in enumerate((G_BQ, G_BK)):
                    dve.tensor_tensor(qkb[:, :, i * H:i * H + H, :], qkb[:, :, i * H:i * H + H, :], gain(g, HD, BLK, H), MUL)
                half = ROPE // 2
                rope((TM[:, :, CKR:CKR + half], TM[:, :, CKR + half:BQ]), cos, sin,
                     [cut(rp[:, i, :], 0, BLK, half) for i in range(4)]).then_inc(sem("rows_final"), 1)
                dve.memset(Qk[:, 2], 0.0)
                dve.memset(Kk[:, 2], 0.0).then_inc(sem("qk_cleared"), 1)

            def latent_qk(l):
                dve.wait_ge(sem("up_copied"), l * 2 + 2)
                dve.tensor_tensor(sq2, Qk, Qk, MUL)
                dve.tensor_tensor(sq3, Kk[:, :, :, 0:NOPE], Kk[:, :, :, 0:NOPE], MUL)
                dve.drain()
                for at, v in ((0, sq2[:, :, :, 0:NOPE]), (12, sq2[:, :, :, NOPE:]), (24, sq3)):
                    last = dve.tensor_reduce(st[:, at:at + 12].rearrange("p (b h) -> p b h", b=BLK), v, AX.X, ADD)
                last.then_inc(sem("squares2"), 1)
                dve.wait_ge(sem("roots2"), l + 1)
                parts = ((0, Qk[:, :, :, 0:NOPE], G_QN, NOPE), (12, Qk[:, :, :, NOPE:], G_QR, ROPE),
                         (24, Kk[:, :, :, 0:NOPE], G_KN, NOPE))
                for at, v, g, w in parts:
                    dve.tensor_tensor(v, v, rep(rs[:, at:at + 12].rearrange("p (b h) -> p b h", b=BLK), 3, w), MUL)
                dve.drain()
                for at, v, g, w in parts:
                    dve.tensor_tensor(v, v, gain(g, w, BLK, H), MUL)
                dve.tensor_copy(Kk[:, :, :, NOPE:], rep(TM[:, :, CKR:BQ], 2, H))
                dve.drain()
                mid = NOPE + ROPE // 2
                rope((Qk[:, :, :, NOPE:mid], Qk[:, :, :, mid:]), rep(cos, 2, H), rep(sin, 2, H),
                     [cut(rp[:, i, :], 0, BLK, H, ROPE // 2) for i in range(4)])
                dve.drain()
                s = slice(0, DEC)
                dve.tensor_tensor(qk[s], Qk[s, 2], Kk[s, 2], MUL)
                dve.tensor_tensor(qtl[s], Qk[s, 2, :, 0:NOPE], rep(gains[s, G_KN:G_KN + NOPE], 1, H), MUL)
                dve.tensor_copy(q4[s], rep(Qk[s, 2, :, NOPE:], 2, 4))
                dve.drain()
                dve.tensor_reduce(nst1[:, 0, :], qk[s], AX.X, ADD)
                dve.drain()
                dve.tensor_tensor(nsm[:, 0], rep(nst1[:, 0, :], 1, DEC), rep(ident[s, 0:DEC], 2, H), MUL)\
                    .then_inc(sem("qk_final"), 1)

            def output_gates(l):
                dve.wait_ge(sem("w_in_copied"), (l + 1) * NTK)
                dve.tensor_scalar(E1g, TM[:, :, GATE:TMW], X_MIN, None, MAX).then_inc(sem("gates_bounded"), 1)
                dve.wait_ge(sem("gates_sigmoid"), l + 1)
                dve.tensor_copy(TM[:, :, GATE:GATE + GW], E1g[:, :, 0:GW])
                dve.tensor_tensor(TM[:, :, GATE + GW:], TM[:, :, GATE + GW:], E1g[:, :, GW:], MUL)
                dve.drain()
                dve.tensor_tensor(TM[:, :, GATE:], TM[:, :, GATE:], gain(G_OUT, 2 * GW, BLK), MUL)

            def mlstm(l):
                dve.wait_ge(sem("w_in_out"), (l + 1) * NTK)
                r = slice(0, H)
                T = slice(0, SEQ)
                dve.tensor_scalar(CG[r, 0, :], sg[r, 0, :], cb[:, 0:1], None, ADD)
                dve.tensor_scalar(CG[r, 3, :], sg[r, 1, :], cb[:, 1:2], None, ADD)
                dve.drain()
                dve.tensor_scalar(CG[r, 6, :], CG[r, 3, :], 0.0, None, MIN)
                dve.scalar_tensor_tensor(CG[r, 2, :], CG[r, 3, :], -1.0, CG[r, 3, :], MUL, MAX).then_inc(sem("mgate"), 1)
                dve.wait_ge(sem("mgate_log"), l + 1)
                dve.tensor_tensor(CG[r, 1, :], CG[r, 6, :], CG[r, 2, :], SUB)
                dve.drain()
                dve.tensor_tensor_scan(CG[r, 3, T], ones[r, T], CG[r, 1, T], 0.0, MUL, ADD)
                dve.drain()
                dve.tensor_tensor(CG[r, 4, T], CG[r, 0, T], CG[r, 3, T], SUB)
                dve.drain()
                dve.tensor_tensor_scan(CG[r, 5, T], CG[r, 4, T], CG[r, 4, T], 0.0, MAX, MAX)
                dve.drain()
                dve.tensor_tensor(CG[r, 7, T], CG[r, 5, T], CG[r, 3, T], ADD).then_inc(sem("mgates_ready"), 1)
                dve.wait_ge(sem("mgates_out"), l + 1)
                dve.tensor_copy(gT[:, 0:4, :], bank(6, P, 4, H))
                dve.tensor_copy(gTs[:, :, :], cut(ps[6], 4 * H, 2, H)[0:DEC])
                for i in range(2):
                    dve.tensor_copy(gT[:, 4, 2 * i:2 * i + 2], bank(4 + i, P, 2, SEQ)[:, :, SEQ - 1])
                dve.drain()
                for h in range(H):
                    m = bank(4 + h // 2, P, 2, SEQ)[:, h % 2, :]
                    dve.tensor_scalar(WT[:, h, 0:SEQ], m, gT[:, 0, h:h + 1], 0.0, SUB, MAX)
                    dve.tensor_scalar(WT[:, h, SEQ:], m[:, P:SEQ], gT[:, 1, h:h + 1], 0.0, SUB, MAX)
                dve.tensor_tensor(wd[:, :, :], rep(gT[:, 4, :], 1, 2), gT[:, 0:2, :], SUB)
                dve.drain()
                dve.tensor_scalar(wd[:, :, :], wd[:, :, :], 0.0, None, MAX).then_inc(sem("mweights"), 1)
                dve.memset(vaug[:, :, :, HD:HD + 1], 1.0)
                dve.tensor_copy(vaug[:, :, :, 0:HD], TM[:, 0:2, MV:MV + GW].rearrange("p b (h d) -> p b h d", h=H))
                dve.wait_ge(sem("mweights_exp"), l + 1)
                dve.tensor_tensor(WT, WT, rep(cst[:, K_WM:K_WM + 3 * P], 1, H), MUL)
                dve.tensor_scalar(wd[:, :, :], wd[:, :, :], M_SCALE, None, MUL)
                dve.drain()
                dve.tensor_tensor(kw, TM[:, 0:2, MK:MK + GW].rearrange("p b (h d) -> p b h d", h=H),
                                  rep(wd[:, :, :], 3, HD), MUL).then_inc(sem("mkeys_ready"), 1)
                for h in range(H):
                    dve.wait_ge(sem("mscores_out"), l * H + (h + 1))
                    dve.tensor_tensor(S[:, h, :], bank(h, P, 3 * P), WT[:, h, :], MUL).then_inc(sem("mprobs_ready"), 1)
                dve.wait_ge(sem("mlstm_out"), l + 1)
                for i in range(2):
                    dve.tensor_copy(den[:, i, :], bank(4 + i, P, H, HD + 1)[:, :, HD])
                dve.tensor_copy(CGS[0:HD], bank(6, HD, H, HD + 1)).then_inc(sem("mlstm_state"), 1)
                dve.drain()
                dend = den[:, :, :].rearrange("p b h -> p (b h)")
                dve.scalar_tensor_tensor(dend, dend, -1.0, dend, MUL, MAX)
                dve.drain()
                dve.tensor_tensor(den[:, :, :], den[:, :, :], emt[:, :, :], MAX)
                dve.drain()
                dve.reciprocal(den[:, :, :], den[:, :, :])
                dve.drain()
                for i in range(2):
                    last = dve.tensor_tensor(HCD[:, i, 0:H, :], bank(4 + i, P, H, HD + 1)[:, :, 0:HD], rep(den[:, i, :], 2, HD), MUL)
                last.then_inc(sem("mlstm_taken"), 1)

            def level_mask(l, i):
                dve.wait_ge(sem("level_out"), l * len(LEVELS) + (i + 1))
                for g in range(2):
                    bk = 2 * (i % 2) + g
                    heads = slice(2 * g, 2 * g + 2)
                    if i == 0:
                        last = dve.tensor_copy(ATD[:, heads, 2, :], bank(bk, P, 2, P))
                    else:
                        last = dve.tensor_tensor(ATD[:, heads, 0:2, :] if i == 1 else TMPD[:, heads], bank(bk, P, 2, 2, P),
                                                 rep(rep(Lmask[:, i - 1, :], 1, 2), 1, 2), MUL)
                last.then_inc(sem("level_taken"), 1)
                if i > 1:
                    dve.drain()
                    last = dve.tensor_tensor(ATD[:, :, 0:2, :], ATD[:, :, 0:2, :], TMPD, ADD)
                dve.drain()
                return last

            def forget(l):
                dve.wait_ge(sem("w_in_copied"), l * NTK + ends[7])
                dve.tensor_scalar(D1, QD, X_MIN, None, MAX)
                dve.tensor_scalar(FD, FD, X_MIN, None, MAX).then_inc(sem("gates_bounded"), 1)
                dve.wait_ge(sem("dgates"), l * 2 + 1)
                for h in range(H):
                    dve.tensor_scalar(FD[:, h, :], E1[:, h, :], lb[:, h:h + 1], 1.0, MUL, ADD)
                dve.drain()
                dve.tensor_tensor(FD, FD, KD, MUL)
                dve.wait_ge(sem("dgates"), l * 2 + 2)
                dve.scalar_tensor_tensor(cut(actf, 0, H * NT), cut(actf, 0, H * NT), D_SCALE,
                                         cut(actf, 4 * H * NT, H * NT), MUL, MUL).then_inc(sem("forget_ready"), 1)
                dve.drain()
                dve.tensor_tensor(KD, KD, E1, MUL)
                dve.drain()
                for h in range(H):
                    dve.tensor_scalar(KD[:, h, :], KD[:, h, :], lb[:, H + h:H + h + 1], None, MUL)
                dve.wait_ge(sem("forget_log"), l + 1)
                for h in range(H):
                    dve.tensor_tensor_scan(FD[:, h, 0:SEQ], ones[:, :], D1[:, h, 0:SEQ], 0.0, MUL, ADD)
                dve.drain()

            def hgrn(l):
                for i, half in enumerate(LEVELS):
                    dve.wait_ge(sem("level_exp"), l * len(LEVELS) + (i + 1))
                    dve.tensor_tensor(QP[i % 2], QD[:, :, 0:SEQ], E1v, MUL)
                    dve.tensor_tensor(KP[i % 2], KD[:, :, 0:SEQ], E1v if half > 1 else E2, MUL).then_inc(sem("level_ready"), 1)
                    if i:
                        level_mask(l, i - 1)
                level_mask(l, len(LEVELS) - 1)
                dve.tensor_copy(lbt[:, 0, :], lb[:, 0:H]).then_inc(sem("levels_done"), 1)
                dve.wait_ge(sem("end_exp"), l + 1)
                dve.tensor_tensor(KP[0], KD[:, :, 0:SEQ], E1v, MUL).then_inc(sem("end_ready"), 1)
                dve.wait_ge(sem("hgrn_out"), l + 1)
                for i in range(2):
                    dve.tensor_copy(HCD[:, i, H:, :], bank(4 + i, P, H, HD))
                dve.wait_ge(sem("hgrn_state_out"), l + 1)
                dve.tensor_copy(DGS, bank(3, P, H, HD)).then_inc(sem("hgrn_state"), 1)
                dve.drain()
                dve.tensor_tensor(sqo, HCD, HCD, MUL)
                dve.drain()
                dve.tensor_reduce(st[:, 0:16].rearrange("p (b h) -> p b h", b=2), sqo, AX.X, ADD).then_inc(sem("squares3"), 1)
                dve.wait_ge(sem("roots3"), l + 1)
                dve.tensor_tensor(HCD, HCD, rep(rs[:, 0:16].rearrange("p (b h) -> p b h", b=2), 3, HD), MUL)
                dve.drain()
                dve.tensor_tensor(HCD, HCD, TM[:, 0:2, GATE:].rearrange("p b (g d) -> p b g d", d=HD), MUL)\
                    .then_inc(sem("mixed_ready"), 1)

            def context(l, b):
                dve.wait_ge(sem("ctx_out"), l * DEC + (b + 1))
                t0, t1 = (cut(dtmp[:, i, :], 0, H) for i in range(2))
                new = PA[:, PAGES * H:]
                dve.tensor_tensor(t0, ps[3][:, 132:136], new, ADD)
                dve.tensor_scalar(t1, new, latn[:, SEQ + b:SEQ + b + 1], None, MUL)
                dve.drain()
                dve.reciprocal(t0, t0)
                dve.tensor_tensor(t1, t1, ps[3][:, 128:132], ADD)
                dve.drain()
                dve.tensor_tensor(ctxT[:, :, SEQ + b], t1, t0, MUL).then_inc(sem("ctx_done"), 1)

            def latent_scores(l, b):
                K = PAGES * H
                dve.wait_ge(sem("page_roots"), l * DEC + (b + 1))
                dve.tensor_tensor(SA[:, 0:K], num[:, b % 2, 0:K], rsk[:, 0:K], MUL)
                dve.drain()
                dve.wait_ge(sem("kr_scores"), l * DEC + (b + 1))
                dve.tensor_tensor(SA[:, 0:K], SA[:, 0:K], ps[2][:, 0:K], ADD).then_inc(sem("kr_taken"), 1)
                dve.drain()
                dve.tensor_reduce(lmx[:, 0, :], SA[:, 0:K].rearrange("p (g h) -> p h g", h=H), AX.X, MAX)\
                    .then_inc(sem("latent_max"), 1)

            def latent_shift(l, b):
                K = PAGES * H
                dve.wait_ge(sem("latent_max_all"), l * DEC + (b + 1))
                new = nsA[:, b * H:b * H + H]
                dve.tensor_tensor(lmx[:, 2, :], lmx[:, 1, :], new, MAX)
                dve.drain()
                dve.tensor_tensor(SA[:, K:], new, lmx[:, 2, :], SUB)
                sv = SA[:, 0:K].rearrange("p (g h) -> p g h", h=H)
                dve.tensor_tensor(sv, sv, rep(lmx[:, 2, :], 1, PAGES), SUB).then_inc(sem("latent_shifted"), 1)

            def latent_sum(l, b):
                dve.wait_ge(sem("latent_exp"), l * DEC + (b + 1))
                dve.tensor_reduce(lsum[:, :], PA[:, 0:PAGES * H].rearrange("p (g h) -> p h g", h=H), AX.X, ADD)\
                    .then_inc(sem("latent_summed"), 1)

            def latent_samples(l):
                for b in range(DEC):
                    for g in range(PAGES):
                        n = (l * DEC + b) * PAGES + g
                        dve.wait_ge(sem("page_squared"), n + 1)
                        dve.tensor_reduce(ssq[:, b % 2, g * H:g * H + H], SQ[:, g % 4, :].rearrange("p (h d) -> p h d", h=H),
                                          AX.X, ADD)
                        c = GW + b * H
                        dve.tensor_copy(num[:, b % 2, g * H:g * H + H], ps[4 + g % 4][:, c:c + H]).then_inc(sem("page_taken"), 1)
                        if b and g == 3:
                            latent_scores(l, b - 1)
                        if b and g == 7:
                            if b > 1:
                                context(l, b - 2)
                            latent_shift(l, b - 1)
                        if b and g == 11:
                            latent_sum(l, b - 1)
                    if b == 2:
                        dve.wait_ge(sem("state_loaded"), (l + 1) * 16 * 20)
                        for j in range(4):
                            r = slice(32 * j, 32 * j + 32)
                            dve.tensor_copy(jq[r, 0:32].rearrange("p (g k) -> p g k", g=2),
                                             SI[r, 0:2 * HD].rearrange("p (g k) -> p g k", g=2)[:, :, 16 * j:16 * j + 16])
                            dve.tensor_copy(jq[r, 32:128].rearrange("p (g k) -> p g k", g=3),
                                             SI[r, X_QD:X_I].rearrange("p (g k) -> p g k", g=3)[:, :, 32 * j:32 * j + 32])
                        dve.tensor_tensor(sst[:, 2:3], sst[:, 0:1], SI[:, X_LF:X_LF + 1], ADD)
                        dve.drain()
                        dve.tensor_tensor(sst[:, 3:4], sst[:, 2:3], SI[:, X_I:X_I + 1], MAX)
                        dve.drain()
                        dve.tensor_tensor(sst[:, 4:5], sst[:, 2:3], sst[:, 3:4], SUB)
                        dve.tensor_tensor(sst[:, 5:6], SI[:, X_I:X_I + 1], sst[:, 3:4], SUB)
                        dve.tensor_scalar(sst[:, 6:7], sst[:, 3:4], -1.0, None, MUL).then_inc(sem("state_m"), 1)
                    if b == 4:
                        dve.wait_ge(sem("state_d_products"), l + 1)
                        dve.tensor_reduce(red[:, HD + 1:], OUTER.rearrange("p k v -> p v k"), AX.X, ADD)\
                            .then_inc(sem("state_d_summed"), 1)
                    if b == 6:
                        dve.wait_ge(sem("states_updated"), l + 1)
                        dve.tensor_reduce(red[:, 0:HD], OUTER[:, 0:16, :].rearrange("p k v -> p v k"), AX.X, ADD)
                        dve.tensor_reduce(red[:, HD:HD + 1], jq[:, 16:32], AX.X, ADD).then_inc(sem("states_summed"), 1)
                latent_scores(l, DEC - 1)
                context(l, DEC - 2)
                latent_shift(l, DEC - 1)
                latent_sum(l, DEC - 1)
                context(l, DEC - 1)

            def spread(l):
                s = slice(0, DEC)
                dve.tensor_tensor(qm[s], rep(TM[s, 2, BQ:BQ + GW], 1, DEC), rep(ident[s, 0:DEC], 2, GW), MUL)
                dve.tensor_tensor(prod[s, 0, :], TM[s, 2, BQ:BQ + GW], TM[s, 2, BK:BK + GW], MUL)
                dve.drain()
                dve.tensor_reduce(nst1[:, 1, :], prod[s, 0, :].rearrange("p (h d) -> p h d", h=H), AX.X, ADD)
                dve.drain()
                dve.tensor_tensor(nsm[:, 1], rep(nst1[:, 1, :], 1, DEC), rep(ident[s, 0:DEC], 2, H), MUL)\
                    .then_inc(sem("q_masked"), 1)

            def states(l):
                dve.wait_ge(sem("red_out"), l + 1)
                r = slice(0, 32)
                dve.tensor_copy(sst[r, 4:5], ps[5][r, HD:HD + 1])
                dve.tensor_copy(HS[:, 1, :], ps[5][r, HD + 1:2 * HD + 1])
                dve.drain()
                dve.scalar_tensor_tensor(sst[r, 4:5], sst[r, 4:5], -1.0, sst[r, 4:5], MUL, MAX)
                dve.drain()
                dve.tensor_tensor(sst[r, 4:5], sst[r, 4:5], sst[r, 9:10], MAX)
                dve.drain()
                dve.reciprocal(sst[r, 4:5], sst[r, 4:5])
                dve.drain()
                dve.tensor_scalar(HS[:, 0, :], ps[5][r, 0:HD], sst[r, 4:5], None, MUL)
                dve.drain()
                dve.tensor_tensor(red[r, 0:2 * HD].rearrange("p (g d) -> p g d", g=2), HS[:, :, :], HS[:, :, :], MUL)
                dve.drain()
                dve.tensor_reduce(st[r, 0:2], red[r, 0:2 * HD].rearrange("p (g d) -> p g d", g=2), AX.X, ADD)\
                    .then_inc(sem("squares4"), 1)
                dve.wait_ge(sem("roots4"), l + 1)
                dve.tensor_tensor(HS[:, :, :], HS[:, :, :], rep(rs[r, 0:2], 2, HD), MUL)
                dve.drain()
                dve.tensor_tensor(HS[:, :, :], HS[:, :, :], SI[r, X_CO:X_QD].rearrange("p (g d) -> p g d", g=2), MUL)\
                    .then_inc(sem("heads_ready"), 1)

            def windows(l):
                dve.wait_ge(sem("q_spread_copied"), l + 1)
                settled(dve)
                for b in range(DEC):
                    slot = b % K_SLOTS
                    dve.drain()
                    dve.wait_ge(k_loaded[slot], (l * (DEC // K_SLOTS) + (b // K_SLOTS + 1)) * 16 * NPAT)
                    dve.tensor_tensor(prod, KB[:, slot], rep(Qbc[:, b, :], 1, NPAT), MUL).then_inc(sem("window_products"), 1)
                    dve.drain()
                    dve.tensor_reduce(SB[:, b], prod.rearrange("p i (h d) -> p i h d", h=H), AX.X, ADD)
                dve.drain()
                dve.wait_ge(sem("vnew_copied"), l + 1)

                def w(i):
                    return wmx[:, i, :].rearrange("p (b h) -> p b h", h=H)

                over_keys = SB[:, :, :, :].rearrange("p b i h -> p b h i")
                dve.tensor_reduce(w(0), over_keys, AX.X, MAX).then_inc(sem("window_max"), 1)
                dve.wait_ge(sem("window_max_all"), l + 1)
                dve.tensor_tensor(wmx[:, 2, :], wmx[:, 2, :], wmx[:, 1, :], MAX)
                dve.drain()
                dve.tensor_tensor(SB[:, :, :, :], SB[:, :, :, :], rep(w(2), 2, NPAT), SUB)
                dve.tensor_tensor(wmx[:, 3, :], wmx[:, 1, :], wmx[:, 2, :], SUB).then_inc(sem("window_shifted_max"), 1)
                dve.wait_ge(sem("window_exp"), l + 1)
                dve.tensor_scalar(wmx[:, 3, :], wmx[:, 3, :], float(NPAT), None, MUL)
                dve.tensor_reduce(w(4), over_keys, AX.X, ADD).then_inc(sem("window_summed"), 1)
                dve.wait_ge(sem("window_sum_out"), l + 1)
                dve.tensor_tensor(wmx[:, 5, :], ps[6][:, 0:DEC * H], wmx[:, 3, :], ADD)
                dve.drain()
                dve.reciprocal(wmx[:, 5, :], wmx[:, 5, :])
                dve.drain()
                dve.tensor_tensor(wmx[:, 3, :], wmx[:, 3, :], wmx[:, 5, :], MUL)
                dve.tensor_tensor(SB[:, :, :, :], SB[:, :, :, :], rep(w(5), 2, NPAT), MUL).then_inc(sem("window_probs"), 1)
                dve.drain()
                for h in range(H):
                    r = slice(HD * (h % 2), HD * (h % 2) + HD)
                    dve.tensor_tensor(bsum[r, :, 0, h], vT[r, h // 2, :], w(3)[r, :, h], MUL)
                dve.drain()
                dve.wait_ge(sem("window_out"), l + 1)
                for h in range(H):
                    r = slice(HD * (h % 2), HD * (h % 2) + HD)
                    last = dve.tensor_tensor(o_T[r, 2 + h // 2, SEQ:NT], bsum[r, :, 0, h],
                                             bank(7, P, DEC, 2, H)[r, :, h // 2, h], ADD)
                last.then_inc(sem("mixer_done"), 1)

            with dve.Fori(0, DEPTH) as l:
                dve.tensor_copy(gcol[:, :], gcols[:, bass.ds(l, 1), :].rearrange("p a n -> p (a n)"))
                dve.tensor_copy(lb[:, :], lbs[:, bass.ds(l, 1), :].rearrange("p a n -> p (a n)"))
                dve.tensor_copy(cb[:, :], cbias[:, bass.ds(l, 1), :].rearrange("p a n -> p (a n)"))
                dve.drain()
                norm(l, 0)
                ffn(l, 0)
                stream(l, 0, 0.5)
                norm(l, 1)
                latent_rows(l)
                latent_qk(l)
                forget(l)
                output_gates(l)
                softmax(l, 0, A_SCALE, K_AADD, None)
                softmax(l, 1, B_SCALE, K_BADD, K_BMUL)
                mlstm(l)
                hgrn(l)
                latent_samples(l)
                spread(l)
                states(l)
                windows(l)
                stream(l, 1, 1.0)
                norm(l, 2)
                dve.wait_ge(sem("sample_states_stored"), (l + 1) * 16 * N_SSTATE)
                settled(dve)
                ffn(l, 1)
                stream(l, 2, 0.5)

        @block.tensor
        def _(pe):
            def turn(out, src, rows):
                return pe.transpose(out, src, ident[0:rows, 0:rows])

            pe.wait_ge(sem("constants_loaded"), 4 * 16)
            pe.wait_ge(sem("x_loaded"), 3 * 16)
            for c in range(KC):
                for b in range(BLK):
                    last = turn(bank(c, P, NT)[:, b * P:b * P + ROWS[b]], xin[0:ROWS[b], b, c * P:(c + 1) * P], ROWS[b])
                last.then_inc(sem("x_turned"), 1)
            pe.wait_ge(sem("ones_set"), 4)

            def norm(l, k):
                pe.wait_ge(sem("squares_ready"), l * 3 + (k + 1))
                pe.matmul(bank(6, P, NT), ones[:, 0:P], ssum[:, :], start=True, stop=True).then_inc(sem("mean_square"), 1)

            def ffn(l, f, n0):
                pe.wait_ge(sem("h_ready"), l * (3 * KC) + (2 * f + 1) * KC)
                settled(pe)

                def gate_up(j, n, more):
                    slab_arrived(pe, l, n, more)
                    w = ring[:, n % RING, :].rearrange("p (g c n) -> p g c n", g=2, c=KC)
                    for q in range(2):
                        pe.wait_ge(sem("ffn_tiles"), l * (2 * FT) + j * 2 + (f * FT + q + 1))
                        for g in range(2):
                            for c in range(KC):
                                last = pe.matmul(bank(2 * q + g, P, NT), w[:, g, c, q * P:(q + 1) * P], h_T[:, c, :],
                                                 start=(c == 0), stop=(c == KC - 1))
                        last.then_inc(sem("gate_up_out"), 1)

                with pe.Fori(0, NG // RING) as i:
                    for r in range(RING):
                        gate_up(i * RING + r, n0 + r, i)
                for j in range(NG // RING * RING, NG):
                    gate_up(j, n0 + j, 0)
                for m in range(ND):
                    n = n0 + NG + m
                    slab_arrived(pe, l, n)
                    pe.wait_ge(sem("stream_added"), l * (3 * KC) + (2 * f * KC + m + 1))
                    w = ring[:, n % RING, 0:FT * P].rearrange("p (c n) -> p c n", c=FT)
                    for c in range(FT):
                        if m == 0:
                            pe.wait_ge(sem("ffn_tiles"), l * (2 * FT) + (f * FT + c + 1 + CREDIT))
                        last = pe.matmul(bank(4 + m % 2, P, NT), w[:, c, :], act_T[:, c, :], start=(c == 0), stop=(c == FT - 1))
                    last.then_inc(sem("stream_out"), 1)

            def project(l, first, last_slab):
                for n in range(first, last_slab):
                    slab_arrived(pe, l, FFN_SLABS + n)
                    w = SLABS[n][1]
                    W = ring[:, (FFN_SLABS + n) % RING, 0:KC * w].rearrange("p (c n) -> p c n", c=KC)
                    for k in range(NTK):
                        if TICKETS[k][0] != n:
                            continue
                        kind, i = TICKETS[k][1:]
                        if k >= 4:
                            pe.wait_ge(sem("w_in_copied"), l * NTK + (k - 3))
                        for c in range(KC):
                            if kind == "rows":
                                cols = GW if n == 4 else w
                                last = pe.matmul(bank(k % 4, ROWS[i], cols), h_T[:, c, i * P:i * P + ROWS[i]], W[:, c, 0:cols],
                                                 start=(c == 0), stop=(c == KC - 1))
                            elif kind == "gate":
                                last = pe.matmul(bank(k % 4, H, NT), W[:, c, GW + i * H:GW + i * H + H], h_T[:, c, :],
                                                 start=(c == 0), stop=(c == KC - 1))
                            else:
                                last = pe.matmul(bank(k % 4, P, NT), W[:, c, i * P:(i + 1) * P], h_T[:, c, :],
                                                 start=(c == 0), stop=(c == KC - 1))
                        last.then_inc(sem("w_in_out"), 1)

            def latent_up(l):
                pe.wait_ge(sem("rows_final"), l + 1)
                for b in range(BLK):
                    for i, c in enumerate((CQ, CQ + P, CKV)):
                        last = turn(bank(4 + i, P, NT)[:, b * P:b * P + ROWS[b]], TM[0:ROWS[b], b, c:c + P], ROWS[b])
                last.then_inc(sem("down_turned"), 1)

            def up(l):
                pe.wait_ge(sem("down_copied"), l + 1)
                for b, bk in enumerate((4, 5, 7)):
                    for c in range(2):
                        pe.matmul(bank(bk, ROWS[b], H * QKW), cqT[:, c, b * P:b * P + ROWS[b]], wuq[:, c, :],
                                  start=(c == 0), stop=(c == 1))
                for b in range(2):
                    last = pe.matmul(cut(ps[6], b * GW, H, NOPE), latn[:, b * P:(b + 1) * P], wukv[:, :, 0:NOPE],
                                     start=True, stop=True)
                last.then_inc(sem("up_out"), 1)
                pe.wait_ge(sem("up_copied"), l * 2 + 1)
                pe.matmul(bank(4, DEC, H, NOPE), latn[:, SEQ:NT], wukv[:, :, 0:NOPE], start=True, stop=True)\
                    .then_inc(sem("up_out"), 1)

            def turn_qk(l):
                pe.wait_ge(sem("qk_final"), l + 1)
                for i, src in enumerate((Qk, Kk)):
                    for h in range(H):
                        for b in range(2):
                            last = turn(bank(4 + 2 * i + h // 2, QKW, 2, SEQ)[:, h % 2, b * P:(b + 1) * P], src[:, b, h, :], P)
                last.then_inc(sem("qk_turned"), 1)
                pe.wait_ge(sem("qk_copied"), l * 2 + 1)
                settled(pe)
                for h in range(H):
                    turn(bank(4, HD, H, DEC)[:, h, :], qtl[0:DEC, h, :], DEC)
                    turn(cut(ps[4], H * DEC, H, DEC)[:, h, :], q4[0:DEC, h].rearrange("p j r -> p (j r)"), DEC)
                    turn(bank(5, HD, H, P)[:, h, :], wukv[:, h, 0:NOPE], P)
                pe.matmul(bank(6, P, DEC, H), ones[0:DEC, 0:P], nsm[:, 0], start=True, stop=True).then_inc(sem("qk_turned"), 1)
                pe.wait_ge(sem("qk_copied"), l * 2 + 2)
                for h in range(H):
                    last = pe.matmul(bank(7, P, H, DEC)[:, h, :], wukT[0:HD, h, :], qtT[0:HD, h, :], start=True, stop=True)
                last.then_inc(sem("u_out"), 1)

            def turn_pairs(l):
                pe.wait_ge(sem("u_copied"), l + 1)
                for i, c in enumerate((BQ, BK, MQ, MK)):
                    for g in range(2):
                        for b in range(2):
                            last = turn(bank(4 + i, P, 2, SEQ)[:, g, b * P:(b + 1) * P], TM[:, b, c + g * P:c + (g + 1) * P], P)
                last.then_inc(sem("pairs_turned"), 1)

            def attend(l, a):
                if a == 0:
                    pe.wait_ge(sem("pairs_copied"), l + 1)
                else:
                    pe.wait_ge(sem("prompt_copied"), l * 2 + 1)
                for h in range(H):
                    if a == 0:
                        q, k = QT[0:QKW, h], KT[0:QKW, h]
                    else:
                        r = slice(HD * (h % 2), HD * (h % 2) + HD)
                        q, k = pairT[r, 0, h // 2], pairT[r, 1, h // 2]
                    pe.matmul(bank(4 + h, P, P), q[:, 0:P], k[:, 0:P], start=True, stop=True)
                    pe.matmul(ps[4 + h][:, P:3 * P], q[:, P:SEQ], k, start=True, stop=True).then_inc(sem("scores_out"), 1)
                pe.wait_ge(sem("scores_taken"), (l * 2 + a + 1) * H)
                pe.wait_ge(sem("probs_ready"), l * 2 + (a + 1))
                for h in range(H):
                    for c in range(3):
                        last = turn(bank(4 + h, P, 3, P)[:, c, :], S[:, h, c * P:(c + 1) * P], P)
                    last.then_inc(sem("probs_turned"), 1)
                for h in range(H):
                    pe.wait_ge(sem("probs_copied"), (l * 2 + a) * H + (h + 1 if h > 1 else 2))
                    for c in range(2):
                        w = TM[:, c, CKV:CKR] if a == 0 else TM[:, c, BV + h * HD:BV + (h + 1) * HD]
                        if a == 0:
                            out = bank(4 + h // 2, P, 2, SEQ)[:, h % 2, c * P:]
                        else:
                            out = bank(4 + h // 2, P, SEQ)[HD * (h % 2):HD * (h % 2) + HD, c * P:]
                        last = pe.matmul(out, w, PT[:, h, 0:SEQ] if c == 0 else PT[:, h, SEQ:], start=(c == 0), stop=(c == 1))
                last.then_inc(sem("prompt_out"), 1)

            def mlstm(l):
                pe.wait_ge(sem("prompt_copied"), l * 2 + 2)
                pe.wait_ge(sem("mgates_ready"), l + 1)
                settled(pe)
                g = bank(6, P, 6, H)
                for b in range(2):
                    turn(g[:, b, :], CG[0:H, 4, b * P:(b + 1) * P], H)
                    turn(g[:, 2 + b, :], CG[0:H, 7, b * P:(b + 1) * P], H)
                    turn(g[0:DEC, 4 + b, :], CG[0:H, b, SEQ:NT], H)
                for h in range(H):
                    last = pe.matmul(bank(4 + h // 2, P, 2, SEQ)[:, h % 2, :], selh[0:H, h, :], CG[0:H, 5, 0:SEQ], start=True, stop=True)
                last.then_inc(sem("mgates_out"), 1)
                for h in range(H):
                    r = slice(HD * (h % 2), HD * (h % 2) + HD)
                    q, k = pairT[r, 2, h // 2], pairT[r, 3, h // 2]
                    pe.matmul(bank(h, P, SEQ), k[:, 0:P], q, start=True, stop=True)
                    pe.matmul(ps[h][:, SEQ:3 * P], k[:, P:], q[:, P:], start=True, stop=True).then_inc(sem("mscores_out"), 1)
                pe.wait_ge(sem("mkeys_ready"), l + 1)
                pe.wait_ge(sem("mprobs_ready"), (l + 1) * H)
                for h in range(H):
                    pe.matmul(bank(4, P, H, HD + 1)[:, h, :], S[:, h, 0:P], vaug[:, 0, h, :], start=True, stop=True)
                for h in range(H):
                    for b in range(2):
                        pe.matmul(bank(5, P, H, HD + 1)[:, h, :], S[:, h, (b + 1) * P:(b + 2) * P], vaug[:, b, h, :],
                                  start=(b == 0), stop=(b == 1))
                for h in range(H):
                    for b in range(2):
                        last = pe.matmul(bank(6, HD, H, HD + 1)[:, h, :], kw[:, b, h, :], vaug[:, b, h, :],
                                         start=(b == 0), stop=(b == 1))
                last.then_inc(sem("mlstm_out"), 1)

            def hgrn(l):
                for i, half in enumerate(LEVELS):
                    pe.wait_ge(sem("level_ready"), l * len(LEVELS) + (i + 1))
                    if i >= 2:
                        pe.wait_ge(sem("level_taken"), l * len(LEVELS) + (i - 1))
                    for h in range(H):
                        bk = 2 * (i % 2) + h // 2
                        if i == 0:
                            last = pe.matmul(bank(bk, P, 2, P)[:, h % 2, :], KP[0][:, h, 0:P], QP[0][:, h, P:], start=True, stop=True)
                        else:
                            for b in range(2):
                                last = pe.matmul(bank(bk, P, 2, 2, P)[:, h % 2, b, :], KP[i % 2][:, h, b * P:(b + 1) * P],
                                                 QP[i % 2][:, h, b * P:(b + 1) * P], start=True, stop=True)
                    last.then_inc(sem("level_out"), 1)
                pe.wait_ge(sem("mlstm_taken"), l + 1)
                pe.wait_ge(sem("levels_done"), l + 1)

                def v(b, h):
                    return TM[:, b, DI + h * HD:DI + (h + 1) * HD]

                for h in range(H):
                    pe.matmul(bank(4, P, H, HD)[:, h, :], ATD[:, h, 0, :], v(0, h), start=True, stop=True)
                for h in range(H):
                    pe.matmul(bank(5, P, H, HD)[:, h, :], ATD[:, h, 2, :], v(0, h), start=True, stop=False)
                    last = pe.matmul(bank(5, P, H, HD)[:, h, :], ATD[:, h, 1, :], v(1, h), start=False, stop=True)
                last.then_inc(sem("hgrn_out"), 1)
                pe.wait_ge(sem("end_ready"), l + 1)
                for b in range(2):
                    for h in range(H):
                        turn(bank(6 + b, P, H, DK)[:, h, :], KP[0][:, h, b * P:(b + 1) * P], P)
                for i, src in enumerate((QD, FD, KD)):
                    for h in range(H):
                        last = turn(bank(i, DEC, H, DK)[:, h, :], src[:, h, SEQ:NT], P)
                last.then_inc(sem("end_turned"), 1)
                pe.wait_ge(sem("end_copied"), l + 1)
                for h in range(H):
                    for b in range(2):
                        last = pe.matmul(bank(3, P, H, HD)[:, h, :], KE[:, b, h, :], v(b, h), start=(b == 0), stop=(b == 1))
                last.then_inc(sem("hgrn_state_out"), 1)
                pe.wait_ge(sem("mixed_ready"), l + 1)
                for i in range(4):
                    for b in range(2):
                        last = turn(bank(4 + i, P, SEQ)[:, b * P:(b + 1) * P],
                                    HCD[:, b, 2 * i:2 * i + 2, :].rearrange("p h d -> p (h d)"), P)
                    last.then_inc(sem("mixed_out"), 1)

            def values(l, b, first, last):
                if first == 0:
                    pe.wait_ge(sem("latent_summed"), l * DEC + (b + 1))
                    if b:
                        pe.wait_ge(sem("ctx_done"), l * DEC + b)
                for g in range(first, last):
                    pe.matmul(ps[3][:, 128:132], lat(b)[:, g, :], PA[:, g * H:(g + 1) * H],
                              start=(g == 0), stop=(g == PAGES - 1))
                if last == PAGES:
                    pe.matmul(ps[3][:, 132:136], ones[:, 0:P], lsum[:, :], start=True, stop=True).then_inc(sem("ctx_out"), 1)

            def latent_samples(l):
                pe.wait_ge(sem("mixed_turned"), (l + 1) * 4)

                def turn_pages(b, c):
                    if c == 0:
                        pe.wait_ge(pages_loaded[b], (l + 1) * ((1 if b in KR_POOL else 2) * PAGES * 16))
                    if b:
                        pe.wait_ge(sem("lat_copied"), (l * DEC + b) * 4 + (c - 1))
                    elif c >= 2:
                        pe.wait_ge(sem("lat_copied"), l * (DEC * 4) + (c - 1))
                    for g in range(4):
                        last = turn(bank(c % 2, P, 4, P)[:, g, :], lat(b)[:, 4 * c + g, :], P)
                    last.then_inc(sem("lat_turned"), 1)

                def rotary_scores(b):
                    pe.wait_ge(sem("kr_copied"), l * DEC + (b + 1))
                    for j in range(4):
                        last = pe.matmul(cut(ps[2], 16 * j, 4, H), krT[:, j * P:(j + 1) * P], qrb[:, b], start=True, stop=True)
                    last.then_inc(sem("kr_scores"), 1)

                turn_pages(0, 0)
                for b in range(DEC):
                    for c in range(4):
                        if c < 3:
                            turn_pages(b, c + 1)
                        elif b + 1 < DEC:
                            turn_pages(b + 1, 0)
                        if c == 2:
                            if b in KR_POOL:
                                pe.wait_ge(kr_loaded[KR_POOL.index(b)], (l + 1) * (PAGES * 16))
                            if b:
                                pe.wait_ge(sem("kr_taken"), l * DEC + b)
                            for j in range(4):
                                last = turn(bank(2, P, 4, P)[:, j, :], kr(b)[:, j * P:(j + 1) * P], P)
                            last.then_inc(sem("kr_turned"), 1)
                        if c == 3 and b:
                            values(l, b - 1, 0, PAGES // 2)
                        if c == 0 and b > 1:
                            values(l, b - 2, PAGES // 2, PAGES)
                        pe.wait_ge(sem("lat_copied"), (l * DEC + b) * 4 + (c + 1))
                        for g in range(4 * c, 4 * c + 4):
                            n = (l * DEC + b) * PAGES + g
                            if b or g >= 4:
                                pe.wait_ge(sem("page_taken"), n - 3)
                            pe.matmul(bank(4 + g % 4, P, GW + DEC * H), latT[:, g, :], wuk[:, :], start=True, stop=True)\
                                .then_inc(sem("page_out"), 1)
                        if c == 3:
                            rotary_scores(b)
                values(l, DEC - 2, PAGES // 2, PAGES)
                values(l, DEC - 1, 0, PAGES)
                pe.wait_ge(sem("ctx_done"), (l + 1) * DEC)
                for h in range(H):
                    last = pe.matmul(bank(4 + h // 2, P, NT)[HD * (h % 2):HD * (h % 2) + HD, :], wukv[:, h, NOPE:], ctxT[:, h, :],
                                     start=True, stop=True)
                last.then_inc(sem("oA_out"), 1)

            def samples(l):
                s = slice(0, DEC)
                pe.wait_ge(sem("q_masked"), l + 1)
                for i in range(4):
                    pe.matmul(bank(i, P, 2, GW), ones[s, 0:P], qm[s, 2 * i:2 * i + 2, :], start=True, stop=True)\
                        .then_inc(sem("q_spread"), 1)
                pe.matmul(bank(6, P, DEC, H), ones[s, 0:P], nsm[:, 1], start=True, stop=True)
                for g in range(2):
                    last = turn(bank(7, P, 2, DEC)[:, g, :], TM[s, 2, BV + g * P:BV + (g + 1) * P], DEC)
                last.then_inc(sem("vnew_turned"), 1)
                pe.wait_ge(sem("oA_copied"), l + 1)
                pe.wait_ge(sem("states_summed"), l + 1)
                pe.matmul(bank(5, 32, 2 * HD + 1), cst[:, K_SELJ:K_SELJ + 32], red[:, :], start=True, stop=True)\
                    .then_inc(sem("red_out"), 1)
                pe.wait_ge(sem("heads_ready"), l + 1)
                settled(pe)
                for g in range(2):
                    last = turn(bank(4 + g, HD, 32), HS[:, g, :], 32)
                last.then_inc(sem("states_turned"), 1)
                pe.wait_ge(sem("window_summed"), l + 1)
                pe.matmul(bank(6, P, DEC * H), ones[:, 0:P], wmx[:, 4, :], start=True, stop=True).then_inc(sem("window_sum_out"), 1)
                pe.wait_ge(sem("window_v_loaded"), (l + 1) * DEC * NPAT * 16)
                pe.wait_ge(sem("window_probs"), l + 1)
                for b in range(DEC):
                    for g in range(2):
                        for i in range(NPAT):
                            last = pe.matmul(bank(7, P, DEC, 2, H)[:, b, g, :], VB[:, b, i, g * P:(g + 1) * P], SB[:, b, i, :],
                                             start=(i == 0), stop=(i == NPAT - 1))
                last.then_inc(sem("window_out"), 1)

            def w_out(l):
                pe.wait_ge(sem("states_copied"), l + 1)
                pe.wait_ge(sem("mixer_done"), l + 1)
                for i, (m0, k) in enumerate(OUT_SLABS):
                    n = FFN_SLABS + len(SLABS) + i
                    slab_arrived(pe, l, n)
                    w = ring[:, n % RING, 0:KC * k * P].rearrange("p (c n) -> p c n", c=KC)
                    for m in range(m0, m0 + k):
                        pe.wait_ge(sem("stream_added"), l * (3 * KC) + (KC + m + 1))
                        for c in range(KC):
                            last = pe.matmul(bank(4 + m % 2, P, NT), w[:, c, (m - m0) * P:(m - m0 + 1) * P], o_T[:, c, :],
                                             start=(c == 0), stop=(c == KC - 1))
                        last.then_inc(sem("stream_out"), 1)

            with pe.Fori(0, DEPTH) as l:
                norm(l, 0)
                ffn(l, 0, 0)
                norm(l, 1)
                pe.wait_ge(sem("h_ready"), l * (3 * KC) + 2 * KC)
                project(l, 0, 4)
                latent_up(l)
                project(l, 4, 5)
                pe.wait_ge(sem("small_loaded"), (l + 1) * 3 * 16)
                up(l)
                project(l, 5, 7)
                turn_qk(l)
                project(l, 7, 8)
                turn_pairs(l)
                project(l, 8, len(SLABS))
                attend(l, 0)
                attend(l, 1)
                mlstm(l)
                hgrn(l)
                latent_samples(l)
                samples(l)
                w_out(l)
                norm(l, 2)
                ffn(l, 1, FFN_SLABS + MIX_SLABS)
            pe.wait_ge(sem("squares_ready"), 3 * DEPTH + 1)
            for b in range(BLK):
                for g in range(2):
                    for c in range(4):
                        last = turn(bank(2 * b + g, ROWS[b], 4, P)[:, c, :], x_T[:, 4 * g + c, b * P:b * P + ROWS[b]], P)
                    last.then_inc(sem("y_out"), 1)


def program(nc, tensors):
    build(nc, tensors)


def constants():
    import numpy as np
    out = np.zeros((P, K_N), np.float32)
    out[:, K_ID:K_ID + P] = np.eye(P)
    t = np.arange(SEQ)
    d = t[:, None] - t[None, :]
    times = sum(((d >= 0) & (d <= w) & (d % s == 0)).astype(np.float32) for w, s in PATTERNS)
    tiles = [(0, 0), (1, 0), (1, 1)]

    def put(at, m):
        for i, (a, b) in enumerate(tiles):
            out[:, at + i * P:at + (i + 1) * P] = m[a * P:(a + 1) * P, b * P:(b + 1) * P]

    put(K_AADD, np.where(d >= 0, 0.0, -1e30))
    put(K_BADD, np.where(times > 0, 0.0, -1e30))
    put(K_BMUL, times)
    for i, (a, b) in enumerate([(0, 0), (1, 0), (1, 1)]):
        out[:, K_WM + i * P:K_WM + (i + 1) * P] = (d[a * P:(a + 1) * P, b * P:(b + 1) * P] >= 0).T * M_SCALE
    s, q = np.arange(P)[:, None], np.arange(P)[None, :]
    for i, half in enumerate(LEVELS[1:]):
        same = s // (2 * half) == q // (2 * half)
        pair = (s % (2 * half) < half) & (q % (2 * half) >= half) if half > 1 else s <= q
        out[:, K_LV + i * P:K_LV + (i + 1) * P] = same & pair
    for h in range(H):
        out[h, K_SELH + h * P:K_SELH + (h + 1) * P] = 1.0
    out[np.arange(P), K_SELJ + np.arange(P) % 32] = 1.0
    half = ROPE // 2
    inv = np.float32(10000.0) ** (-np.arange(half, dtype=np.float32) / np.float32(half))
    for b in range(BLK):
        pos = (b * P + np.arange(P) if b < 2 else np.full(P, PAST)).astype(np.float32)
        ang = pos[:, None] * inv[None, :]
        out[:, K_COS + b * half:K_COS + (b + 1) * half] = np.cos(ang)
        out[:, K_SIN + b * half:K_SIN + (b + 1) * half] = np.sin(ang)
    return out


def kernel(**x):
    import numpy as np
    import concourse.bacc as bacc
    from concourse.bass_utils import run_bass_kernel_spmd

    f32 = mybir.dt.float32
    a = {k: np.ascontiguousarray(np.asarray(v)) for k, v in x.items()}
    pool = a["cache_mla_latent"].shape[1]
    ins = {k: a[k] for k in ("x_prompt", "x_sample", "cache_mla_latent", "cache_mla_krope", "state_mlstm_C", "state_mlstm_n",
                             "state_mlstm_m", "state_hgrn_S", "w1_gate", "w1_up", "w1_down", "w2_gate", "w2_up", "w2_down",
                             "w_in", "a_wuq", "a_wukv", "w_out")}
    for k in ("cache_swa_k", "cache_swa_v"):
        ins[k] = a[k].reshape(DEPTH, DEC, PAST, GW)
    ins["page_table"] = a["page_table"].reshape(1, DEC * PAGES)
    ins["gains"] = np.concatenate([a[k] for k in ("a_gq", "a_gkv", "a_gkr", "b_gq", "b_gk", "a_gqn", "a_gqr", "a_gkn",
                                                  "c_gout", "d_gout")], axis=1)
    cols = np.stack([a[k] for k in ("g_ffn1", "g_mix", "g_ffn2")], axis=1)
    ins["g_col"] = np.ascontiguousarray(cols.reshape(DEPTH, 3 * KC, P).transpose(2, 0, 1))
    ins["lb_col"] = np.ascontiguousarray(a["d_lb_logits"].reshape(DEPTH, H, DK).transpose(2, 0, 1))
    ins["c_bias"] = np.ascontiguousarray(np.stack([a["c_bi"], a["c_bf"]], axis=2).transpose(1, 0, 2))
    ins["constants"] = constants()

    nc = bacc.Bacc("TRN2", target_bir_lowering=False, num_devices=1)
    t = {k: nc.dram_tensor("in_" + k, v.shape, mybir.dt.from_np(v.dtype), kind="ExternalInput").ap() for k, v in ins.items()}
    outs = {"y_prompt": (1, SEQ, D_MODEL), "y_sample": (DEC, 1, D_MODEL),
            "p_mla_latent": (DEPTH, SEQ, KVL), "p_mla_krope": (DEPTH, SEQ, ROPE), "p_swa_k": (DEPTH, SEQ, GW), "p_swa_v": (DEPTH, SEQ, GW),
            "p_mlstm_C": (DEPTH, H, HD, HD), "p_mlstm_n": (DEPTH, H, HD), "p_mlstm_m": (DEPTH, H), "p_hgrn_S": (DEPTH, H, DK, HD),
            "s_mla_latent": (DEPTH, DEC, KVL), "s_mla_krope": (DEPTH, DEC, ROPE), "s_swa_k": (DEPTH, DEC, PAST, GW),
            "s_swa_v": (DEPTH, DEC, PAST, GW), "s_mlstm_C": (DEPTH, DEC, H, HD, HD), "s_mlstm_n": (DEPTH, DEC, H, HD),
            "s_mlstm_m": (DEPTH, DEC, H), "s_hgrn_S": (DEPTH, DEC, H, DK, HD)}
    for k, shape in outs.items():
        t[k] = nc.dram_tensor("out_" + k, shape, f32, kind="ExternalOutput").ap()
    t["scratch"] = nc.dram_tensor("scratch", (DEPTH, DEC, H, X_N), f32, kind="Internal").ap()
    nc.disable_value_cache = True
    program(nc, t)
    got = run_bass_kernel_spmd(nc, [{"in_" + k: v for k, v in ins.items()}], core_ids=[0]).results[0]
    r = {k: got["out_" + k] for k in outs}
    heads = (H, HD)
    return (r["y_prompt"], r["y_sample"],
            r["p_mla_latent"].reshape(DEPTH, 1, SEQ, KVL), r["p_mla_krope"].reshape(DEPTH, 1, SEQ, ROPE),
            r["p_swa_k"].reshape(DEPTH, 1, SEQ, *heads), r["p_swa_v"].reshape(DEPTH, 1, SEQ, *heads),
            r["p_mlstm_C"].reshape(DEPTH, 1, H, HD, HD), r["p_mlstm_n"].reshape(DEPTH, 1, H, HD),
            r["p_mlstm_m"].reshape(DEPTH, 1, H), r["p_hgrn_S"].reshape(DEPTH, 1, H, DK, HD),
            r["s_mla_latent"].reshape(DEPTH, DEC, 1, KVL), r["s_mla_krope"].reshape(DEPTH, DEC, 1, ROPE),
            r["s_swa_k"].reshape(DEPTH, DEC, PAST, *heads), r["s_swa_v"].reshape(DEPTH, DEC, PAST, *heads),
            r["s_mlstm_C"], r["s_mlstm_n"], r["s_mlstm_m"], r["s_hgrn_S"])
```
